# Optimizing a Trainium2 kernel written in Bass

```python
import math
import jax, jax.numpy as jnp
from jax import lax
import numpy as np

D_MODEL = 2048
BATCH = 1
SEQ = 256
DEPTH = 2

ATTN_WIDTH = D_MODEL // 2
ATTN_HEAD_DIM = 128
N_ATTN_HEADS = ATTN_WIDTH // ATTN_HEAD_DIM
N_IDX_HEADS = 16
IDX_HEAD_DIM = 64
IDX_Q_WIDTH = N_IDX_HEADS * IDX_HEAD_DIM
TOPK_MAX = 256
Q_BLOCK = 128
N_BUCKETS = 32
MAX_DISTANCE = 128
NEG_INF = -1e30
POOL_WINDOWS = (2, 4, 8, 16)
POOL_GROUP_WIDTH = D_MODEL // 8
POOL_WIDTH = len(POOL_WINDOWS) * POOL_GROUP_WIDTH
EVEN_SPLITS = (ATTN_WIDTH, 2 * ATTN_WIDTH, 3 * ATTN_WIDTH,
               3 * ATTN_WIDTH + IDX_Q_WIDTH,
               3 * ATTN_WIDTH + IDX_Q_WIDTH + IDX_HEAD_DIM,
               3 * ATTN_WIDTH + IDX_Q_WIDTH + IDX_HEAD_DIM + N_IDX_HEADS)
EVEN_IN_WIDTH = EVEN_SPLITS[-1] + POOL_WIDTH
EVEN_OUT_WIDTH = ATTN_WIDTH + POOL_WIDTH
GDN_DK = 128
GDN_DV = 128
GDN_NK = D_MODEL // 128
GDN_NV = 2 * GDN_NK
GDN_QK_WIDTH = GDN_NK * GDN_DK
GDN_V_WIDTH = GDN_NV * GDN_DV
CONV_K = 4
CONV_WIDTH = 2 * GDN_QK_WIDTH + GDN_V_WIDTH
CHUNK = 64
ODD_IN_WIDTH = CONV_WIDTH + GDN_V_WIDTH + 2 * GDN_NV
D_FF = -(-8 * D_MODEL // (3 * 256)) * 256
RMS_EPS = 1e-6

kernel_name = "hybrid_dsa_pool_gdn_trunk"

def rms_norm(x, g):
    xf = x.astype(jnp.float32)
    y = xf * lax.rsqrt(jnp.mean(xf * xf, axis=-1, keepdims=True) + RMS_EPS)
    return (y * g.astype(jnp.float32)).astype(x.dtype)

def l2_norm(x):
    xf = x.astype(jnp.float32)
    return xf * lax.rsqrt(jnp.sum(xf * xf, axis=-1, keepdims=True) + RMS_EPS)

def t5_bucket(dist):
    max_exact = N_BUCKETS // 2
    d = jnp.maximum(dist, 0)
    log_ratio = jnp.log(jnp.maximum(d, 1).astype(jnp.float32) / max_exact) / math.log(MAX_DISTANCE / max_exact)
    large = jnp.minimum(max_exact + (log_ratio * (N_BUCKETS - max_exact)).astype(jnp.int32), N_BUCKETS - 1)
    return jnp.where(d < max_exact, d, large)

def dsa_attention(q, k, v, q_idx, k_idx, w_idx, rel_bias):
    B, S, H, Dh = q.shape
    topk = min(TOPK_MAX, S // 4)
    n_blk = S // Q_BLOCK

    def to_blocks(a):
        return a.reshape((B, n_blk, Q_BLOCK) + a.shape[2:]).swapaxes(0, 1)

    q_pos = jnp.arange(S, dtype=jnp.int32).reshape(n_blk, Q_BLOCK)
    key_pos = jnp.arange(S, dtype=jnp.int32)
    k_idx_f = k_idx.astype(jnp.float32)
    idx_scale = IDX_HEAD_DIM ** -0.5
    head_w_scale = N_IDX_HEADS ** -0.5
    attn_scale = Dh ** -0.5
    gather = jax.vmap(lambda a, i: a[i])

    def block(args):
        qb, qib, wb, tb = args
        dots = jnp.einsum('bqhd,bsd->bqhs', qib.astype(jnp.float32), k_idx_f) * idx_scale
        score = jnp.einsum('bqh,bqhs->bqs', wb.astype(jnp.float32) * head_w_scale, jax.nn.relu(dots))
        causal = key_pos[None, :] <= tb[:, None]
        score = jnp.where(causal[None], score, NEG_INF)
        _, sel = lax.top_k(score, topk)
        k_sel = gather(k, sel)
        v_sel = gather(v, sel)
        dist = tb[None, :, None] - sel
        bias = rel_bias[t5_bucket(dist)].astype(jnp.float32)
        logits = jnp.einsum('bqhd,bqjhd->bhqj', qb, k_sel).astype(jnp.float32) * attn_scale
        logits = logits + bias.transpose(0, 3, 1, 2)
        logits = jnp.where((dist >= 0)[:, None], logits, NEG_INF)
        p = jax.nn.softmax(logits, axis=-1).astype(v.dtype)
        return jnp.einsum('bhqj,bqjhd->bqhd', p, v_sel)

    out = lax.map(block, (to_blocks(q), to_blocks(q_idx), to_blocks(w_idx), q_pos))
    return out.swapaxes(0, 1).reshape(B, S, H * Dh)

def multiscale_pool(xp, pool_w, pool_scale):
    B, S, _ = xp.shape
    xf = xp.astype(jnp.float32)
    cs = jnp.concatenate([jnp.zeros((B, 1, POOL_WIDTH), jnp.float32), jnp.cumsum(xf, axis=1)], axis=1)
    t = jnp.arange(S, dtype=jnp.int32)
    groups = []
    for gi, w in enumerate(POOL_WINDOWS):
        sl = slice(gi * POOL_GROUP_WIDTH, (gi + 1) * POOL_GROUP_WIDTH)
        lo = jnp.maximum(t + 1 - w, 0)
        win_sum = cs[:, 1:, sl] - cs[:, lo, sl]
        count = (t + 1 - lo).astype(jnp.float32)
        groups.append(win_sum / count[None, :, None] - xf[..., sl])
    pooled = jnp.stack(groups, axis=2).astype(xp.dtype)
    mixed = jnp.einsum('bsgc,gcd->bsgd', pooled, pool_w).reshape(B, S, POOL_WIDTH)
    return mixed * pool_scale

def even_mixer(h, w_in, w_o, pool_w, pool_scale, rel_bias):
    B, S, _ = h.shape
    p = h @ w_in
    q, k, v, qi, ki, wi, xp = jnp.split(p, list(EVEN_SPLITS), axis=-1)
    q = q.reshape(B, S, N_ATTN_HEADS, ATTN_HEAD_DIM)
    k = k.reshape(B, S, N_ATTN_HEADS, ATTN_HEAD_DIM)
    v = v.reshape(B, S, N_ATTN_HEADS, ATTN_HEAD_DIM)
    qi = qi.reshape(B, S, N_IDX_HEADS, IDX_HEAD_DIM)
    attn_out = dsa_attention(q, k, v, qi, ki, wi, rel_bias)
    pool_out = multiscale_pool(xp, pool_w, pool_scale)
    return jnp.concatenate([attn_out, pool_out], axis=-1) @ w_o

def causal_depthwise_conv(x, w):
    C = x.shape[-1]
    return lax.conv_general_dilated(x, w[:, None, :], window_strides=(1,), padding=[(CONV_K - 1, 0)],
                                    dimension_numbers=('NWC', 'WIO', 'NWC'), feature_group_count=C)

def gated_delta_rule(q, k, v, g, beta):
    B, L, H, Dk = q.shape
    Dv = v.shape[-1]
    N = L // CHUNK

    def chunks(a):
        return a.reshape(B, N, CHUNK, H, a.shape[-1]).transpose(1, 0, 3, 2, 4)

    qc = chunks(q * Dk ** -0.5)
    kc = chunks(k)
    vc = chunks(v)
    bc = beta.reshape(B, N, CHUNK, H).transpose(1, 0, 3, 2)
    gc = jnp.cumsum(g.reshape(B, N, CHUNK, H).transpose(1, 0, 3, 2), axis=-1)
    tril = jnp.tril(jnp.ones((CHUNK, CHUNK), bool))
    strict = jnp.tril(jnp.ones((CHUNK, CHUNK), bool), -1)
    diff = gc[..., :, None] - gc[..., None, :]
    decay = jnp.where(tril, jnp.exp(jnp.where(tril, diff, 0.0)), 0.0)
    kb = kc * bc[..., None]
    vb = vc * bc[..., None]
    m = jnp.where(strict, jnp.einsum('nbhid,nbhjd->nbhij', kb, kc) * decay, 0.0)
    a_mat = m + jnp.eye(CHUNK, dtype=jnp.float32)
    rhs = jnp.concatenate([vb, kb * jnp.exp(gc)[..., None]], axis=-1)
    sol = lax.linalg.triangular_solve(a_mat, rhs, left_side=True, lower=True, unit_diagonal=True)
    u, w = sol[..., :Dv], sol[..., Dv:]
    intra = jnp.where(tril, jnp.einsum('nbhid,nbhjd->nbhij', qc, kc) * decay, 0.0)
    g_last = gc[..., -1]
    q_dec = qc * jnp.exp(gc)[..., None]
    k_dec = kc * jnp.exp(g_last[..., None] - gc)[..., None]
    d_last = jnp.exp(g_last)

    def step(state, xs):
        q_i, k_i, u_i, w_i, intra_i, dl_i = xs
        v_new = u_i - jnp.einsum('bhcd,bhde->bhce', w_i, state)
        out = jnp.einsum('bhcd,bhde->bhce', q_i, state) + jnp.einsum('bhij,bhje->bhie', intra_i, v_new)
        state = state * dl_i[..., None, None] + jnp.einsum('bhcd,bhce->bhde', k_i, v_new)
        return state, out

    state0 = jnp.zeros((B, H, Dk, Dv), jnp.float32)
    _, out = lax.scan(step, state0, (q_dec, k_dec, u, w, intra, d_last))
    return out.transpose(1, 0, 3, 2, 4).reshape(B, L, H, Dv)

def odd_mixer(h, w_in, conv_w, a_log, dt_bias, norm_w, w_o):
    B, S, _ = h.shape
    p = h @ w_in
    qkv = jax.nn.silu(causal_depthwise_conv(p[..., :CONV_WIDTH], conv_w))
    z = p[..., CONV_WIDTH:CONV_WIDTH + GDN_V_WIDTH]
    b = p[..., CONV_WIDTH + GDN_V_WIDTH:CONV_WIDTH + GDN_V_WIDTH + GDN_NV]
    a = p[..., CONV_WIDTH + GDN_V_WIDTH + GDN_NV:]
    q, k, v = jnp.split(qkv, [GDN_QK_WIDTH, 2 * GDN_QK_WIDTH], axis=-1)
    rep = GDN_NV // GDN_NK
    q = jnp.repeat(l2_norm(q.reshape(B, S, GDN_NK, GDN_DK)), rep, axis=2)
    k = jnp.repeat(l2_norm(k.reshape(B, S, GDN_NK, GDN_DK)), rep, axis=2)
    v = v.reshape(B, S, GDN_NV, GDN_DV).astype(jnp.float32)
    beta = jax.nn.sigmoid(b.astype(jnp.float32))
    g = -jnp.exp(a_log.astype(jnp.float32)) * jax.nn.softplus(a.astype(jnp.float32) + dt_bias.astype(jnp.float32))
    o = gated_delta_rule(q, k, v, g, beta).astype(h.dtype)
    o = rms_norm(o, norm_w) * jax.nn.silu(z.reshape(B, S, GDN_NV, GDN_DV))
    return o.reshape(B, S, GDN_V_WIDTH) @ w_o

def swiglu(h, w_gate, w_up, w_down):
    return (jax.nn.silu(h @ w_gate) * (h @ w_up)) @ w_down

def setup_inputs(seed: int = 0) -> dict:
    key = jax.random.key(seed)
    ks = jax.random.split(key, 20)
    n_even = (DEPTH + 1) // 2
    n_odd = DEPTH // 2
    f32 = jnp.float32

    def nrm(k, shape, fan_in):
        return jax.random.normal(k, shape, f32) * fan_in ** -0.5

    def gain(k, shape):
        return 1.0 + 0.05 * jax.random.normal(k, shape, f32)

    dt = jnp.exp(jax.random.uniform(ks[9], (n_odd, GDN_NV), f32, math.log(1e-3), math.log(1e-1)))
    return {
        "x": jax.random.normal(ks[0], (BATCH, SEQ, D_MODEL), f32),
        "rel_bias": 0.5 * jax.random.normal(ks[1], (N_BUCKETS, N_ATTN_HEADS), f32),
        "even_w_in": nrm(ks[2], (n_even, D_MODEL, EVEN_IN_WIDTH), D_MODEL),
        "even_w_o": nrm(ks[3], (n_even, EVEN_OUT_WIDTH, D_MODEL), EVEN_OUT_WIDTH),
        "pool_w": nrm(ks[4], (n_even, len(POOL_WINDOWS), POOL_GROUP_WIDTH, POOL_GROUP_WIDTH), POOL_GROUP_WIDTH),
        "pool_scale": gain(ks[5], (n_even, POOL_WIDTH)),
        "odd_w_in": nrm(ks[6], (n_odd, D_MODEL, ODD_IN_WIDTH), D_MODEL),
        "conv_w": nrm(ks[7], (n_odd, CONV_K, CONV_WIDTH), CONV_K),
        "a_log": jnp.log(jax.random.uniform(ks[8], (n_odd, GDN_NV), f32, 1.0, 16.0)),
        "dt_bias": dt + jnp.log(-jnp.expm1(-dt)),
        "gdn_norm_w": gain(ks[10], (n_odd, GDN_DV)),
        "odd_w_o": nrm(ks[11], (n_odd, GDN_V_WIDTH, D_MODEL), GDN_V_WIDTH),
        "ffn_w_gate": nrm(ks[12], (DEPTH, D_MODEL, D_FF), D_MODEL),
        "ffn_w_up": nrm(ks[13], (DEPTH, D_MODEL, D_FF), D_MODEL),
        "ffn_w_down": nrm(ks[14], (DEPTH, D_FF, D_MODEL), D_FF),
        "mix_pre_g": gain(ks[15], (DEPTH, D_MODEL)),
        "mix_post_g": gain(ks[16], (DEPTH, D_MODEL)),
        "ffn_pre_g": gain(ks[17], (DEPTH, D_MODEL)),
        "ffn_post_g": gain(ks[18], (DEPTH, D_MODEL)),
    }

def reference(x, rel_bias, even_w_in, even_w_o, pool_w, pool_scale, odd_w_in, conv_w, a_log, dt_bias,
              gdn_norm_w, odd_w_o, ffn_w_gate, ffn_w_up, ffn_w_down, mix_pre_g, mix_post_g, ffn_pre_g, ffn_post_g):
    for layer in range(DEPTH):
        i = layer // 2
        hn = rms_norm(x, mix_pre_g[layer])
        if layer % 2 == 0:
            m = even_mixer(hn, even_w_in[i], even_w_o[i], pool_w[i], pool_scale[i], rel_bias)
        else:
            m = odd_mixer(hn, odd_w_in[i], conv_w[i], a_log[i], dt_bias[i], gdn_norm_w[i], odd_w_o[i])
        x = x + rms_norm(m, mix_post_g[layer])
        hn = rms_norm(x, ffn_pre_g[layer])
        x = x + rms_norm(swiglu(hn, ffn_w_gate[layer], ffn_w_up[layer], ffn_w_down[layer]), ffn_post_g[layer])
    return x


_drawn_inputs = setup_inputs


def setup_inputs(seed=0):
    import zlib

    import numpy as np

    out = dict(_drawn_inputs(seed))
    spreads = {}
    factors = {}
    for name, (base, spread) in spreads.items():
        noise = np.random.default_rng([zlib.crc32(name.encode()), seed]).standard_normal(out[name].shape)
        drawn = base * np.exp(spread * noise) if base else spread * noise
        out[name] = __import__('jax').numpy.asarray(drawn.astype(out[name].dtype))
    for name, factor in factors.items():
        out[name] = (out[name] * factor).astype(out[name].dtype)
    return out
```

```python
from contextlib import ExitStack
import math

import numpy as np

import concourse.bass as bass
from concourse import mybir

F32 = mybir.dt.float32
F32R = mybir.dt.float32r
ALU = mybir.AluOpType
ACT = mybir.ActivationFunctionType
AX = mybir.AxisListType.X

P = 128
D = 2048
S = 256
NT = S // P
KT = D // P
AW = D // 2
DH = 128
NH = AW // DH
NIH, DIH = 16, 64
TOPK = min(256, S // 4)
NEG = -1e30
TAKEN = -3e38
WINDOWS = (2, 4, 8, 16)
PGW = D // 8
NB = 32
EVEN_IN = 3 * AW + NIH * DIH + DIH + NIH + len(WINDOWS) * PGW
C_QI, C_KI, C_XP = 3 * AW, 3 * AW + NIH * DIH, 3 * AW + NIH * DIH + DIH + NIH
NKH = D // 128
NVH = 2 * NKH
QKW, VW = NKH * 128, NVH * 128
CONVW = 2 * QKW + VW
NTAP = 4
ODD_IN = CONVW + VW + 2 * NVH
FF = -(-8 * D // (3 * 256)) * 256
EPS = 1e-6
NSEG = P + S - 1
SEG = S + P

CH = 1024
RING = 4
LEAD = 2
TW, NW = 256, 512
NCB = D // NW
FI = FF // TW
NG = NKH // 2
GSLOT = 24
NLEV = 6

PH_IN0 = dict(c=0, b=0, t=0)
PH_OUT0 = dict(c=82, b=21, t=17)


def _after(ph, c, b, t):
    return dict(c=ph["c"] + c, b=ph["b"] + b, t=ph["t"] + t)


PH_FF0 = _after(PH_OUT0, NCB * KT // 2, NCB, 0)
PH_DN0 = _after(PH_FF0, 8 * FI, 2 * FI, 2 * FI)
PH_BA = _after(PH_DN0, NCB * FF // P // 2, NCB, 0)
PH_IN1 = _after(PH_BA, 2, 1, 1)
PH_OUT1 = _after(PH_IN1, GSLOT * NG, 6 * NG, 6 * NG)
PH_FF1 = _after(PH_OUT1, NCB * NVH // 2, NCB, 0)
PH_DN1 = _after(PH_FF1, 8 * FI, 2 * FI, 2 * FI)
CHUNKS = PH_DN1["c"] + NCB * FF // P // 2

K_ID, K_ONE, K_U, K_M0 = 0, P, 2 * P, 3 * P
K_MT = 4 * P
K_INV = K_MT + NLEV * P
K_END = K_INV + len(WINDOWS) * 16


def constants():
    k = np.zeros((P, K_END), np.float32)
    i, j = np.arange(P)[:, None], np.arange(P)[None, :]
    k[:, K_ID:K_ID + P] = np.eye(P)
    k[:, K_ONE:K_ONE + P] = 1
    k[:, K_U:K_U + P] = i <= j
    for lev in range(NLEV + 1):
        s = 2 ** lev
        off = (i // (2 * s) == j // (2 * s)) & (i // s % 2 == 1) & (j // s % 2 == 0)
        m = np.eye(P) - off
        at = K_M0 if lev == 0 else K_MT + (lev - 1) * P
        k[:, at:at + P] = m.T if lev == 0 else m
    for n, w in enumerate(WINDOWS):
        k[:, K_INV + 16 * n:K_INV + 16 * n + 16] = 1.0 / np.minimum(np.arange(16) + 1, w)
    return k


def bucket_onehot():
    d = np.maximum(S - 1 - np.arange(SEG), 0)
    half = NB // 2
    ratio = np.log(np.maximum(d, 1).astype(np.float32) / half) / math.log(128 / half)
    large = np.minimum(half + (ratio.astype(np.float32) * (NB - half)).astype(np.int32), NB - 1)
    b = np.where(d < half, d, large)
    return (np.arange(NB)[:, None] == b[None, :]).astype(np.float32)


def looped(d):
    return not isinstance(d, int)


def trunk(nc, io):
    with ExitStack() as ctx:
        program(nc, io, ctx)


def program(nc, io, ctx):
    names = set()

    def sb(name, shape, dt=F32, at=ctx):
        return at.enter_context(nc.sbuf_tensor(name, shape, dt))

    def sem(name):
        assert name not in names
        names.add(name)
        return ctx.enter_context(nc.semaphore(name))

    x = sb("x_res", [P, NT, D])
    raw = sb("w_raw", [P, RING, CH])
    whi = sb("w_hi", [P, RING, CH], F32R)
    wlo = sb("w_lo", [P, RING, CH], F32R)
    halfa = sb("halfa", [P, 2, S])
    scr = sb("scr", [P, D])
    cst = sb("cst", [P, K_END])
    vecT = sb("vecT", [P, 4 * KT + 8 + 1])
    junk = sb("junk", [P, NW])
    ssx = sb("ssx", [P, NT, NCB])
    ssm = sb("ssm", [P, NT, NCB])
    tot = sb("tot", [P, 2, NT])
    meansq = sb("meansq", [P, 2, NT])
    rstd = sb("rstd", [P, 2, NT])
    mhalf = sb("mhalf", [P, NT])
    nwh = sb("nwh", [P, 1])
    epsc = sb("epsc", [P, 2])
    ident = cst[:, K_ID:K_ID + P]
    ones = cst[:, K_ONE:K_ONE + P]
    triu = cst[:, K_U:K_U + P]

    with ExitStack() as a1:
        hn = sb("hn", [P, KT, 2 * S], F32R, a1)
    with ExitStack() as a2:
        m_a = sb("m_a", [P, NT, D], F32, a2)
        gain = sb("gain", [P, D], F32, a2)
    with ExitStack() as a3:
        ohi = sb("ohi", [P, NVH, S], F32R, a3)
    sb("region_a", [P, KT * 2 * S])

    with ExitStack() as b1:
        mix = sb("mix", [P, KT, 2 * S], F32R, b1)
        qiT = sb("qiT", [P, 2, 2, S], F32, b1)
        kiw = sb("kiw", [P, S], F32, b1)
        kid = sb("kid", [P, S], F32, b1)
        wi = sb("wi", [P, NT, NIH], F32, b1)
        rel = sb("rel", [P, 2, 3 * P], F32, b1)
        score = sb("score", [P, 3 * P], F32, b1)
        top8 = sb("top8", [P, NT, 8], F32, b1)
        bm = sb("bm", [P, NH, 3 * P], F32, b1)
        kqT = sb("kqT", [P, 2, 2, S], F32, b1)
        vtm = sb("vtm", [P, 2, NT, TW], F32, b1)
        prob = sb("prob", [P, 2, 3 * P], F32, b1)
        pT = sb("pT", [P, 3 * P], F32, b1)
        mx = sb("mx", [P, NH, NT], F32, b1)
        psm = sb("psm", [P, NH, NT], F32, b1)
        rps = sb("rps", [P, NH, NT], F32, b1)
        xpad = sb("xpad", [P, 2, 16 + S], F32, b1)
        wina = sb("wina", [P, 2, 16 + S], F32, b1)
        winb = sb("winb", [P, 2, 16 + S], F32, b1)
        poolw = sb("poolw", [P, len(WINDOWS), 2, PGW], F32, b1)
        onehot = sb("onehot", [NB, SEG], F32, b1)
        relb = sb("relb", [NB, NH], F32, b1)
        vrow = sb("vrow", [4 * KT + 8 + 1, P], F32, b1)
    with ExitStack() as b1b:
        bseg = sb("bseg", [P, NH, SEG], F32, b1b)
    with ExitStack() as b2:
        hid = sb("hid", [P, FF // P, 2 * S], F32R, b2)
    with ExitStack() as b3:
        o32 = sb("o32", [P, NVH, S], F32, b3)
        kqr = sb("kqr", [P, 2, 2, S], F32, b3)
        kq = sb("kq", [P, 2, 2, S], F32, b3)
        cpad = sb("cpad", [P, 2, 3 + S + 1], F32, b3)
        vfm = sb("vfm", [P, 2, S], F32, b3)
        vtok = sb("vtok", [P, 2, 4, P], F32, b3)
        zs = sb("zs", [P, 4, S], F32, b3)
        dec = sb("dec", [P, 2, 4, P], F32, b3)
        at = sb("at", [P, 2, 4, P], F32, b3)
        intra = sb("intra", [P, 2, 4, P], F32, b3)
        xi = sb("xi", [P, 2, 4, P], F32, b3)
        xt = sb("xt", [P, 2, 4, P], F32, b3)
        wy = sb("wy", [P, 2, 4, P], F32, b3)
        qd = sb("qd", [P, 4, P], F32, b3)
        ktok = sb("ktok", [P, 2, P], F32, b3)
        kdec = sb("kdec", [P, 4, P], F32, b3)
        vn = sb("vn", [P, 2, 4, P], F32, b3)
        st = sb("st", [P, 4, P], F32, b3)
        ba = sb("ba", [P, 2, 2 * NVH], F32, b3)
        sc4 = sb("sc4", [P, 4, 2, NVH], F32, b3)
        cur = sb("cur", [P, 4, 2, 4], F32, b3)
        bat = sb("bat", [P, 4, 2, NVH], F32, b3)
        avec = sb("avec", [P, 2, NVH], F32, b3)
        cwT = sb("cwT", [P, NTAP, 64], F32, b3)
        cwc = sb("cwc", [P, NTAP, 8], F32, b3)
        cwrow = sb("cwrow", [P, 2, P], F32, b3)
    with ExitStack() as b4:
        olo = sb("olo", [P, NVH, S], F32R, b4)
        m_b = sb("m_b", [P, NT, D], F32, b4)
        gain_b = sb("gain_b", [P, D], F32, b4)
    conv_y, conv_th = (scr[:, i * 512:(i + 1) * 512].rearrange("p (a b) -> p a b", a=2) for i in (0, 1))
    sqkq = scr[:, 1024:2048].rearrange("p (a b) -> p a b", a=2)
    osq = wy[:, :, :, :].rearrange("p a b c -> p a (b c)")
    fg, fth, fu, fh = (scr[:, i * 512:(i + 1) * 512].rearrange("p (a b) -> p a b", a=2) for i in range(4))

    dn = ctx.enter_context(nc.psum_tensor("dense", [P, 4, 512], F32))
    mi = ctx.enter_context(nc.psum_tensor("misc", [P, 4, 512], F32))
    BM, BY, BX, BT = range(4)
    seg_dram = nc.dram_tensor("bias_segments", (P, NH * SEG), F32).ap()

    s_raw = [sem(f"raw_loaded{i}") for i in range(RING)]
    s_hi, s_lo, s_used = sem("hi_made"), sem("lo_made"), sem("chunk_used")
    s_ca, s_evac, s_sqm = sem("half_copied"), sem("block_evacuated"), sem("out_squared")
    s_x, s_cst, s_vrow, s_relb, s_poolw = (sem(n) for n in ("x_loaded", "cst_loaded", "vrow_loaded", "relb_loaded", "poolw_loaded"))
    s_vecp, s_vec, s_mh = sem("vec_turned"), sem("vec_ready"), sem("mhalf_set")
    s_sqx, s_tot, s_ms, s_rs = sem("x_squared"), sem("squares_summed"), sem("meansq_ready"), sem("rstd_ready")
    s_xs0, s_xs1, s_xtp, s_hnh, s_hnl = sem("x_scaled_act"), sem("x_scaled_dve"), sem("x_turned"), sem("hn_hi"), sem("hn_lo")
    s_gain, s_xup, s_out = sem("gain_loaded"), sem("x_updated"), sem("out_stored")
    s_bsp, s_bs, s_bsw, s_bmr, s_bm = sem("bias_row_psum"), sem("bias_row"), sem("bias_rows_stored"), sem("bias_read"), sem("bias_masked")
    s_kid, s_wip, s_wi, s_dot, s_rel, s_sc = sem("ki_copied"), sem("wi_turned"), sem("wi_ready"), sem("dots"), sem("relu_dots"), sem("score_added")
    s_causal, s_max8, s_repl, s_seln, s_selm = sem("score_masked"), sem("max8"), sem("replaced"), sem("selection"), sem("selection_masked")
    s_lg, s_lb, s_mx, s_ex, s_rp, s_pn = sem("logits"), sem("logits_biased"), sem("logits_max"), sem("probs"), sem("probs_sum_inv"), sem("probs_scaled")
    s_ptp, s_pt, s_ov, s_mh_, s_ml = sem("probs_turned"), sem("probsT"), sem("attn_out"), sem("attn_hi"), sem("attn_lo")
    s_pad, s_win, s_pd, s_mp, s_ph, s_pl = sem("pads_zeroed"), sem("window_sum"), sem("pooled"), sem("pool_mixed"), sem("pool_hi"), sem("pool_lo")
    s_th, s_t1, s_h, s_hh, s_hl = sem("ff_tanh"), sem("ff_gate"), sem("ff_hidden"), sem("ff_hi"), sem("ff_lo")
    s_nwh, s_cwr, s_cwp, s_cw, s_av, s_pz = (sem(n) for n in ("nwh_ready", "cw_loaded", "cw_turned", "cw_ready", "avec_loaded", "cpad_zeroed"))
    s_bap, s_ba, s_t, s_mn, s_ea, s_el, s_sp, s_g, s_gcp, s_gc, s_eg, s_sc4 = (sem(n) for n in (
        "ba_turned", "ba_ready", "a_biased", "a_folded", "ba_exps", "a_log1p", "softplus", "g_ready", "gc_psum", "gc_ready", "gc_exp", "scalars_ready"))
    s_cur, s_cwc, s_tap0, s_tap, s_thc, s_silu, s_zg = (sem(n) for n in ("cur_ready", "cwc_ready", "tap0", "taps", "conv_tanh", "silu_done", "z_gated"))
    s_gb, s_clamp, s_dec, s_eq, s_qd = (sem(n) for n in ("gc_rows", "decay_clamped", "decay_ready", "exp_gc_row", "q_decayed"))
    s_sqk, s_ss, s_rt, s_rc, s_kqn = (sem(n) for n in ("kq_squared", "norm_sums", "norm_roots", "norm_inverses", "kq_normed"))
    s_gq, s_atr, s_inr, s_ats, s_at, s_in = (sem(n) for n in ("kk_qk", "a_raw", "intra_raw", "a_strict", "a_ready", "intra_ready"))
    s_vtp, s_vt, s_ktp, s_kt, s_kd = (sem(n) for n in ("v_turned", "v_tok", "k_turned", "k_tok", "k_decayed"))
    s_x1t, s_x1p, s_x1, s_y, s_w, s_xx, s_xe = (sem(n) for n in ("x1T", "x1_turned", "x1", "ax_psum", "w_ready", "x_psum", "x_evacuated"))
    s_y0, s_v0, s_sp_, s_st, s_ks, s_r1, s_y1, s_v1 = (sem(n) for n in ("y0", "vnew0", "state_psum", "state", "k_state", "rhs1", "y1", "vnew1"))
    s_op, s_osq, s_on, s_og = (sem(n) for n in ("o_psum", "o_squared", "o_normed", "o_gated"))
    s_og_ss, s_ort, s_orc = sem("o_norm_sums"), sem("o_norm_roots"), sem("o_norm_inverses")
    s_oh, s_ol, s_eps = sem("o_hi"), sem("o_lo"), sem("eps_set")

    KTI = KT // 4

    def cols(start, width):
        return bass.ds(start, width)

    kmap0 = list(range(NH // 2)) + [NH // 2 + gi for gi in (3, 2, 1, 0)]
    xp_order = (3, 2, 1, 0)

    blocks0 = [("kw", 0, C_KI, 2)] + [("qi", b, C_QI + b * TW, 4) for b in range(4)]
    for p in range(NH // 2):
        blocks0 += [("v", p, 2 * AW + p * TW, 4), ("k", p, AW + p * TW, 4), ("q", p, p * TW, 4)]
    blocks0 += [("xp", gi, C_XP + gi * PGW, 4) for gi in xp_order]
    chunks0 = [(n, j) for n, blk in enumerate(blocks0) for j in range(blk[3])]
    end0 = np.cumsum([blk[3] for blk in blocks0]).tolist()
    tidx0 = np.cumsum([0] + [blk[0] != "v" for blk in blocks0]).tolist()
    assert len(chunks0) == PH_OUT0["c"] and len(blocks0) == PH_OUT0["b"] and tidx0[-1] == PH_OUT0["t"]
    evac_at = {e: n for n, e in enumerate(end0)}
    SC0 = 23
    NR = TOPK // 8
    ATT = [SC0 + NR + 3 + 12 * p for p in range(NH // 2)]
    head_at = {ATT[h // 2] + 2 * (h % 2): h for h in range(NH)}
    GB_COL = {0: QKW, 1: 0, 2: 2 * QKW, 3: 2 * QKW + TW, 4: CONVW, 5: CONVW + TW}
    GB_STEP = {0: TW, 1: TW, 2: 2 * TW, 3: 2 * TW, 4: 2 * TW, 5: 2 * TW}
    w_in0, w_in1 = io["even_w_in"][0], io["odd_w_in"][0]

    block = ctx.enter_context(nc.Block())

    @block.sync
    def _(sp):
        def load(c, d, view, src):
            if c >= RING or looped(d):
                sp.wait_ge(s_lo, d + (c - RING + 1))
            sp.dma_start(view, src).then_inc(s_raw[c % RING], 16)

        def slot(c, k):
            return raw[:, c % RING, :].rearrange("p (k n) -> p k n", k=k)

        def load_t(c, d, w, j, col):
            load(c, d, slot(c, 4), w[4 * j * P:(4 * j + 4) * P, cols(col, TW)].rearrange("(k p) n -> p k n", p=P))

        def load_n(c, d, w, kp, col):
            load(c, d, slot(c, 2), w[2 * kp * P:(2 * kp + 2) * P, cols(col, NW)].rearrange("(k p) n -> p k n", p=P))

        def load_w128(c, w, j, col):
            load(c, 0, slot(c, 8), w[8 * j * P:(8 * j + 8) * P, cols(col, P)].rearrange("(k p) n -> p k n", p=P))

        def out_projection(ph, w, kmap):
            n = len(kmap)
            with sp.Fori(0, NCB // 2) as i:
                for u in range(2):
                    for j in range(n):
                        load_n(ph["c"] + u * n + j, i * (2 * n), w, kmap[j], i * (2 * NW) + u * NW)

        def feed_forward(layer, ph, pd):
            wg, wu, wd = io["ffn_w_gate"][layer], io["ffn_w_up"][layer], io["ffn_w_down"][layer]
            with sp.Fori(0, FI) as i:
                for j in range(8):
                    load_t(ph["c"] + j, i * 8, wg if j < 4 else wu, j % 4, i * TW)
            out_projection(pd, wd, list(range(FF // P // 2)))

        for c, (n, j) in enumerate(chunks0):
            kind, _, col, _ = blocks0[n]
            if kind == "kw":
                load_w128(c, w_in0, j, col)
            else:
                load_t(c, 0, w_in0, j, col)
        out_projection(PH_OUT0, io["even_w_o"][0], kmap0)
        feed_forward(0, PH_FF0, PH_DN0)
        for j in range(2):
            load_w128(PH_BA["c"] + j, w_in1, j, ODD_IN - P)
        with sp.Fori(0, NG) as g:
            for b in range(GSLOT // 4):
                col = (g * (GB_STEP[b] // P) * P + GB_COL[b]) if GB_COL[b] == 0 else g * GB_STEP[b] + GB_COL[b]
                for j in range(4):
                    load_t(PH_IN1["c"] + 4 * b + j, g * GSLOT, w_in1, j, col)
        out_projection(PH_OUT1, io["odd_w_o"][0], list(range(NVH // 2)))
        feed_forward(1, PH_FF1, PH_DN1)

    @block.gpsimd
    def _(pool):
        for t in range(NT):
            pool.dma_start(x[:, t, :], io["x"][0, t * P:(t + 1) * P, :]).then_inc(s_x, 16)
        pool.dma_start(cst[:, :], io["consts"]).then_inc(s_cst, 16)
        rows = 0
        for nm, n in (("mix_pre_g", 2 * KT), ("ffn_pre_g", 2 * KT), ("pool_scale", 8), ("gdn_norm_w", 1)):
            a = io[nm]
            if nm == "gdn_norm_w":
                src = a
            else:
                src = a.rearrange("a (k p) -> (a k) p", p=P)
            pool.dma_start(vrow[rows:rows + n, :], src).then_inc(s_vrow, 16)
            rows += n
        pool.dma_start(onehot[:, :], io["onehot"]).then_inc(s_relb, 16)
        pool.dma_start(relb[:, :], io["rel_bias"]).then_inc(s_relb, 16)
        pool.memset(mhalf[:, :], -0.5).then_inc(s_mh, 1)
        pool.wait_ge(s_mh, 1)

        def inverse_root(n):
            pool.wait_ge(s_ms, n + 1)
            pool.tensor_tensor(rstd[:, n % 2, :], meansq[:, n % 2, :], mhalf[:, :], ALU.pow).then_inc(s_rs, 1)

        def load_gain(n, dst, src, free_sem, free_val):
            pool.wait_ge(free_sem, free_val)
            pool.dma_start(dst[:, :], src.partition_broadcast(P)).then_inc(s_gain, 16)

        inverse_root(0)
        pool.wait_ge(s_bs, NH)
        pool.dma_start(seg_dram, bseg[:, :, :].rearrange("p h s -> p (h s)")).then_inc(s_bsw, 16)
        pool.wait_ge(s_bsw, 16)
        for t in range(NT):
            w = P * (t + 1)
            src = bass.AP(seg_dram.tensor, S - 1 - P * t, [[NH * SEG - 1, P], [SEG, NH], [1, w]])
            pool.dma_start(bm[:, :, t * P:t * P + w], src).then_inc(s_bmr, 16)
        pool.dma_start(poolw[:, :, :, :], io["pool_w"][0].rearrange("g (c p) d -> p g c d", p=P)).then_inc(s_poolw, 16)
        pool.memset(xpad[:, :, 0:16], 0.0).then_inc(s_pad, 1)
        pool.memset(wina[:, :, 0:16], 0.0).then_inc(s_pad, 1)
        pool.memset(winb[:, :, 0:16], 0.0).then_inc(s_pad, 1)
        pool.wait_ge(s_evac, 1)
        pool.dma_start(kid[DIH:2 * DIH, :], kiw[0:DIH, :]).then_inc(s_kid, 16)
        pool.wait_ge(s_sc, NIH * NT)
        for t in range(NT):
            w = P * (t + 1)
            v = score[:, t * P:t * P + w]
            pool.affine_select(out=v, in_=v, compare_op=ALU.is_ge, fill=NEG, base=t * P,
                               pattern=[[-1, w]], channel_multiplier=1).then_inc(s_causal, 1)
        pool.wait_ge(s_seln, 1)
        for t in range(NT):
            w = P * (t + 1)
            v = score[:, t * P:t * P + w]
            pool.affine_select(out=v, in_=v, compare_op=ALU.is_ge, fill=NEG, base=t * P,
                               pattern=[[-1, w]], channel_multiplier=1).then_inc(s_selm, 1)
        pool.wait_ge(s_selm, 2)
        pool.wait_ge(s_bmr, 32)
        for h in range(NH):
            pool.tensor_tensor(bm[:, h, :], bm[:, h, :], score[:, :], ALU.add).then_inc(s_bm, 1)
        load_gain(0, gain, io["mix_post_g"][0], s_used, PH_OUT0["c"])
        inverse_root(1)
        inverse_root(2)
        load_gain(1, gain, io["ffn_post_g"][0], s_used, PH_DN0["c"])
        inverse_root(3)
        inverse_root(4)
        pool.dma_start(cwrow[:, :, :], io["conv_w"][0].rearrange("k (t p) -> (k t) p", p=P)
                       .rearrange("(a r) p -> r a p", a=2)).then_inc(s_cwr, 16)
        pool.dma_start(avec[:, 0, :], io["dt_bias"][0].partition_broadcast(P)).then_inc(s_av, 16)
        pool.dma_start(avec[:, 1, :], io["a_log"][0].partition_broadcast(P)).then_inc(s_av, 16)
        pool.memset(cpad[:, :, 0:3], 0.0).then_inc(s_pz, 1)

        def masks(c, g):
            v, w = at[:, c, :, :], intra[:, c, :, :]
            pool.wait_ge(s_atr, g * 2 + (c + 1))
            pool.affine_select(out=v, in_=v, compare_op=ALU.is_ge, fill=0.0, base=-1,
                               pattern=[[0, 4], [1, P]], channel_multiplier=-1).then_inc(s_ats, 1)
            pool.wait_ge(s_ats, g * 2 + (c + 1))
            pool.affine_select(out=v, in_=v, compare_op=ALU.not_equal, fill=1.0, base=0,
                               pattern=[[0, 4], [1, P]], channel_multiplier=-1).then_inc(s_at, 1)
            pool.wait_ge(s_inr, g * 2 + (c + 1))
            pool.affine_select(out=w, in_=w, compare_op=ALU.is_ge, fill=0.0, base=0,
                               pattern=[[0, 4], [1, P]], channel_multiplier=-1).then_inc(s_in, 1)

        for g in range(NG):
            for c in range(2):
                masks(c, g)
        load_gain(2, gain_b, io["mix_post_g"][1], s_og, 2 * NG)
        inverse_root(5)
        inverse_root(6)
        load_gain(3, gain, io["ffn_post_g"][1], s_used, PH_DN1["c"])
        inverse_root(7)
        for b in range(NCB):
            for t in range(NT):
                pool.wait_ge(s_xup, 8 * 3 + NT * b + t + 1)
                pool.dma_start(io["out"][0, t * P:(t + 1) * P, b * NW:(b + 1) * NW],
                               x[:, t, b * NW:(b + 1) * NW]).then_inc(s_out, 16)
        pool.wait_ge(s_out, 16 * NT * NCB)

    @block.tensor
    def _(pe):
        def begin_block(b, d):
            if b >= 2:
                pe.wait_ge(s_evac, d + (b - 1))

        def chunk_t(c, dc, b, j, kts=4, tiles=2, hn_ready=None):
            pe.wait_ge(s_lo, dc + (c + 1))
            if hn_ready is not None:
                pe.wait_ge(s_hnl, hn_ready)
            sl = c % RING
            w = tiles * P
            for f in range(tiles):
                bank = 2 * (b % 2) + f
                for kk in range(kts):
                    kt = kts * j + kk
                    at_ = slice(kk * w + f * P, kk * w + f * P + P)
                    if kt == 0:
                        nc.tensor.matmul(dn[:, bank, :], whi[:, sl, at_], hn[:, kt, :], start=True, stop=False)
                    mm = nc.tensor.matmul(dn[:, bank, 0:S], wlo[:, sl, at_], hn[:, kt, 0:S], start=False, stop=False)
                    if kt > 0:
                        mm = nc.tensor.matmul(dn[:, bank, :], whi[:, sl, at_], hn[:, kt, :], start=False,
                                              stop=kt == KT - 1)
            mm.then_inc(s_used, 1)

        def chunk_n(c, dc, b, first, last, lhs, width):
            pe.wait_ge(s_lo, dc + (c + 1))
            sl = c % RING
            for t in range(NT):
                bank = 2 * (b % 2) + t
                for kk, (hi, lo) in enumerate(lhs):
                    tok = slice(t * P, (t + 1) * P)
                    ws = slice(kk * width, (kk + 1) * width)
                    o = dn[:, bank, 0:width]
                    nc.tensor.matmul(o, hi(tok), whi[:, sl, ws], start=first and kk == 0, stop=False)
                    nc.tensor.matmul(o, hi(tok), wlo[:, sl, ws], start=False, stop=False)
                    mm = nc.tensor.matmul(o, lo(tok), whi[:, sl, ws], start=False,
                                          stop=last and kk == len(lhs) - 1)
            mm.then_inc(s_used, 1)

        def pair(t, kt, lo_at=S):
            return (lambda k: t[:, kt, k]), (lambda k: t[:, kt, lo_at + k.start:lo_at + k.stop])

        def norm_turn(n):
            if n == 0:
                pe.wait_ge(s_cst, 16)
            for kg in range(4):
                pe.wait_ge(s_xs0, 4 * n + kg + 1)
                pe.wait_ge(s_xs1, 4 * n + kg + 1)
                if kg >= 2:
                    pe.wait_ge(s_hnl, 16 * n + 4 * (kg - 1))
                for q in range(4):
                    for t in range(NT):
                        at_ = ((kg % 2) * NT + t) * 512 + q * P
                        mm = nc.tensor.transpose(mi[:, 2 * (kg % 2) + q // 2, (q % 2) * S + t * P:(q % 2) * S + (t + 1) * P],
                                                 scr[:, at_:at_ + P], ident)
                mm.then_inc(s_xtp, 1)

        def out_projection(ph, kmap, lhs_of, ready):
            n = len(kmap)
            with pe.Fori(0, NCB // 2) as i:
                for u in range(2):
                    begin_block(ph["b"] + u, i * 2)
                    for j in range(n):
                        ready(j)
                        kt = 2 * kmap[j]
                        chunk_n(ph["c"] + u * n + j, i * (2 * n), ph["b"] + u, j == 0, j == n - 1,
                                [lhs_of(kt), lhs_of(kt + 1)], NW)

        def feed_forward(n, ph, pd):
            with pe.Fori(0, FI) as i:
                for j in range(8):
                    if j % 4 == 0:
                        begin_block(ph["b"] + j // 4, i * 2)
                    chunk_t(ph["c"] + j, i * 8, ph["b"] + j // 4, j % 4, hn_ready=16 * n + 4 * (j % 4 + 1))
            layer = n // 2
            out_projection(pd, list(range(FF // P // 2)), lambda kt: pair(hid, kt),
                           lambda j: pe.wait_ge(s_hl, FI * layer + j + 1))

        pe.wait_ge(s_cst, 16)
        pe.wait_ge(s_vrow, 64)
        R = 4 * KT + 9
        nc.tensor.transpose(mi[:, BX, 0:R], vrow[:, :], ident[0:R, 0:R]).then_inc(s_vecp, 1)
        pe.wait_ge(s_relb, 32)
        for h in range(NH):
            if h >= 2:
                pe.wait_ge(s_bs, h - 1)
            nc.tensor.matmul(mi[:, h % 2, 0:SEG], relb[:, h:h + 1].broadcast_to([NB, P]), onehot[:, :],
                             start=True, stop=True).then_inc(s_bsp, 1)
        pe.wait_ge(s_bs, NH)
        pe.wait_ge(s_vec, 1)
        norm_turn(0)

        def turn_index_weights():
            pe.wait_ge(s_evac, 1)
            pe.wait_ge(s_hnl, 16)
            for t in range(NT):
                mm = nc.tensor.transpose(mi[:, BX, t * P:(t + 1) * P], kiw[:, t * P:(t + 1) * P], ident)
            mm.then_inc(s_wip, 1)

        def dots(ih):
            lo = DIH * (ih % 2)
            src = kiw if ih % 2 == 0 else kid
            pe.wait_ge(s_evac, 2 + ih // 4)
            if ih == 1:
                pe.wait_ge(s_kid, 16)
            if ih >= 2:
                pe.wait_ge(s_rel, ih - 1)
            for t in range(NT):
                w = P * (t + 1)
                mm = nc.tensor.matmul(mi[:, ih % 2, t * P:t * P + w],
                                      qiT[lo:lo + DIH, ih // 4 % 2, ih % 4 // 2, t * P:(t + 1) * P],
                                      src[lo:lo + DIH, 0:w], start=t == 0, stop=True, skip_group_check=True)
            mm.then_inc(s_dot, 1)

        def logits(h):
            pe.wait_ge(s_evac, end0.index(end0[5 + 3 * (h // 2) + 2]) + 1)
            if h >= 1:
                pe.wait_ge(s_lb, h)
            else:
                pe.wait_ge(s_rel, NIH)
            for t in range(NT):
                w = P * (t + 1)
                mm = nc.tensor.matmul(mi[:, 0, t * P:t * P + w], kqT[:, 1, h % 2, t * P:(t + 1) * P],
                                      kqT[:, 0, h % 2, 0:w], start=t == 0, stop=True, skip_group_check=True)
            mm.then_inc(s_lg, 1)

        def turn_probs(h):
            pe.wait_ge(s_pn, NT * (h + 1))
            if h >= 1:
                pe.wait_ge(s_pt, h)
            for n_, at_ in enumerate((0, P, 2 * P)):
                mm = nc.tensor.transpose(mi[:, 1, n_ * P:(n_ + 1) * P], prob[:, h % 2, at_:at_ + P], ident)
            mm.then_inc(s_ptp, 1)

        def attend(h):
            pe.wait_ge(s_pt, h + 1)
            if h >= 1:
                pe.wait_ge(s_ml, h)
            v = vtm[:, h // 2 % 2, :, (h % 2) * DH:(h % 2 + 1) * DH]
            nc.tensor.matmul(mi[:, 2, 0:P], v[:, 0, :], pT[:, 0:P], start=True, stop=True)
            nc.tensor.matmul(mi[:, 2, P:S], v[:, 0, :], pT[:, P:S], start=True, stop=False)
            nc.tensor.matmul(mi[:, 2, P:S], v[:, 1, :], pT[:, S:S + P], start=False, stop=True).then_inc(s_ov, 1)

        def mix_pool(k):
            gi = xp_order[k]
            pe.wait_ge(s_pd, 2 * (k + 1))
            if k == 0:
                pe.wait_ge(s_poolw, 16)
            else:
                pe.wait_ge(s_pl, k)
            for dt in range(2):
                for ct in range(2):
                    mm = nc.tensor.matmul(mi[:, 3, dt * S:(dt + 1) * S], poolw[:, gi, ct, dt * P:(dt + 1) * P],
                                          wina[:, ct, 16:16 + S], start=ct == 0, stop=ct == 1)
            mm.then_inc(s_mp, 1)

        for s, (n, j) in enumerate(chunks0 + [(None, None)] * 3):
            if n is not None:
                kind = blocks0[n][0]
                if j == 0:
                    begin_block(n, 0)
                if kind == "kw":
                    chunk_t(s, 0, n, j, kts=8, tiles=1, hn_ready=8 * (j + 1))
                elif kind == "v":
                    chunk_n(s, 0, n, j == 0, j == 3, [pair(hn, 4 * j + kk) for kk in range(4)], TW)
                else:
                    chunk_t(s, 0, n, j)
            if s == 3:
                turn_index_weights()
            if 7 <= s < 7 + NIH:
                dots(s - 7)
            if s in head_at:
                logits(head_at[s])
            if s - 2 in head_at:
                turn_probs(head_at[s - 2])
            if s - 3 in head_at:
                attend(head_at[s - 3])
            for k in range(4):
                if s == end0[17 + k] + 2:
                    mix_pool(k)

        def mix_ready(j):
            if j < NH // 2:
                pe.wait_ge(s_ml, 2 * (j + 1))
            else:
                pe.wait_ge(s_pl, j - NH // 2 + 1)

        out_projection(PH_OUT0, kmap0, lambda kt: pair(mix, kt), mix_ready)
        norm_turn(1)
        feed_forward(1, PH_FF0, PH_DN0)
        norm_turn(2)
        pe.wait_ge(s_cwr, 16)
        pe.wait_ge(s_hnl, 16 * 3)
        for a in range(2):
            mm = nc.tensor.transpose(mi[:, BX, a * P:(a + 1) * P], cwrow[:, a, :], ident)
        mm.then_inc(s_cwp, 1)
        begin_block(PH_BA["b"], 0)
        for j in range(2):
            chunk_t(PH_BA["c"] + j, 0, PH_BA["b"], j, kts=8, tiles=1)
        pe.wait_ge(s_evac, PH_IN1["b"])
        for t in range(NT):
            mm = nc.tensor.transpose(mi[:, BY, t * P:(t + 1) * P], conv_y[:, 0, t * P:(t + 1) * P], ident)
        mm.then_inc(s_bap, 1)

        def log_decay_sums():
            pe.wait_ge(s_g, 1)
            for c in range(2):
                mm = nc.tensor.matmul(mi[:, BX, 256 + c * NVH:256 + (c + 1) * NVH], triu, sc4[:, 0, c, :],
                                      start=True, stop=True)
            mm.then_inc(s_gcp, 1)

        def decay_rows(g, c):
            pe.wait_ge(s_cur, g * 1 + 1)
            if c == 1:
                pe.wait_ge(s_clamp, g * 2 + 1)
            for u in range(4):
                mm = nc.tensor.matmul(mi[:, BM, u * P:(u + 1) * P], cur[:, 0, c, u:u + 1].broadcast_to([P, P]),
                                      triu, start=True, stop=True)
            mm.then_inc(s_gb, 1)

        def norm_sums(g, k, o_too):
            pe.wait_ge(s_sqk, g * 1 + 1)
            if k == 0:
                pe.wait_ge(s_clamp, g * 2 + 2)
                pe.wait_ge(s_eq, g * 1 + 1)
            nc.tensor.matmul(mi[:, (BM, BY)[k], :], ones, sqkq[:, k, :], start=True, stop=True).then_inc(s_ss, 1)

        def o_norm_sums(g, k):
            pe.wait_ge(s_osq, g * 2 + (k + 1))
            nc.tensor.matmul(mi[:, (BM, BY)[k], :], ones, osq[:, k, :], start=True, stop=True).then_inc(s_og_ss, 1)

        def products(g, c):
            pe.wait_ge(s_kqn, g * 2 + 2)
            if c == 1:
                pe.wait_ge(s_atr, g * 2 + 1)
                pe.wait_ge(s_inr, g * 2 + 1)
            tok = slice(c * P, (c + 1) * P)
            for kp in range(2):
                mm = nc.tensor.matmul(mi[:, BM, kp * 256:(kp + 1) * 256].rearrange("p (a b) -> p a b", a=2),
                                      kq[:, 0, kp, tok], kq[:, :, kp, tok], start=True, stop=True)
            mm.then_inc(s_gq, 1)

        def turn_v(g, half):
            pe.wait_ge(s_silu, g * 4 + (3 + half))
            if half == 0:
                pe.wait_ge(s_atr, g * 2 + 2)
                pe.wait_ge(s_inr, g * 2 + 2)
            else:
                pe.wait_ge(s_x1, g * 2 + 2)
            for c in range(2):
                for u in range(2):
                    mm = nc.tensor.transpose(mi[:, BM, (2 * c + u) * P:(2 * c + u + 1) * P],
                                             vfm[:, u, c * P:(c + 1) * P], ident)
            mm.then_inc(s_vtp, 1)

        def turn_x1(g, b):
            pe.wait_ge(s_x1t, g * 2 + (b + 1))
            if b == 0:
                pe.wait_ge(s_vt, g * 2 + 1)
            else:
                pe.wait_ge(s_x1, g * 2 + 1)
            for u in range(4):
                mm = nc.tensor.transpose(mi[:, BM, u * P:(u + 1) * P], xt[:, b, u, :], ident)
            mm.then_inc(s_x1p, 1)

        def turn_k(g):
            pe.wait_ge(s_vt, g * 2 + 2)
            for kp in range(2):
                mm = nc.tensor.transpose(mi[:, BM, kp * P:(kp + 1) * P], kq[:, 0, kp, 0:P], ident)
            mm.then_inc(s_ktp, 1)

        def times_a(g, b, lev):
            n = 2 * (lev - 1) + b
            if lev == 1:
                pe.wait_ge(s_x1, g * 2 + (b + 1))
            else:
                pe.wait_ge(s_xe, g * 12 + (2 * (lev - 2) + b + 1))
            if n >= 1:
                pe.wait_ge(s_w, g * 12 + n)
            for u in range(4):
                mm = nc.tensor.matmul(mi[:, BY, u * P:(u + 1) * P], at[:, b, u, :], xi[:, b, u, :],
                                      start=True, stop=True)
            mm.then_inc(s_y, 1)

        def next_x(g, b, lev):
            n = 2 * (lev - 1) + b
            pe.wait_ge(s_w, g * 12 + (n + 1))
            if n >= 1:
                pe.wait_ge(s_xe, g * 12 + n)
            for u in range(4):
                mm = nc.tensor.matmul(mi[:, BT, u * P:(u + 1) * P], wy[:, b, u, :], xt[:, b, u, :],
                                      start=True, stop=True)
                if lev < NLEV:
                    mm = nc.tensor.matmul(mi[:, BX, u * P:(u + 1) * P], xt[:, b, u, :], wy[:, b, u, :],
                                          start=True, stop=True)
            mm.then_inc(s_xx, 1)

        def solve(g, c):
            pe.wait_ge(s_xe, g * 12 + (11 + c))
            if c == 1:
                pe.wait_ge(s_r1, g * 1 + 1)
            for u in range(4):
                mm = nc.tensor.matmul(mi[:, BY, u * P:(u + 1) * P], xt[:, c, u, :], vtok[:, c, u, :],
                                      start=True, stop=True)
            mm.then_inc((s_y0, s_y1)[c], 1)

        def state(g):
            pe.wait_ge(s_v0, g * 1 + 1)
            for u in range(4):
                mm = nc.tensor.matmul(mi[:, BY, u * P:(u + 1) * P], kdec[:, u, :], vn[:, 0, u, :],
                                      start=True, stop=True)
            mm.then_inc(s_sp_, 1)

        def keys_times_state(g):
            pe.wait_ge(s_st, g * 1 + 1)
            for kp in range(2):
                mm = nc.tensor.matmul(mi[:, BY, kp * 256:(kp + 1) * 256], kq[:, 0, kp, P:S],
                                      st[:, 2 * kp:2 * kp + 2, :].rearrange("p a b -> p (a b)"),
                                      start=True, stop=True)
            mm.then_inc(s_ks, 1)

        def outputs(g, half):
            pe.wait_ge(s_v1, g * 1 + 1)
            pe.wait_ge(s_in, g * 2 + 2)
            for e in range(2):
                u = 2 * half + e
                o = mi[:, (BX, BT)[half], e * S:(e + 1) * S]
                nc.tensor.matmul(o[:, 0:P], vn[:, 0, u, :], intra[:, 0, u, :], start=True, stop=True)
                nc.tensor.matmul(o[:, P:S], vn[:, 1, u, :], intra[:, 1, u, :], start=True, stop=False)
                mm = nc.tensor.matmul(o[:, P:S], st[:, u, :], qd[:, u, :], start=False, stop=True)
            mm.then_inc(s_op, 1)

        def slot(n, g, cur_on, prev_on):
            if prev_on:
                h = g - 1
                m = n + GSLOT
                for b in range(2):
                    lev, odd = divmod(m - 20 - b, 2)
                    if odd == 1 and 1 <= lev + 1 <= NLEV:
                        next_x(h, b, lev + 1)
                for b in range(2):
                    lev, odd = divmod(m - 20 - b, 2)
                    if odd == 0 and 1 <= lev + 1 <= NLEV:
                        times_a(h, b, lev + 1)
                if m == 32:
                    solve(h, 0)
                if m == 33:
                    state(h)
                if m == 34:
                    keys_times_state(h)
                if m == 35:
                    solve(h, 1)
                if m == 36:
                    outputs(h, 0)
                if m == 37:
                    outputs(h, 1)
            if cur_on:
                if n == 12:
                    decay_rows(g, 0)
                if n == 13:
                    decay_rows(g, 1)
                if n == 14:
                    norm_sums(g, 0, prev_on)
                    norm_sums(g, 1, prev_on)
            if prev_on and n == 14:
                if cur_on:
                    pe.wait_ge(s_rt, g * 2 + 2)
                o_norm_sums(g - 1, 0)
                o_norm_sums(g - 1, 1)
            if cur_on:
                if n in (16, 17):
                    if n == 16:
                        if prev_on:
                            pe.wait_ge(s_ort, (g - 1) * 2 + 2)
                        else:
                            pe.wait_ge(s_rt, g * 2 + 2)
                    products(g, n - 16)
                if n == 18:
                    turn_v(g, 0)
                if n == 19:
                    turn_x1(g, 0)
                if n == 20:
                    turn_x1(g, 1)
                for b in range(2):
                    lev, odd = divmod(n - 20 - b, 2)
                    if odd == 1 and lev >= 0:
                        next_x(g, b, lev + 1)
                for b in range(2):
                    lev, odd = divmod(n - 20 - b, 2)
                    if odd == 0 and lev >= 0:
                        times_a(g, b, lev + 1)
                if n == 21:
                    turn_v(g, 1)
                if n == 22:
                    turn_k(g)

        def group(g, d, prev_on):
            for n in range(GSLOT):
                b = n // 4
                if n % 4 == 0:
                    begin_block(PH_IN1["b"] + b, d * 6)
                chunk_t(PH_IN1["c"] + n, d * GSLOT, PH_IN1["b"] + b, n % 4)
                if n == 3 and not prev_on:
                    log_decay_sums()
                slot(n, g, True, prev_on)

        group(0, 0, False)
        with pe.Fori(1, NG) as g:
            group(g, g, True)
        for n in range(14 + 1):
            slot(n, NG, False, True)
        out_projection(PH_OUT1, list(range(NVH // 2)),
                       lambda kt: ((lambda k: ohi[:, kt, k]), (lambda k: olo[:, kt, k])),
                       lambda j: pe.wait_ge(s_ol, (2 * j + 1) // 4 + 1))
        norm_turn(3)
        feed_forward(3, PH_FF1, PH_DN1)

    @block.scalar
    def _(act):
        def split_hi(c, d):
            if c >= CHUNKS and not looped(d):
                return
            act.wait_ge(s_raw[c % RING], d * (16 // RING) + 16 * (c // RING + 1))
            if c >= RING or looped(d):
                act.wait_ge(s_used, d + (c - RING + 1))
            nc.scalar.activation(whi[:, c % RING, :], raw[:, c % RING, :], ACT.Copy).then_inc(s_hi, 1)

        def copy_half(c_last, dc, b, db, tiles=2):
            act.wait_ge(s_used, dc + (c_last + 1))
            if b >= 1:
                act.wait_ge(s_evac, db + b)
            b2 = 2 * (b % 2)
            nc.scalar.activation(halfa[:, 0:tiles, :], dn[:, b2:b2 + tiles, 0:S], ACT.Copy).then_inc(s_ca, 1)

        def square_x(n):
            for b in range(NCB):
                for t in range(NT):
                    if n == 0:
                        act.wait_ge(s_x, 32)
                    else:
                        act.wait_ge(s_xup, 8 * (n - 1) + NT * b + t + 1)
                    seq = 8 * n + NT * b + t
                    if n >= 1:
                        act.wait_ge(s_sqm, 8 * n)
                    if seq >= 1:
                        act.wait_ge(s_sqx, seq)
                    nc.scalar.activation(junk[:, :], x[:, t, b * NW:(b + 1) * NW], ACT.Square,
                                         accum_out=ssx[:, t, b:b + 1]).then_inc(s_sqx, 1)

        def norm(n):
            square_x(n)
            g0 = n // 2 * KT + (2 * KT if n % 2 else 0)
            act.wait_ge(s_rs, 2 * n + 1)

            def scale(kg):
                if kg >= 2:
                    act.wait_ge(s_xtp, 4 * n + kg - 1)
                at_ = (kg % 2) * NT * 512
                nc.scalar.activation(scr[:, at_:at_ + 512], x[:, 0, kg * 512:(kg + 1) * 512], ACT.Copy,
                                     scale=rstd[:, 0, 0:1]).then_inc(s_xs0, 1)

            scale(0)
            scale(1)
            for kg in range(4):
                act.wait_ge(s_xtp, 4 * n + kg + 1)
                for q in range(4):
                    kt = 4 * kg + q
                    nc.scalar.activation(hn[:, kt, 0:S], mi[:, 2 * (kg % 2) + q // 2, (q % 2) * S:(q % 2 + 1) * S],
                                         ACT.Copy, scale=vecT[:, g0 + kt:g0 + kt + 1]).then_inc(s_hnh, 1)
                if kg + 2 < 4:
                    scale(kg + 2)

        def out_projection(ph, n, sq_base, final=False):
            def body(i, d):
                for u in range(2):
                    for j in range(n):
                        c = ph["c"] + u * n + j
                        if not (final and c + LEAD + (d if isinstance(d, int) else 0) >= CHUNKS):
                            split_hi(c + LEAD, d)
                        if j == n - 1:
                            act.wait_ge(s_used, d + (c + 1))
                            act.wait_ge(s_sqx, sq_base + 8)
                            for t in range(NT):
                                act.wait_ge(s_sqm, i * 4 + (sq_base + 2 * u + t))
                                nc.scalar.activation(junk[:, :], dn[:, 2 * ((ph["b"] + u) % 2) + t, :], ACT.Square,
                                                     accum_out=ssm[:, t, i * 2 + u:i * 2 + u + 1] if isinstance(i, int)
                                                     else ssm[:, t, bass.ds(i * 2 + u, 1)]).then_inc(s_sqm, 1)
            if final:
                for i in range(NCB // 2):
                    body(i, i * 2 * n)
            else:
                with act.Fori(0, NCB // 2) as i:
                    body(i, i * (2 * n))

        def feed_forward(layer, ph, pd, final):
            with act.Fori(0, FI) as i:
                for j in range(8):
                    split_hi(ph["c"] + j + LEAD, i * 8)
                    if j == 3:
                        copy_half(ph["c"] + 3, i * 8, ph["b"], i * 2)
                    if j == 4:
                        act.wait_ge(s_evac, i * 2 + (ph["b"] + 1))
                        nc.scalar.activation(fth, fg, ACT.Tanh, scale=0.5).then_inc(s_th, 1)
                    if j == 7:
                        copy_half(ph["c"] + 7, i * 8, ph["b"] + 1, i * 2)
                        act.wait_ge(s_h, i + (FI * layer + 1))
                        nc.scalar.activation(hid[:, bass.ds(i * 2, 2), 0:S], fh, ACT.Copy).then_inc(s_hh, 1)
            out_projection(pd, FF // P // 2, 8 * (2 * layer + 1), final)

        act.wait_ge(s_vecp, 1)
        nc.scalar.activation(vecT[:, :], mi[:, BX, 0:4 * KT + 9], ACT.Copy).then_inc(s_vec, 1)
        for h in range(NH):
            act.wait_ge(s_bsp, h + 1)
            nc.scalar.activation(bseg[:, h, :], mi[:, h % 2, 0:SEG], ACT.Copy).then_inc(s_bs, 1)
        split_hi(0, 0)
        split_hi(1, 0)
        act.wait_ge(s_vec, 1)
        norm(0)

        def exps(h):
            act.wait_ge(s_mx, NT * (h + 1))
            for t in range(NT):
                w = P * (t + 1)
                v = prob[:, h % 2, t * P:t * P + w]
                nc.scalar.activation(v, v, ACT.Exp, bias=mx[:, h, t:t + 1],
                                     accum_out=psm[:, h, t:t + 1]).then_inc(s_ex, 1)

        for s in range(len(chunks0) + 3):
            if s < len(chunks0):
                split_hi(s + LEAD, 0)
            if s in evac_at and blocks0[evac_at[s]][0] != "v":
                n = evac_at[s]
                copy_half(s - 1, 0, n, 0, tiles=1 if n == 0 else 2)
            if 7 <= s < 7 + NIH:
                ih = s - 7
                act.wait_ge(s_dot, ih + 1)
                if ih >= 2:
                    act.wait_ge(s_sc, NT * (ih - 1))
                nc.scalar.activation(rel[:, ih % 2, :], mi[:, ih % 2, 0:3 * P], ACT.Relu,
                                     scale=DIH ** -0.5).then_inc(s_rel, 1)
            if s - 1 in head_at:
                exps(head_at[s - 1])
            if s - 2 in head_at:
                h = head_at[s - 2]
                act.wait_ge(s_ptp, h + 1)
                if h >= 1:
                    act.wait_ge(s_ov, h)
                nc.scalar.activation(pT[:, :], mi[:, 1, 0:3 * P], ACT.Copy).then_inc(s_pt, 1)
            if s - 3 in head_at:
                h = head_at[s - 3]
                act.wait_ge(s_ov, h + 1)
                nc.scalar.activation(mix[:, h, 0:S], mi[:, 2, 0:S], ACT.Copy).then_inc(s_mh_, 1)
            for k in range(4):
                if s == end0[17 + k] + 2:
                    gi = xp_order[k]
                    act.wait_ge(s_mp, k + 1)
                    for dt in range(2):
                        col = 4 * KT + 2 * gi + dt
                        nc.scalar.activation(mix[:, NH + 2 * gi + dt, 0:S], mi[:, 3, dt * S:(dt + 1) * S], ACT.Copy,
                                             scale=vecT[:, col:col + 1]).then_inc(s_ph, 1)
        out_projection(PH_OUT0, KT // 2, 0)
        norm(1)
        feed_forward(0, PH_FF0, PH_DN0, False)
        norm(2)
        act.wait_ge(s_cwp, 1)
        nc.scalar.activation(cwT[:, :, :].rearrange("p a b -> p (a b)"), mi[:, BX, 0:256], ACT.Copy,
                             scale=0.5).then_inc(s_cw, 1)
        split_hi(PH_BA["c"] + LEAD, 0)
        split_hi(PH_BA["c"] + 1 + LEAD, 0)
        copy_half(PH_BA["c"] + 1, 0, PH_BA["b"], 0, tiles=1)

        def gates(step):
            if step == 0:
                act.wait_ge(s_mn, 1)
                nc.scalar.activation(bat[:, 0, :, :], ba[:, :, 0:NVH], ACT.Exp, scale=-1.0).then_inc(s_ea, 1)
                nc.scalar.activation(bat[:, 2, :, :], bat[:, 2, :, :], ACT.Exp).then_inc(s_ea, 1)
                nc.scalar.activation(avec[:, 1, :], avec[:, 1, :], ACT.Exp).then_inc(s_ea, 1)
            if step == 1:
                act.wait_ge(s_ea, 2)
                nc.scalar.activation(bat[:, 3, :, :], bat[:, 2, :, :], ACT.Ln, bias=1.0).then_inc(s_el, 1)
            if step == 2:
                act.wait_ge(s_gc, 1)
                nc.scalar.activation(sc4[:, 2, :, :], sc4[:, 1, :, :], ACT.Exp).then_inc(s_eg, 1)

        def evac(g, b):
            copy_half(PH_IN1["c"] + 4 * b + 3, g * GSLOT, PH_IN1["b"] + b, g * 6)

        def tap0(g, b):
            act.wait_ge(s_evac, g * 6 + (PH_IN1["b"] + b + 1))
            act.wait_ge(s_cwc, g * 1 + 1)
            for f in range(2):
                k = 2 * b + f
                i = nc.scalar.activation(conv_y[:, f, :], cpad[:, f, 3:3 + S], ACT.Copy,
                                         scale=cwc[:, 3, k:k + 1])
            i.then_inc(s_tap0, 1)

        def tanh(g, k):
            if k < 4:
                act.wait_ge(s_tap, g * 24 + 6 * (k + 1))
                nc.scalar.activation(conv_th, conv_y, ACT.Tanh).then_inc(s_thc, 1)
            else:
                act.wait_ge(s_evac, g * 6 + (PH_IN1["b"] + k + 1))
                z = zs[:, 2 * (k - 4):2 * (k - 4) + 2, :]
                nc.scalar.activation(conv_th, z, ACT.Tanh, scale=0.5).then_inc(s_thc, 1)

        def decays(g, c):
            act.wait_ge(s_clamp, g * 2 + (c + 1))
            if c == 1:
                nc.scalar.activation(qd[:, :, :].rearrange("p a b -> p (a b)"), mi[:, BM, :], ACT.Exp).then_inc(s_eq, 1)
            nc.scalar.activation(dec[:, c, :, :], dec[:, c, :, :], ACT.Exp).then_inc(s_dec, 1)

        def squares(g):
            act.wait_ge(s_silu, g * 4 + 2)
            nc.scalar.activation(sqkq, kqr[:, :, :, :].rearrange("p a b c -> p a (b c)"), ACT.Square).then_inc(s_sqk, 1)

        def o_squares(g, k):
            act.wait_ge(s_op, g * 2 + (k + 1))
            nc.scalar.activation(osq[:, k, :], mi[:, (BX, BT)[k], :], ACT.Square).then_inc(s_osq, 1)

        def roots(g, k):
            act.wait_ge(s_ss, g * 2 + (k + 1))
            sc_ = 1.0 if k == 0 else float(DH)
            nc.scalar.activation(sqkq[:, k, :], mi[:, (BM, BY)[k], :], ACT.Sqrt, scale=sc_,
                                 bias=epsc[:, k:k + 1]).then_inc(s_rt, 1)

        def o_roots(g, k):
            act.wait_ge(s_og_ss, g * 2 + (k + 1))
            nc.scalar.activation(osq[:, k, :], mi[:, (BM, BY)[k], :], ACT.Sqrt, scale=1.0 / DH,
                                 bias=epsc[:, 0:1]).then_inc(s_ort, 1)

        def copy_v(g, half):
            act.wait_ge(s_vtp, g * 2 + (half + 1))
            nc.scalar.activation(vtok[:, :, 2 * half:2 * half + 2, :],
                                 mi[:, BM, :].rearrange("p (a b c) -> p a b c", a=2, b=2), ACT.Copy).then_inc(s_vt, 1)

        def copy_x1(g, b):
            act.wait_ge(s_x1p, g * 2 + (b + 1))
            nc.scalar.activation(xi[:, b, :, :].rearrange("p a b -> p (a b)"), mi[:, BM, :], ACT.Copy).then_inc(s_x1, 1)

        def copy_k(g):
            act.wait_ge(s_ktp, g * 1 + 1)
            nc.scalar.activation(ktok[:, :, :].rearrange("p a b -> p (a b)"), mi[:, BM, 0:256], ACT.Copy).then_inc(s_kt, 1)

        def copy_x(g, b, lev):
            act.wait_ge(s_xx, g * 12 + (2 * (lev - 1) + b + 1))
            if lev < NLEV:
                nc.scalar.activation(xi[:, b, :, :].rearrange("p a b -> p (a b)"), mi[:, BX, :], ACT.Copy)
            nc.scalar.activation(xt[:, b, :, :].rearrange("p a b -> p (a b)"), mi[:, BT, :], ACT.Copy).then_inc(s_xe, 1)

        def slot(n, g, cur_on, prev_on):
            if prev_on:
                h, m = g - 1, n + GSLOT
                if m == 24:
                    evac(h, 5)
                if m == 25:
                    tanh(h, 5)
                for b in range(2):
                    lev, odd = divmod(m - 20 - b, 2)
                    if odd == 1 and 1 <= lev + 1 <= NLEV:
                        copy_x(h, b, lev + 1)
                if m == 33:
                    act.wait_ge(s_sp_, h * 1 + 1)
                    nc.scalar.activation(st[:, :, :].rearrange("p a b -> p (a b)"), mi[:, BY, :], ACT.Copy).then_inc(s_st, 1)
            if cur_on:
                if n % 4 == 0 and n > 0:
                    evac(g, n // 4 - 1)
                if n in (5, 9, 13, 17):
                    tap0(g, n // 4 - 1)
                if n in (6, 10, 14, 18):
                    tanh(g, n // 4 - 1)
                if n == 21:
                    tanh(g, 4)
                if n in (12, 13):
                    decays(g, n - 12)
                if n == 12:
                    squares(g)
            if prev_on:
                if m == 37:
                    o_squares(h, 0)
                    o_squares(h, 1)
            if cur_on and n == 14:
                roots(g, 0)
                roots(g, 1)
            if prev_on and n == 14:
                o_roots(h, 0)
                o_roots(h, 1)
            if cur_on:
                if n == 18:
                    copy_v(g, 0)
                if n == 19:
                    copy_x1(g, 0)
                if n == 20:
                    copy_x1(g, 1)
                for b in range(2):
                    lev, odd = divmod(n - 20 - b, 2)
                    if odd == 1 and lev >= 0:
                        copy_x(g, b, lev + 1)
                if n == 21:
                    copy_v(g, 1)
                if n == 22:
                    copy_k(g)

        def group(g, d, prev_on):
            for n in range(GSLOT):
                split_hi(PH_IN1["c"] + n + LEAD, d * GSLOT)
                if not prev_on and n in (0, 1):
                    gates(n)
                if not prev_on and n == 4:
                    gates(2)
                slot(n, g, True, prev_on)

        group(0, 0, False)
        with act.Fori(1, NG) as g:
            group(g, g, True)
        for n in range(15):
            slot(n, NG, False, True)
        for k in range(NVH // 4):
            act.wait_ge(s_og, 2 * NG)
            act.wait_ge(s_used, PH_OUT1["c"])
            nc.scalar.activation(ohi[:, 4 * k:4 * k + 4, :], o32[:, 4 * k:4 * k + 4, :], ACT.Copy).then_inc(s_oh, 1)
        out_projection(PH_OUT1, NVH // 2, 16)
        norm(3)
        feed_forward(1, PH_FF1, PH_DN1, True)

    @block.vector
    def _(v):
        def split_lo(c, d):
            if c >= CHUNKS and not looped(d):
                return
            v.wait_ge(s_hi, d + (c + 1))
            nc.vector.tensor_tensor(wlo[:, c % RING, :], raw[:, c % RING, :], whi[:, c % RING, :].bitcast(F32),
                                    ALU.subtract).then_inc(s_lo, 1)

        def add_halves(out, b, t, dt, tiles=2):
            v.wait_ge(s_ca, dt + (t + 1))
            b2 = 2 * (b % 2)
            nc.vector.tensor_tensor(out, dn[:, b2:b2 + tiles, S:2 * S], halfa[:, 0:tiles, :], ALU.add).then_inc(s_evac, 1)

        def root_input(n, sums, cond):
            v.wait_ge(*cond)
            if n >= 2:
                v.wait_ge(s_rs, n - 1)
            nc.vector.tensor_reduce(tot[:, n % 2, :], sums[:, :, :], AX, ALU.add).then_inc(s_tot, 1)
            v.wait_ge(s_tot, n + 1)
            nc.vector.tensor_scalar(meansq[:, n % 2, :], tot[:, n % 2, :], 1.0 / D, EPS, ALU.mult, ALU.add).then_inc(s_ms, 1)

        def norm(n):
            root_input(2 * n, ssx, (s_sqx, 8 * (n + 1)))
            v.wait_ge(s_rs, 2 * n + 1)
            g0 = n // 2 * KT + (2 * KT if n % 2 else 0)

            def scale(kg):
                if kg >= 2:
                    v.wait_ge(s_xtp, 4 * n + kg - 1)
                at_ = ((kg % 2) * NT + 1) * 512
                nc.vector.tensor_scalar(scr[:, at_:at_ + 512], x[:, 1, kg * 512:(kg + 1) * 512], rstd[:, 0, 1:2],
                                        None, ALU.mult).then_inc(s_xs1, 1)

            scale(0)
            scale(1)
            for kg in range(4):
                for q in range(4):
                    kt = 4 * kg + q
                    v.wait_ge(s_hnh, 16 * n + 2 * (kt // 2) + 2)
                    nc.vector.scalar_tensor_tensor(out=hn[:, kt, S:2 * S],
                                                   in0=mi[:, 2 * (kg % 2) + q // 2, (q % 2) * S:(q % 2 + 1) * S],
                                                   scalar=vecT[:, g0 + kt:g0 + kt + 1], in1=hn[:, kt, 0:S].bitcast(F32),
                                                   op0=ALU.mult, op1=ALU.subtract).then_inc(s_hnl, 1)
                if kg + 2 < 4:
                    scale(kg + 2)

        def update_x(n, m):
            root_input(2 * n + 1, ssm, (s_sqm, 8 * (n + 1)))
            v.wait_ge(s_rs, 2 * n + 2)
            for b in range(NCB):
                for t in range(NT):
                    cs = slice(b * NW, (b + 1) * NW)
                    nc.vector.scalar_tensor_tensor(out=x[:, t, cs], in0=m[:, t, cs], scalar=rstd[:, 1, t:t + 1],
                                                   in1=x[:, t, cs], op0=ALU.mult, op1=ALU.add).then_inc(s_xup, 1)

        def out_projection(n_norm, ph, n, m, gn, final=False):
            def body(i, d):
                for u in range(2):
                    for j in range(n):
                        c = ph["c"] + u * n + j
                        if not (final and c + LEAD + (d if isinstance(d, int) else 0) >= CHUNKS):
                            split_lo(c + LEAD, d)
                        if j == n - 1:
                            v.wait_ge(s_gain, 16 * (n_norm + 1))
                            cs = bass.ds(i * (2 * NW) + u * NW, NW)
                            for t in range(NT):
                                v.wait_ge(s_sqm, i * 4 + (8 * n_norm + 2 * u + t + 1))
                                e = nc.vector.tensor_tensor(m[:, t, cs], dn[:, 2 * ((ph["b"] + u) % 2) + t, :],
                                                            gn[:, cs], ALU.mult)
                            e.then_inc(s_evac, 1)
            if final:
                for i in range(NCB // 2):
                    body(i, i * 2 * n)
            else:
                with v.Fori(0, NCB // 2) as i:
                    body(i, i * (2 * n))
            v.wait_ge(s_evac, ph["b"] + NCB)
            update_x(n_norm, m)

        def feed_forward(layer, ph, pd, final):
            with v.Fori(0, FI) as i:
                for j in range(8):
                    split_lo(ph["c"] + j + LEAD, i * 8)
                    if j == 3:
                        add_halves(fg, ph["b"], ph["t"], i * 2)
                    if j == 5:
                        v.wait_ge(s_th, i + (FI * layer + 1))
                        nc.vector.scalar_tensor_tensor(out=fth, in0=fth, scalar=1.0, in1=fg, op0=ALU.add,
                                                       op1=ALU.mult).then_inc(s_t1, 1)
                    if j == 7:
                        add_halves(fu, ph["b"] + 1, ph["t"] + 1, i * 2)
                        v.wait_ge(s_evac, i * 2 + (ph["b"] + 2))
                        v.wait_ge(s_t1, i + (FI * layer + 1))
                        nc.vector.scalar_tensor_tensor(out=fh, in0=fth, scalar=0.5, in1=fu, op0=ALU.mult,
                                                       op1=ALU.mult).then_inc(s_h, 1)
                        v.wait_ge(s_hh, i + (FI * layer + 1))
                        nc.vector.tensor_tensor(hid[:, bass.ds(i * 2, 2), S:2 * S], fh,
                                                hid[:, bass.ds(i * 2, 2), 0:S].bitcast(F32), ALU.subtract).then_inc(s_hl, 1)
            out_projection(2 * layer + 1, pd, FF // P // 2, m_a, gain, final)

        nc.vector.memset(epsc[:, 0:1], EPS).then_inc(s_eps, 1)
        nc.vector.memset(epsc[:, 1:2], EPS * DH).then_inc(s_eps, 1)
        split_lo(0, 0)
        split_lo(1, 0)
        v.wait_ge(s_vec, 1)
        nc.vector.tensor_scalar(nwh[:, :], vecT[:, 4 * KT + 8:4 * KT + 9], 0.5, None, ALU.mult).then_inc(s_nwh, 1)
        norm(0)

        def score_add(ih):
            v.wait_ge(s_rel, ih + 1)
            for t in range(NT):
                w = P * (t + 1)
                cs = slice(t * P, t * P + w)
                if ih == 0:
                    nc.vector.tensor_scalar(score[:, cs], rel[:, 0, cs], wi[:, t, 0:1], None, ALU.mult).then_inc(s_sc, 1)
                else:
                    v.wait_ge(s_sc, NT * (ih - 1) + t + 1)
                    nc.vector.scalar_tensor_tensor(out=score[:, cs], in0=rel[:, ih % 2, cs], scalar=wi[:, t, ih:ih + 1],
                                                   in1=score[:, cs], op0=ALU.mult, op1=ALU.add).then_inc(s_sc, 1)

        def topk_round(r):
            if r == 0:
                v.wait_ge(s_causal, NT)
            for t in range(NT):
                w = P * (t + 1)
                if r >= 1:
                    v.wait_ge(s_repl, NT * (r - 1) + t + 1)
                nc.vector.max(top8[:, t, :], score[:, t * P:t * P + w]).then_inc(s_max8, 1)
            for t in range(NT):
                w = P * (t + 1)
                cs = slice(t * P, t * P + w)
                v.wait_ge(s_max8, NT * r + t + 1)
                nc.vector.match_replace(score[:, cs], top8[:, t, :], score[:, cs], TAKEN).then_inc(s_repl, 1)

        def soften(h):
            v.wait_ge(s_lg, h + 1)
            v.wait_ge(s_bm, h + 1)
            nc.vector.scalar_tensor_tensor(out=prob[:, h % 2, :], in0=mi[:, 0, 0:3 * P], scalar=float(DH) ** -0.5,
                                           in1=bm[:, h, :], op0=ALU.mult, op1=ALU.add).then_inc(s_lb, 1)
            v.wait_ge(s_lb, h + 1)
            for t in range(NT):
                w = P * (t + 1)
                nc.vector.tensor_reduce(mx[:, h, t:t + 1], prob[:, h % 2, t * P:t * P + w], AX, ALU.max,
                                        negate=True).then_inc(s_mx, 1)

        def scale_probs(h):
            v.wait_ge(s_ex, NT * (h + 1))
            nc.vector.reciprocal(rps[:, h, :], psm[:, h, :]).then_inc(s_rp, 1)
            v.wait_ge(s_rp, h + 1)
            for t in range(NT):
                w = P * (t + 1)
                pv = prob[:, h % 2, t * P:t * P + w]
                nc.vector.tensor_scalar(pv, pv, rps[:, h, t:t + 1], None, ALU.mult).then_inc(s_pn, 1)

        wins = [0]

        def pool_window(k):
            gi = xp_order[k]
            n = len(blocks0) - 4 + k
            v.wait_ge(s_evac, n + 1)
            if k >= 1:
                v.wait_ge(s_mp, k)
            src, step = xpad, 1
            for lev in range(gi + 1):
                dst = winb if (gi - lev) % 2 == 0 else wina
                lo = 2 * step - 1
                if wins[0]:
                    v.wait_ge(s_win, wins[0])
                nc.vector.tensor_tensor(dst[:, :, lo:16 + S], src[:, :, lo:16 + S], src[:, :, lo - step:16 + S - step],
                                        ALU.add).then_inc(s_win, 1)
                wins[0] += 1
                src, step = dst, 2 * step
            v.wait_ge(s_win, wins[0])
            inv = cst[:, K_INV + 16 * gi:K_INV + 16 * gi + 16].unsqueeze(1).broadcast_to([P, 2, 16])
            nc.vector.tensor_tensor(wina[:, :, 16:32], winb[:, :, 16:32], inv, ALU.mult).then_inc(s_win, 1)
            wins[0] += 1
            v.wait_ge(s_win, wins[0])
            nc.vector.tensor_tensor(wina[:, :, 16:32], wina[:, :, 16:32], xpad[:, :, 16:32], ALU.subtract).then_inc(s_pd, 1)
            nc.vector.scalar_tensor_tensor(out=wina[:, :, 32:16 + S], in0=winb[:, :, 32:16 + S], scalar=1.0 / WINDOWS[gi],
                                           in1=xpad[:, :, 32:16 + S], op0=ALU.mult, op1=ALU.subtract).then_inc(s_pd, 1)

        for s in range(len(chunks0) + 3):
            if s < len(chunks0):
                split_lo(s + LEAD, 0)
            if s in evac_at:
                n = evac_at[s]
                kind, idx, _, _ = blocks0[n]
                if kind == "kw":
                    add_halves(kiw[:, :].unsqueeze(1), n, tidx0[n], 0, tiles=1)
                elif kind == "qi":
                    add_halves(qiT[:, idx % 2, :, :], n, tidx0[n], 0)
                elif kind == "v":
                    v.wait_ge(s_used, s)
                    b2 = 2 * (n % 2)
                    nc.vector.tensor_copy(vtm[:, idx % 2, :, :], dn[:, b2:b2 + 2, 0:TW]).then_inc(s_evac, 1)
                elif kind == "k":
                    add_halves(kqT[:, 0, :, :], n, tidx0[n], 0)
                elif kind == "q":
                    add_halves(kqT[:, 1, :, :], n, tidx0[n], 0)
                else:
                    if n == len(blocks0) - 4:
                        v.wait_ge(s_pad, 3)
                    else:
                        v.wait_ge(s_pd, 2 * (n - len(blocks0) + 4))
                    add_halves(xpad[:, :, 16:16 + S], n, tidx0[n], 0)
            if s == 4:
                v.wait_ge(s_wip, 1)
                nc.vector.tensor_scalar(wi[:, :, :], mi[:, BX, 0:2 * P].rearrange("p (t f) -> p t f", t=2)[:, :, DIH:DIH + NIH],
                                        NIH ** -0.5, None, ALU.mult).then_inc(s_wi, 1)
                v.wait_ge(s_wi, 1)
            if 7 <= s < 7 + NIH:
                score_add(s - 7)
            if SC0 < s <= SC0 + NR:
                topk_round(s - SC0 - 1)
            if s == SC0 + NR + 1:
                v.wait_ge(s_repl, NT * NR)
                nc.vector.tensor_scalar(score[:, :], score[:, :], TAKEN / 3, NEG, ALU.is_gt, ALU.mult).then_inc(s_seln, 1)
            if s in head_at:
                soften(head_at[s])
            if s - 1 in head_at:
                scale_probs(head_at[s - 1])
            if s - 3 in head_at:
                h = head_at[s - 3]
                v.wait_ge(s_mh_, h + 1)
                nc.vector.tensor_tensor(mix[:, h, S:2 * S], mi[:, 2, 0:S], mix[:, h, 0:S].bitcast(F32),
                                        ALU.subtract).then_inc(s_ml, 1)
            for k in range(4):
                if s == end0[17 + k] + 1:
                    pool_window(k)
                if s == end0[17 + k] + 2:
                    gi = xp_order[k]
                    v.wait_ge(s_ph, 2 * (k + 1))
                    for dt in range(2):
                        col = 4 * KT + 2 * gi + dt
                        i = nc.vector.scalar_tensor_tensor(out=mix[:, NH + 2 * gi + dt, S:2 * S], in0=mi[:, 3, dt * S:(dt + 1) * S],
                                                           scalar=vecT[:, col:col + 1], in1=mix[:, NH + 2 * gi + dt, 0:S].bitcast(F32),
                                                           op0=ALU.mult, op1=ALU.subtract)
                    i.then_inc(s_pl, 1)
        out_projection(0, PH_OUT0, KT // 2, m_a, gain)
        norm(1)
        feed_forward(0, PH_FF0, PH_DN0, False)
        norm(2)
        split_lo(PH_BA["c"] + LEAD, 0)
        split_lo(PH_BA["c"] + 1 + LEAD, 0)
        add_halves(conv_y[:, 0:1, :], PH_BA["b"], PH_BA["t"], 0, tiles=1)

        def gates(step):
            if step == 0:
                v.wait_ge(s_bap, 1)
                nc.vector.tensor_copy(ba[:, :, :], mi[:, BY, 0:2 * P].rearrange("p (t f) -> p t f", t=2)[:, :, P - 2 * NVH:P]).then_inc(s_ba, 1)
                v.wait_ge(s_ba, 1)
                v.wait_ge(s_av, 32)
                nc.vector.tensor_tensor(bat[:, 1, :, :], ba[:, :, NVH:2 * NVH],
                                        avec[:, 0:1, :].broadcast_to([P, 2, NVH]), ALU.add).then_inc(s_t, 1)
                v.wait_ge(s_t, 1)
                nc.vector.scalar_tensor_tensor(out=bat[:, 2, :, :], in0=bat[:, 1, :, :], scalar=-1.0,
                                               in1=bat[:, 1, :, :], op0=ALU.mult, op1=ALU.min).then_inc(s_mn, 1)
            if step == 1:
                v.wait_ge(s_ea, 3)
                nc.vector.tensor_scalar(bat[:, 0, :, :], bat[:, 0, :, :], 1.0, None, ALU.add).then_inc(s_t, 1)
                v.wait_ge(s_t, 2)
                nc.vector.reciprocal(sc4[:, 3, :, :], bat[:, 0, :, :]).then_inc(s_t, 1)
            if step == 2:
                v.wait_ge(s_el, 1)
                nc.vector.scalar_tensor_tensor(out=bat[:, 1, :, :], in0=bat[:, 1, :, :], scalar=0.0,
                                               in1=bat[:, 3, :, :], op0=ALU.max, op1=ALU.add).then_inc(s_sp, 1)
                v.wait_ge(s_sp, 1)
                nc.vector.scalar_tensor_tensor(out=sc4[:, 0, :, :], in0=bat[:, 1, :, :], scalar=-1.0,
                                               in1=avec[:, 1:2, :].broadcast_to([P, 2, NVH]), op0=ALU.mult,
                                               op1=ALU.mult).then_inc(s_g, 1)
            if step == 3:
                v.wait_ge(s_gcp, 1)
                nc.vector.tensor_copy(sc4[:, 1, :, :], mi[:, BX, 256:256 + 2 * NVH].rearrange("p (a b) -> p a b", a=2)).then_inc(s_gc, 1)
            if step == 4:
                v.wait_ge(s_eg, 1)
                nc.vector.tensor_scalar(sc4[:, 2, :, :], sc4[:, 2, :, :], -1.0, None, ALU.mult).then_inc(s_sc4, 1)

        def take_scalars(g):
            if not looped(g):
                v.wait_ge(s_sc4, 1)
                v.wait_ge(s_t, 3)
            else:
                v.wait_ge(s_v1, g * 1)
            nc.vector.tensor_copy(cur[:, :, :, :], sc4[:, :, :, bass.ds(g * 4, 4)]).then_inc(s_cur, 1)

        def take_taps(g):
            if not looped(g):
                v.wait_ge(s_cw, 1)
            for at_, w, base, step in ((0, 2, NKH, 2), (2, 2, 0, 2), (4, 4, 2 * NKH, 4)):
                i = nc.vector.tensor_copy(cwc[:, :, at_:at_ + w], cwT[:, :, bass.ds(g * step + base, w)])
            i.then_inc(s_cwc, 1)

        def evac(g, b):
            out = cpad[:, :, 3:3 + S] if b < 4 else zs[:, 2 * (b - 4):2 * (b - 4) + 2, :]
            add_halves(out, PH_IN1["b"] + b, PH_IN1["t"] + b, g * 6)

        def taps(g, b):
            v.wait_ge(s_tap0, g * 4 + (b + 1))
            for k in range(3):
                for f in range(2):
                    if k >= 1:
                        v.wait_ge(s_tap, g * 24 + (6 * b + 2 * (k - 1) + f + 1))
                    nc.vector.scalar_tensor_tensor(out=conv_y[:, f, :], in0=cpad[:, f, 2 - k:2 - k + S],
                                                   scalar=cwc[:, 2 - k, 2 * b + f:2 * b + f + 1], in1=conv_y[:, f, :],
                                                   op0=ALU.mult, op1=ALU.add).then_inc(s_tap, 1)

        def silu(g, b):
            v.wait_ge(s_thc, g * 6 + (b + 1))
            out = kqr[:, b, :, :] if b < 2 else vfm[:, :, :]
            if b == 3:
                v.wait_ge(s_vtp, g * 2 + 1)
            nc.vector.scalar_tensor_tensor(out=out, in0=conv_th, scalar=1.0, in1=conv_y, op0=ALU.add,
                                           op1=ALU.mult).then_inc(s_silu, 1)

        def gate_z(g, k):
            v.wait_ge(s_thc, g * 6 + (5 + k))
            z = zs[:, 2 * k:2 * k + 2, :]
            nc.vector.scalar_tensor_tensor(out=z, in0=conv_th, scalar=1.0, in1=z, op0=ALU.add,
                                           op1=ALU.mult).then_inc(s_zg, 1)

        def clamp(g, c):
            v.wait_ge(s_gb, g * 2 + (c + 1))
            for u in range(4):
                i = nc.vector.tensor_scalar(dec[:, c, u, :], mi[:, BM, u * P:(u + 1) * P], cur[:, 1, c, u:u + 1], 0.0,
                                            ALU.subtract, ALU.min)
            i.then_inc(s_clamp, 1)

        def norm_kq(g):
            for k in range(2):
                v.wait_ge(s_rt, g * 2 + (k + 1))
                nc.vector.reciprocal(sqkq[:, k, :], sqkq[:, k, :]).then_inc(s_rc, 1)
            for k in range(2):
                v.wait_ge(s_rc, g * 2 + (k + 1))
                nc.vector.tensor_tensor(kq[:, k, :, :].rearrange("p b c -> p (b c)"),
                                        kqr[:, k, :, :].rearrange("p b c -> p (b c)"), sqkq[:, k, :], ALU.mult).then_inc(s_kqn, 1)

        def norm_o(g):
            for k in range(2):
                v.wait_ge(s_ort, g * 2 + (k + 1))
                nc.vector.reciprocal(osq[:, k, :], osq[:, k, :]).then_inc(s_orc, 1)
            for k in range(2):
                v.wait_ge(s_orc, g * 2 + (k + 1))
                nc.vector.tensor_tensor(osq[:, k, :], mi[:, (BX, BT)[k], :], osq[:, k, :], ALU.mult).then_inc(s_on, 1)
            for k in range(2):
                v.wait_ge(s_on, g * 2 + (k + 1))
                v.wait_ge(s_zg, g * 2 + (k + 1))
                nc.vector.scalar_tensor_tensor(out=o32[:, bass.ds(g * 4 + 2 * k, 2), :],
                                               in0=osq[:, k, :].rearrange("p (a b) -> p a b", a=2), scalar=nwh[:, 0:1],
                                               in1=zs[:, 2 * k:2 * k + 2, :], op0=ALU.mult, op1=ALU.mult).then_inc(s_og, 1)

        def weigh(g, c):
            v.wait_ge(s_gq, g * 2 + (c + 1))
            v.wait_ge(s_dec, g * 2 + (c + 1))
            for u in range(4):
                kp = u // 2
                i = nc.vector.scalar_tensor_tensor(out=at[:, c, u, :], in0=mi[:, BM, kp * 256:kp * 256 + P],
                                                   scalar=cur[:, 3, c, u:u + 1], in1=dec[:, c, u, :], op0=ALU.mult,
                                                   op1=ALU.mult)
            i.then_inc(s_atr, 1)
            for kp in range(2):
                i = nc.vector.tensor_tensor(intra[:, c, 2 * kp:2 * kp + 2, :],
                                            mi[:, BM, kp * 256 + P:kp * 256 + 2 * P].unsqueeze(1).broadcast_to([P, 2, P]),
                                            dec[:, c, 2 * kp:2 * kp + 2, :], ALU.mult)
            i.then_inc(s_inr, 1)

        def first_x(g, b):
            v.wait_ge(s_at, g * 2 + (b + 1))
            nc.vector.tensor_tensor(xt[:, b, :, :], at[:, b, :, :],
                                    cst[:, K_M0:K_M0 + P].unsqueeze(1).broadcast_to([P, 4, P]), ALU.mult).then_inc(s_x1t, 1)

        def mask_w(g, b, lev):
            v.wait_ge(s_y, g * 12 + (2 * (lev - 1) + b + 1))
            mk = cst[:, K_MT + (lev - 1) * P:K_MT + lev * P].unsqueeze(1).broadcast_to([P, 4, P])
            nc.vector.tensor_tensor(wy[:, b, :, :], mi[:, BY, :].rearrange("p (a b) -> p a b", a=4), mk,
                                    ALU.mult).then_inc(s_w, 1)

        def decay_q(g):
            v.wait_ge(s_eq, g * 1 + 1)
            v.wait_ge(s_kqn, g * 2 + 2)
            for kp in range(2):
                i = nc.vector.tensor_tensor(qd[:, 2 * kp:2 * kp + 2, :], qd[:, 2 * kp:2 * kp + 2, :],
                                            kq[:, 1, kp:kp + 1, P:S].broadcast_to([P, 2, P]), ALU.mult)
            i.then_inc(s_qd, 1)

        def decay_k(g):
            v.wait_ge(s_kt, g * 1 + 1)
            for u in range(4):
                i = nc.vector.tensor_scalar(kdec[:, u, :], ktok[:, u // 2, :], dec[:, 0, u, P - 1:P], None, ALU.mult)
            i.then_inc(s_kd, 1)

        def times_beta(g, c):
            v.wait_ge((s_y0, s_y1)[c], g * 1 + 1)
            for u in range(4):
                i = nc.vector.tensor_scalar(vn[:, c, u, :], mi[:, BY, u * P:(u + 1) * P], cur[:, 3, c, u:u + 1], None,
                                            ALU.mult)
            i.then_inc((s_v0, s_v1)[c], 1)

        def rhs1(g):
            v.wait_ge(s_ks, g * 1 + 1)
            for u in range(4):
                i = nc.vector.scalar_tensor_tensor(out=vtok[:, 1, u, :], in0=mi[:, BY, u * P:(u + 1) * P],
                                                   scalar=cur[:, 2, 1, u:u + 1], in1=vtok[:, 1, u, :], op0=ALU.mult,
                                                   op1=ALU.add)
            i.then_inc(s_r1, 1)

        def slot(n, g, cur_on, prev_on):
            if prev_on:
                h, m = g - 1, n + GSLOT
                if m == 24:
                    evac(h, 5)
                if m == 26:
                    gate_z(h, 1)
                for b in range(2):
                    lev, odd = divmod(m - 20 - b, 2)
                    if odd == 0 and 1 <= lev + 1 <= NLEV:
                        mask_w(h, b, lev + 1)
                if m == 32:
                    times_beta(h, 0)
                if m == 34:
                    rhs1(h)
                if m == 35:
                    times_beta(h, 1)
            if cur_on:
                if n == 3:
                    take_taps(g)
                if n % 4 == 0 and n > 0:
                    evac(g, n // 4 - 1)
                if n in (5, 9, 13, 17):
                    taps(g, n // 4 - 1)
                if n in (7, 11, 15, 19):
                    silu(g, n // 4 - 1)
                if n == 11:
                    take_scalars(g)
                if n in (12, 13):
                    clamp(g, n - 12)
                if n == 15:
                    norm_kq(g)
            if prev_on and n == 15:
                norm_o(h)
            if cur_on:
                if n in (16, 17):
                    weigh(g, n - 16)
                if n == 17:
                    first_x(g, 0)
                if n == 18:
                    first_x(g, 1)
                    decay_q(g)
                if n == 22:
                    gate_z(g, 0)
                if n == 23:
                    decay_k(g)
                for b in range(2):
                    lev, odd = divmod(n - 20 - b, 2)
                    if odd == 0 and lev >= 0:
                        mask_w(g, b, lev + 1)

        def group(g, d, prev_on):
            for n in range(GSLOT):
                split_lo(PH_IN1["c"] + n + LEAD, d * GSLOT)
                if not prev_on and n < 5:
                    gates(n)
                slot(n, g, True, prev_on)

        v.wait_ge(s_pz, 1)
        group(0, 0, False)
        with v.Fori(1, NG) as g:
            group(g, g, True)
        for n in range(16):
            slot(n, NG, False, True)
        for k in range(NVH // 4):
            v.wait_ge(s_oh, k + 1)
            nc.vector.tensor_tensor(olo[:, 4 * k:4 * k + 4, :], o32[:, 4 * k:4 * k + 4, :],
                                    ohi[:, 4 * k:4 * k + 4, :].bitcast(F32), ALU.subtract).then_inc(s_ol, 1)
        out_projection(2, PH_OUT1, NVH // 2, m_b, gain_b)
        norm(3)
        feed_forward(1, PH_FF1, PH_DN1, True)


_INS = ["x", "rel_bias", "even_w_in", "even_w_o", "pool_w", "pool_scale", "odd_w_in", "conv_w", "a_log", "dt_bias",
        "gdn_norm_w", "odd_w_o", "ffn_w_gate", "ffn_w_up", "ffn_w_down", "mix_pre_g", "mix_post_g", "ffn_pre_g",
        "ffn_post_g"]


def kernel(**inputs):
    import numpy as _np
    import concourse.bacc as _bacc
    from concourse.bass_utils import run_bass_kernel_spmd as _run

    nc = _bacc.Bacc("TRN2", target_bir_lowering=False, num_devices=1)
    arrays, io = {}, {}
    given = {n: _np.ascontiguousarray(inputs[n]) for n in _INS}
    given["consts"] = constants()
    given["onehot"] = bucket_onehot()
    for name, a in given.items():
        arrays[f"in_{name}"] = a
        io[name] = nc.dram_tensor(f"in_{name}", a.shape, F32, kind="ExternalInput").ap()
    io["out"] = nc.dram_tensor("out_x", (1, S, D), F32, kind="ExternalOutput").ap()
    trunk(nc, io)
    r = _run(nc, [arrays], core_ids=[0])
    return r.results[0]["out_x"]
```

```python
from contextlib import ExitStack
import math

import numpy as np

import concourse.bass as bass
from concourse import mybir

F32 = mybir.dt.float32
F32R = mybir.dt.float32r
ALU = mybir.AluOpType
ACT = mybir.ActivationFunctionType
AX = mybir.AxisListType.X

P = 128
D = 2048
S = 256
NT = S // P
KT = D // P
AW = D // 2
DH = 128
NH = AW // DH
NIH, DIH = 16, 64
TOPK = min(256, S // 4)
NEG = -1e30
TAKEN = -3e38
WINDOWS = (2, 4, 8, 16)
PGW = D // 8
NB = 32
EVEN_IN = 3 * AW + NIH * DIH + DIH + NIH + len(WINDOWS) * PGW
C_QI, C_KI, C_XP = 3 * AW, 3 * AW + NIH * DIH, 3 * AW + NIH * DIH + DIH + NIH
NKH = D // 128
NVH = 2 * NKH
QKW, VW = NKH * 128, NVH * 128
CONVW = 2 * QKW + VW
NTAP = 4
ODD_IN = CONVW + VW + 2 * NVH
FF = -(-8 * D // (3 * 256)) * 256
EPS = 1e-6
NSEG = P + S - 1
SEG = S + P

CH = 1024
RING = 4
LEAD = 3
TW, NW = 256, 512
NCB = D // NW
FI = FF // TW
NG = NKH // 2
GSLOT = 24
OVER0 = 3
NFREE = NKH - 2
NLEV = 6

PH_IN0 = dict(c=0, b=0, t=0)
PH_OUT0 = dict(c=82, b=21, t=17)


def _after(ph, c, b, t):
    return dict(c=ph["c"] + c, b=ph["b"] + b, t=ph["t"] + t)


PH_FF0 = _after(PH_OUT0, NCB * KT // 2, NCB, 0)
PH_DN0 = _after(PH_FF0, 8 * FI, 2 * FI, 2 * FI)
PH_BA = _after(PH_DN0, NCB * FF // P // 2, NCB, 0)
PH_IN1 = _after(PH_BA, 2, 1, 1)
PH_OUT1 = _after(PH_IN1, GSLOT * NG, 6 * NG, 6 * NG)
PH_FF1 = _after(PH_OUT1, NCB * NVH // 2, NCB, 0)
PH_DN1 = _after(PH_FF1, 8 * FI, 2 * FI, 2 * FI)
CHUNKS = PH_DN1["c"] + NCB * FF // P // 2

K_ID, K_ONE, K_U, K_M0 = 0, P, 2 * P, 3 * P
K_MT = 4 * P
K_INV = K_MT + (NLEV - 1) * P + P // 2
K_END = K_INV + len(WINDOWS) * 16


def constants():
    k = np.zeros((P, K_END), np.float32)
    i, j = np.arange(P)[:, None], np.arange(P)[None, :]
    k[:, K_ID:K_ID + P] = np.eye(P)
    k[:, K_ONE:K_ONE + P] = 1
    k[:, K_U:K_U + P] = i <= j
    hf = P // 2
    for lev in range(NLEV + 1):
        s = 2 ** lev
        off = (i // (2 * s) == j // (2 * s)) & (i // s % 2 == 1) & (j // s % 2 == 0)
        m = np.eye(P) - off
        if lev == 0:
            k[:, K_M0:K_M0 + P] = m.T
        else:
            even = m[:, j[0] // s % 2 == 0]
            at = K_MT + (lev - 1) * P
            if lev == NLEV:
                k[:, at:at + hf] = even
            else:
                q = even[:hf, :hf // 2]
                for seg in range(4):
                    r = (0, hf, 0, hf)[seg]
                    k[r:r + hf, at + seg * hf // 2:at + (seg + 1) * hf // 2] = q
    for n, w in enumerate(WINDOWS):
        k[:, K_INV + 16 * n:K_INV + 16 * n + 16] = 1.0 / np.minimum(np.arange(16) + 1, w)
    return k


def bucket_onehot():
    d = np.maximum(S - 1 - np.arange(SEG), 0)
    half = NB // 2
    ratio = np.log(np.maximum(d, 1).astype(np.float32) / half) / math.log(128 / half)
    large = np.minimum(half + (ratio.astype(np.float32) * (NB - half)).astype(np.int32), NB - 1)
    b = np.where(d < half, d, large)
    return (np.arange(NB)[:, None] == b[None, :]).astype(np.float32)


def level_half(ap, lev, odd):
    s = 2 ** lev
    return ap.rearrange("p u (g t s) -> p u g t s", t=2, s=s)[:, :, :, odd, :]


def looped(d):
    return not isinstance(d, int)


def trunk(nc, io):
    with ExitStack() as ctx:
        program(nc, io, ctx)


def program(nc, io, ctx):
    names = set()

    def sb(name, shape, dt=F32, at=ctx):
        return at.enter_context(nc.sbuf_tensor(name, shape, dt))

    def sem(name):
        assert name not in names
        names.add(name)
        return ctx.enter_context(nc.semaphore(name))

    x = sb("x_res", [P, NT, D])
    raw = sb("w_raw", [P, RING, CH])
    whi = sb("w_hi", [P, RING, CH], F32R)
    wlo = sb("w_lo", [P, RING, CH], F32R)
    halfa = sb("halfa", [P, 2, S])
    scr = sb("scr", [P, D])
    cst = sb("cst", [P, K_END])
    nrm = sb("nrm", [P, 16])
    vecT = sb("vecT", [P, 4 * KT + 8 + 1])
    junk = sb("junk", [P, NW])
    ssx = sb("ssx", [P, NT, NCB])
    ssm = sb("ssm", [P, NT, NCB])
    tot = sb("tot", [P, 2, NT])
    meansq = sb("meansq", [P, 2, NT])
    rstd = sb("rstd", [P, 2, NT])
    mhalf = sb("mhalf", [P, NT])
    nwh = sb("nwh", [P, 1])
    epsc = sb("epsc", [P, 2])
    warm = sb("warm", [P, 1])
    ident = cst[:, K_ID:K_ID + P]
    ones = cst[:, K_ONE:K_ONE + P]
    triu = cst[:, K_U:K_U + P]

    with ExitStack() as a1:
        hn = sb("hn", [P, KT, 2 * S], F32R, a1)
    with ExitStack() as a2:
        m_a = sb("m_a", [P, NT, D], F32, a2)
        gain = sb("gain", [P, D], F32, a2)
    with ExitStack() as a3:
        ohi = sb("ohi", [P, NVH, S], F32R, a3)
    sb("region_a", [P, KT * 2 * S])

    with ExitStack() as b1:
        mix = sb("mix", [P, KT, 2 * S], F32R, b1)
        qiT = sb("qiT", [P, 2, 2, S], F32, b1)
        kiw = sb("kiw", [P, S], F32, b1)
        kid = sb("kid", [P, S], F32, b1)
        wi = sb("wi", [P, NT, NIH], F32, b1)
        rel = sb("rel", [P, 2, 3 * P], F32, b1)
        score = sb("score", [P, 3 * P], F32, b1)
        top8 = sb("top8", [P, NT, 8], F32, b1)
        bm = sb("bm", [P, NH, 3 * P], F32, b1)
        kqT = sb("kqT", [P, 2, 2, S], F32, b1)
        vtm = sb("vtm", [P, 2, NT, TW], F32, b1)
        prob = sb("prob", [P, 2, 3 * P], F32, b1)
        pT = sb("pT", [P, 3 * P], F32, b1)
        mx = sb("mx", [P, NH, NT], F32, b1)
        psm = sb("psm", [P, NH, NT], F32, b1)
        rps = sb("rps", [P, NH, NT], F32, b1)
        xpad = sb("xpad", [P, 2, 16 + S], F32, b1)
        wina = sb("wina", [P, 2, 16 + S], F32, b1)
        winb = sb("winb", [P, 2, 16 + S], F32, b1)
        poolw = sb("poolw", [P, len(WINDOWS), 2, PGW], F32, b1)
        onehot = sb("onehot", [NB, SEG], F32, b1)
        relb = sb("relb", [NB, NH], F32, b1)
        vrow = sb("vrow", [4 * KT + 8 + 1, P], F32, b1)
    with ExitStack() as b1b:
        bseg = sb("bseg", [P, NH, SEG], F32, b1b)
    with ExitStack() as b2:
        hid = sb("hid", [P, FF // P, 2 * S], F32R, b2)
    with ExitStack() as b3:
        o32 = sb("o32", [P, NVH, S], F32, b3)
        kqr = sb("kqr", [P, 2, 2, S], F32, b3)
        vfm = sb("vfm", [P, 2, S], F32, b3)
        cpad = sb("cpad", [P, 2, 3 + S + 1], F32, b3)
        kq = sb("kq", [P, 2, 2, S], F32, b3)
        vtok = sb("vtok", [P, 2, 4, P], F32, b3)
        zs = sb("zs", [P, 4, S], F32, b3)
        dec = sb("dec", [P, 2, 4, P], F32, b3)
        at = sb("at", [P, 2, 4, P], F32, b3)
        intra = sb("intra", [P, 2, 4, P], F32, b3)
        xi = sb("xi", [P, 2, 2, 2 * P], F32, b3)
        xt = sb("xt", [P, 2, 4, P], F32, b3)
        wy = sb("wy", [P, 2, 4, P], F32, b3)
        qd = sb("qd", [P, 4, P], F32, b3)
        egc = sb("egc", [P, 4, P], F32, b3)
        gch = sb("gch", [P, 2, 4], F32, b3)
        ktok = sb("ktok", [P, 2, P], F32, b3)
        kdec = sb("kdec", [P, 4, P], F32, b3)
        vn = sb("vn", [P, 2, 4, P], F32, b3)
        st = sb("st", [P, 4, P], F32, b3)
        ba = sb("ba", [P, 2, 2 * NVH], F32, b3)
        sc4 = sb("sc4", [P, 4, 2, NVH], F32, b3)
        cur = sb("cur", [P, 4, 2, 4], F32, b3)
        bat = sb("bat", [P, 4, 2, NVH], F32, b3)
        avec = sb("avec", [P, 2, NVH], F32, b3)
        cwT = sb("cwT", [P, NTAP, 64], F32, b3)
        cwc = sb("cwc", [P, NTAP, 8], F32, b3)
    with ExitStack() as b4:
        olo = sb("olo", [P, NVH, S], F32R, b4)
        gain_b = sb("gain_b", [P, D], F32, b4)
        m_b = sb("m_b", [P, NT, D], F32, b4)
    cwrow = vfm[:, :, 0:P]
    conv_y, conv_th = (scr[:, i * 512:(i + 1) * 512].rearrange("p (a b) -> p a b", a=2) for i in (0, 1))
    sqkq = scr[:, 1024:2048].rearrange("p (a b) -> p a b", a=2)
    atp = egc[:, :, :].rearrange("p (c h) x -> p c h x", c=2)
    osq = wy[:, :, :, :].rearrange("p a b c -> p a (b c)")
    fg, fth, fu, fh = (scr[:, i * 512:(i + 1) * 512].rearrange("p (a b) -> p a b", a=2) for i in range(4))

    dn = ctx.enter_context(nc.psum_tensor("dense", [P, 4, 512], F32))
    mi = ctx.enter_context(nc.psum_tensor("misc", [P, 4, 512], F32))
    BM, BY, BX, BT = range(4)
    seg_dram = nc.dram_tensor("bias_segments", (P, NH * SEG), F32).ap()

    s_raw = [sem(f"raw_loaded{i}") for i in range(RING)]
    s_hi, s_lo, s_used = sem("hi_made"), sem("lo_made"), sem("chunk_used")
    s_ca, s_evac, s_sqm = sem("half_copied"), sem("block_evacuated"), sem("out_squared")
    s_x = [sem(f"x_loaded{b}") for b in range(NCB)]
    s_id, s_cst, s_vrow, s_relb, s_poolw = (sem(n) for n in ("ident_loaded", "cst_loaded", "vrow_loaded", "relb_loaded", "poolw_loaded"))
    s_vecp, s_vec, s_mh = sem("vec_turned"), sem("vec_ready"), sem("mhalf_set")
    s_sqx, s_tot, s_ms, s_rs = sem("x_squared"), sem("squares_summed"), sem("meansq_ready"), sem("rstd_ready")
    s_xs0, s_xs1, s_xtp, s_hnh, s_hnl = sem("x_scaled_act"), sem("x_scaled_dve"), sem("x_turned"), sem("hn_hi"), sem("hn_lo")
    s_gain, s_xup, s_out = sem("gain_loaded"), sem("x_updated"), sem("out_stored")
    s_bsp, s_bs, s_bsw, s_bmr, s_bm = sem("bias_row_psum"), sem("bias_row"), sem("bias_rows_stored"), sem("bias_read"), sem("bias_masked")
    s_kid, s_wip, s_wi, s_dot, s_rel, s_sc = sem("ki_copied"), sem("wi_turned"), sem("wi_ready"), sem("dots"), sem("relu_dots"), sem("score_added")
    s_causal, s_max8, s_repl, s_seln, s_selm = sem("score_masked"), sem("max8"), sem("replaced"), sem("selection"), sem("selection_masked")
    s_lg, s_lb, s_mx, s_ex, s_rp, s_pn = sem("logits"), sem("logits_biased"), sem("logits_max"), sem("probs"), sem("probs_sum_inv"), sem("probs_scaled")
    s_ptp, s_pt, s_ov, s_mh_, s_ml = sem("probs_turned"), sem("probsT"), sem("attn_out"), sem("attn_hi"), sem("attn_lo")
    s_pad, s_win, s_pd, s_mp, s_ph, s_pl = sem("pads_zeroed"), sem("window_sum"), sem("pooled"), sem("pool_mixed"), sem("pool_hi"), sem("pool_lo")
    s_th, s_t1, s_h, s_hh, s_hl = sem("ff_tanh"), sem("ff_gate"), sem("ff_hidden"), sem("ff_hi"), sem("ff_lo")
    s_nwh, s_cwr, s_cwp, s_cw, s_av, s_pz = (sem(n) for n in ("nwh_ready", "cw_loaded", "cw_turned", "cw_ready", "avec_loaded", "cpad_zeroed"))
    s_bap, s_ba, s_t, s_mn, s_ea, s_el, s_sp, s_g, s_gcp, s_gc, s_eg, s_sc4 = (sem(n) for n in (
        "ba_turned", "ba_ready", "a_biased", "a_folded", "ba_exps", "a_log1p", "softplus", "g_ready", "gc_psum", "gc_ready", "gc_exp", "scalars_ready"))
    s_cur, s_cwc, s_tap0, s_tap, s_thc, s_silu, s_zg = (sem(n) for n in ("cur_ready", "cwc_ready", "tap0", "taps", "conv_tanh", "silu_done", "z_gated"))
    s_gb, s_clamp, s_dec, s_eq, s_qd = (sem(n) for n in ("gc_rows", "decay_clamped", "decay_ready", "exp_gc_row", "q_decayed"))
    s_sqk, s_ss, s_rt, s_rc, s_kqn = (sem(n) for n in ("kq_squared", "norm_sums", "norm_roots", "norm_inverses", "kq_normed"))
    s_gq, s_atr, s_inr, s_ats, s_at, s_in = (sem(n) for n in ("kk_qk", "a_raw", "intra_raw", "a_strict", "a_ready", "intra_ready"))
    s_vtp, s_vt, s_ktp, s_kt, s_kd = (sem(n) for n in ("v_turned", "v_tok", "k_turned", "k_tok", "k_decayed"))
    s_x1t, s_x1p, s_x1, s_y, s_w, s_xx, s_xe = (sem(n) for n in ("x1T", "x1_turned", "x1", "ax_psum", "w_ready", "x_psum", "x_evacuated"))
    s_y0, s_v0, s_sp_, s_st, s_ks, s_r1, s_y1, s_v1 = (sem(n) for n in ("y0", "vnew0", "state_psum", "state", "k_state", "rhs1", "y1", "vnew1"))
    s_op, s_osq, s_on, s_og = (sem(n) for n in ("o_psum", "o_squared", "o_normed", "o_gated"))
    s_og_ss = sem("o_norm_sums")
    s_atp, s_xtu, s_xte, s_gch, s_nr, s_onr, s_wid = sem("a_paired"), sem("x_turned_level"), sem("xT_evacuated"), sem("gc_taken"), sem("norm_rows"), sem("o_norm_rows"), sem("w_identity_part")
    s_oh, s_ol, s_eps = sem("o_hi"), sem("o_lo"), sem("eps_set")

    KTI = KT // 4

    def cols(start, width):
        return bass.ds(start, width)

    kmap0 = list(range(NH // 2)) + [NH // 2 + gi for gi in (3, 2, 1, 0)]
    xp_order = (3, 2, 1, 0)

    blocks0 = [("kw", 0, C_KI, 2)] + [("qi", b, C_QI + b * TW, 4) for b in range(4)]
    for p in range(NH // 2):
        blocks0 += [("v", p, 2 * AW + p * TW, 4), ("k", p, AW + p * TW, 4), ("q", p, p * TW, 4)]
    blocks0 += [("xp", gi, C_XP + gi * PGW, 4) for gi in xp_order]
    chunks0 = [(n, j) for n, blk in enumerate(blocks0) for j in range(blk[3])]
    end0 = np.cumsum([blk[3] for blk in blocks0]).tolist()
    tidx0 = np.cumsum([0] + [blk[0] != "v" for blk in blocks0]).tolist()
    assert len(chunks0) == PH_OUT0["c"] and len(blocks0) == PH_OUT0["b"] and tidx0[-1] == PH_OUT0["t"]
    evac_at = {e: n for n, e in enumerate(end0)}
    SC0 = 23
    NR = TOPK // 8
    ATT = [SC0 + NR + 3 + 12 * p for p in range(NH // 2)]
    head_at = {ATT[h // 2] + 2 * (h % 2): h for h in range(NH)}
    GB_COL = {0: QKW, 1: 0, 2: 2 * QKW, 3: 2 * QKW + TW, 4: CONVW, 5: CONVW + TW}
    GB_STEP = {0: TW, 1: TW, 2: 2 * TW, 3: 2 * TW, 4: 2 * TW, 5: 2 * TW}
    w_in0, w_in1 = io["even_w_in"][0], io["odd_w_in"][0]

    block = ctx.enter_context(nc.Block())

    @block.sync
    def _(sp):
        def load(c, d, view, src):
            if c >= RING or looped(d):
                sp.wait_ge(s_lo, d + (c - RING + 1))
            sp.dma_start(view, src).then_inc(s_raw[c % RING], 16)

        def slot(c, k):
            return raw[:, c % RING, :].rearrange("p (k n) -> p k n", k=k)

        def load_t(c, d, w, j, col):
            load(c, d, slot(c, 4), w[4 * j * P:(4 * j + 4) * P, cols(col, TW)].rearrange("(k p) n -> p k n", p=P))

        def load_n(c, d, w, kp, col):
            load(c, d, slot(c, 2), w[2 * kp * P:(2 * kp + 2) * P, cols(col, NW)].rearrange("(k p) n -> p k n", p=P))

        def load_w128(c, w, j, col):
            load(c, 0, slot(c, 8), w[8 * j * P:(8 * j + 8) * P, cols(col, P)].rearrange("(k p) n -> p k n", p=P))

        def out_projection(ph, w, kmap):
            n = len(kmap)
            with sp.Fori(0, NCB // 2) as i:
                for u in range(2):
                    for j in range(n):
                        load_n(ph["c"] + u * n + j, i * (2 * n), w, kmap[j], i * (2 * NW) + u * NW)

        def feed_forward(layer, ph, pd):
            wg, wu, wd = io["ffn_w_gate"][layer], io["ffn_w_up"][layer], io["ffn_w_down"][layer]
            with sp.Fori(0, FI) as i:
                for j in range(8):
                    load_t(ph["c"] + j, i * 8, wg if j < 4 else wu, j % 4, i * TW)
            out_projection(pd, wd, list(range(FF // P // 2)))

        sp.dma_start(cst[:, 0:P], io["consts"][:, 0:P]).then_inc(s_id, 16)
        rows = 0
        for nm, n in (("mix_pre_g", 2 * KT), ("ffn_pre_g", 2 * KT), ("pool_scale", 8), ("gdn_norm_w", 1)):
            a = io[nm]
            sp.dma_start(vrow[rows:rows + n, :],
                         a if n == 1 else a.rearrange("a (k p) -> (a k) p", p=P)).then_inc(s_vrow, 16)
            rows += n
        for b in range(NCB):
            sp.dma_start(x[:, :, b * NW:(b + 1) * NW],
                         io["x"][0, :, b * NW:(b + 1) * NW].rearrange("(t p) d -> p t d", p=P)).then_inc(s_x[b], 16)
        for c, (n, j) in enumerate(chunks0):
            kind, _, col, _ = blocks0[n]
            if kind == "kw":
                load_w128(c, w_in0, j, col)
            else:
                load_t(c, 0, w_in0, j, col)
        out_projection(PH_OUT0, io["even_w_o"][0], kmap0)
        feed_forward(0, PH_FF0, PH_DN0)
        for j in range(2):
            load_w128(PH_BA["c"] + j, w_in1, j, ODD_IN - P)
        with sp.Fori(0, NG) as g:
            for b in range(GSLOT // 4):
                col = (g * (GB_STEP[b] // P) * P + GB_COL[b]) if GB_COL[b] == 0 else g * GB_STEP[b] + GB_COL[b]
                for j in range(4):
                    load_t(PH_IN1["c"] + 4 * b + j, g * GSLOT, w_in1, j, col)
        out_projection(PH_OUT1, io["odd_w_o"][0], list(range(NVH // 2)))
        feed_forward(1, PH_FF1, PH_DN1)
        for b in range(NCB):
            sp.wait_ge(s_xup, 8 * 3 + NT * (b + 1))
            sp.dma_start(io["out"][0, :, b * NW:(b + 1) * NW].rearrange("(t p) d -> p t d", p=P),
                         x[:, :, b * NW:(b + 1) * NW]).then_inc(s_out, 16)
        sp.wait_ge(s_out, 16 * NCB)

    @block.gpsimd
    def _(pool):
        pool.dma_start(cst[:, P:K_END], io["consts"][:, P:K_END]).then_inc(s_cst, 16)
        pool.dma_start(onehot[:, :], io["onehot"]).then_inc(s_relb, 16)
        pool.dma_start(relb[:, :], io["rel_bias"]).then_inc(s_relb, 16)
        pool.memset(mhalf[:, :], -0.5).then_inc(s_mh, 1)
        pool.wait_ge(s_mh, 1)

        def inverse_root(n):
            pool.wait_ge(s_ms, n + 1)
            pool.tensor_tensor(rstd[:, n % 2, :], meansq[:, n % 2, :], mhalf[:, :], ALU.pow).then_inc(s_rs, 1)

        def load_gain(n, dst, src, free_sem, free_val):
            pool.wait_ge(free_sem, free_val)
            pool.dma_start(dst[:, :], src.partition_broadcast(P)).then_inc(s_gain, 16)

        inverse_root(0)
        pool.wait_ge(s_evac, 1)
        pool.dma_start(kid[DIH:2 * DIH, :], kiw[0:DIH, :]).then_inc(s_kid, 16)
        pool.wait_ge(s_bs, NH)
        pool.dma_start(seg_dram, bseg[:, :, :].rearrange("p h s -> p (h s)")).then_inc(s_bsw, 16)
        pool.wait_ge(s_bsw, 16)
        for t in range(NT):
            w = P * (t + 1)
            src = bass.AP(seg_dram.tensor, S - 1 - P * t, [[NH * SEG - 1, P], [SEG, NH], [1, w]])
            pool.dma_start(bm[:, :, t * P:t * P + w], src).then_inc(s_bmr, 16)
        pool.dma_start(poolw[:, :, :, :], io["pool_w"][0].rearrange("g (c p) d -> p g c d", p=P)).then_inc(s_poolw, 16)
        pool.memset(xpad[:, :, 0:16], 0.0).then_inc(s_pad, 1)
        pool.memset(wina[:, :, 0:16], 0.0).then_inc(s_pad, 1)
        pool.memset(winb[:, :, 0:16], 0.0).then_inc(s_pad, 1)
        pool.wait_ge(s_sc, NIH * NT)
        for t in range(NT):
            w = P * (t + 1)
            v = score[:, t * P:t * P + w]
            pool.affine_select(out=v, in_=v, compare_op=ALU.is_ge, fill=NEG, base=t * P,
                               pattern=[[-1, w]], channel_multiplier=1).then_inc(s_causal, 1)
        pool.wait_ge(s_seln, 1)
        for t in range(NT):
            w = P * (t + 1)
            v = score[:, t * P:t * P + w]
            pool.affine_select(out=v, in_=v, compare_op=ALU.is_ge, fill=NEG, base=t * P,
                               pattern=[[-1, w]], channel_multiplier=1).then_inc(s_selm, 1)
        pool.wait_ge(s_selm, 2)
        pool.wait_ge(s_bmr, 32)
        for h in range(NH):
            pool.tensor_tensor(bm[:, h, :], bm[:, h, :], score[:, :], ALU.add).then_inc(s_bm, 1)
        load_gain(0, gain, io["mix_post_g"][0], s_used, PH_OUT0["c"])
        inverse_root(1)
        inverse_root(2)
        load_gain(1, gain, io["ffn_post_g"][0], s_used, PH_DN0["c"])
        inverse_root(3)
        inverse_root(4)
        pool.dma_start(cwrow[:, :, :], io["conv_w"][0].rearrange("k (t p) -> (k t) p", p=P)
                       .rearrange("(a r) p -> r a p", a=2)).then_inc(s_cwr, 16)
        pool.dma_start(avec[:, 0, :], io["dt_bias"][0].partition_broadcast(P)).then_inc(s_av, 16)
        pool.dma_start(avec[:, 1, :], io["a_log"][0].partition_broadcast(P)).then_inc(s_av, 16)
        pool.memset(cpad[:, :, 0:3], 0.0).then_inc(s_pz, 1)
        pool.memset(xi[:, :, :, :].rearrange("p a b c -> p (a b c)"), 0.0).then_inc(s_pz, 1)

        def masks(c, g):
            v, w = at[:, c, :, :], intra[:, c, :, :]
            pool.wait_ge(s_atr, g * 2 + (c + 1))
            pool.affine_select(out=v, in_=v, compare_op=ALU.is_ge, fill=0.0, base=-1,
                               pattern=[[0, 4], [1, P]], channel_multiplier=-1).then_inc(s_ats, 1)
            pool.wait_ge(s_ats, g * 2 + (c + 1))
            pool.affine_select(out=v, in_=v, compare_op=ALU.not_equal, fill=1.0, base=0,
                               pattern=[[0, 4], [1, P]], channel_multiplier=-1).then_inc(s_at, 1)
            pool.wait_ge(s_inr, g * 2 + (c + 1))
            pool.affine_select(out=w, in_=w, compare_op=ALU.is_ge, fill=0.0, base=0,
                               pattern=[[0, 4], [1, P]], channel_multiplier=-1).then_inc(s_in, 1)

        def identity_part(g):
            if g > 0:
                pool.wait_ge(s_og_ss, g)
            half = P // 2
            pool.tensor_copy(wy[:, :, :, half:P].rearrange("p a b c -> p (a b) c"),
                             ident[:, half:P].unsqueeze(1).broadcast_to([P, 8, half])).then_inc(s_wid, 1)

        for g in range(NG):
            for c in range(2):
                masks(c, g)
            identity_part(g)
        load_gain(2, gain_b, io["mix_post_g"][1], s_vtp, 2 * NG)
        inverse_root(5)
        inverse_root(6)
        load_gain(3, gain, io["ffn_post_g"][1], s_used, PH_DN1["c"])
        inverse_root(7)

    @block.tensor
    def _(pe):
        def begin_block(b, d):
            if b >= 2:
                pe.wait_ge(s_evac, d + (b - 1))

        def chunk_t(c, dc, b, j, kts=4, tiles=2, hn_ready=None):
            pe.wait_ge(s_lo, dc + (c + 1))
            if hn_ready is not None:
                pe.wait_ge(s_hnl, hn_ready)
            sl = c % RING
            w = tiles * P
            for f in range(tiles):
                bank = 2 * (b % 2) + f
                for kk in range(kts):
                    kt = kts * j + kk
                    at_ = slice(kk * w + f * P, kk * w + f * P + P)
                    if kt == 0:
                        nc.tensor.matmul(dn[:, bank, :], whi[:, sl, at_], hn[:, kt, :], start=True, stop=False)
                    mm = nc.tensor.matmul(dn[:, bank, 0:S], wlo[:, sl, at_], hn[:, kt, 0:S], start=False, stop=False)
                    if kt > 0:
                        mm = nc.tensor.matmul(dn[:, bank, :], whi[:, sl, at_], hn[:, kt, :], start=False,
                                              stop=kt == KT - 1)
            mm.then_inc(s_used, 1)

        def chunk_n(c, dc, b, first, last, lhs, width):
            pe.wait_ge(s_lo, dc + (c + 1))
            sl = c % RING
            for t in range(NT):
                bank = 2 * (b % 2) + t
                for kk, (hi, lo) in enumerate(lhs):
                    tok = slice(t * P, (t + 1) * P)
                    ws = slice(kk * width, (kk + 1) * width)
                    o = dn[:, bank, 0:width]
                    nc.tensor.matmul(o, hi(tok), whi[:, sl, ws], start=first and kk == 0, stop=False)
                    nc.tensor.matmul(o, hi(tok), wlo[:, sl, ws], start=False, stop=False)
                    mm = nc.tensor.matmul(o, lo(tok), whi[:, sl, ws], start=False,
                                          stop=last and kk == len(lhs) - 1)
            mm.then_inc(s_used, 1)

        def pair(t, kt, lo_at=S):
            return (lambda k: t[:, kt, k]), (lambda k: t[:, kt, lo_at + k.start:lo_at + k.stop])

        def turn(n, kg):
            pe.wait_ge(s_xs0, 4 * n + kg + 1)
            pe.wait_ge(s_xs1, 4 * n + kg + 1)
            if kg >= 2:
                pe.wait_ge(s_hnl, 16 * n + 4 * (kg - 1))
            for q in range(4):
                for t in range(NT):
                    at_ = ((kg % 2) * NT + t) * 512 + q * P
                    mm = nc.tensor.transpose(mi[:, 2 * (kg % 2) + q // 2, (q % 2) * S + t * P:(q % 2) * S + (t + 1) * P],
                                             scr[:, at_:at_ + P], ident)
            mm.then_inc(s_xtp, 1)

        def idle_products(k):
            for _ in range(k):
                nc.tensor.matmul(mi[:, BT, 0:P], ident, ident, start=True, stop=True)

        def keep_warm(n):
            if n == 0:
                pe.wait_ge(s_id, 16)
                for k in range(1, 9, 2):
                    pe.wait_ge(s_sqx, k)
                    idle_products(5)
            else:
                idle_products(14)
                pe.wait_ge(s_rs, 2 * n)
                idle_products(12)
                pe.wait_ge(s_xup, 8 * (n - 1) + 6)
                idle_products(10)

        def turn_before(n, j, chunks):
            if j == 0:
                keep_warm(n)
                turn(n, 0)
                turn(n, 1)
            elif chunks == 2:
                turn(n, 2)
                turn(n, 3)
            elif j < 3:
                turn(n, j + 1)

        def out_chunk(ph, i, u, j, kmap, lhs_of, ready):
            n = len(kmap)
            if j == 0:
                begin_block(ph["b"] + u, i * 2)
            ready(j)
            kt = 2 * kmap[j]
            chunk_n(ph["c"] + u * n + j, i * (2 * n), ph["b"] + u, j == 0, j == n - 1, [lhs_of(kt), lhs_of(kt + 1)], NW)

        def out_projection(ph, kmap, lhs_of, ready, done=0):
            def blocks(i, done):
                for u in range(2):
                    for j in range(0 if u else done, len(kmap)):
                        out_chunk(ph, i, u, j, kmap, lhs_of, ready)
            if done:
                blocks(0, done)
            with pe.Fori(1 if done else 0, NCB // 2) as i:
                blocks(i, 0)

        def feed_forward(n, ph, pd):
            def gate_and_up(i, first=False):
                for j in range(8):
                    if j % 4 == 0:
                        begin_block(ph["b"] + j // 4, i * 2)
                    if first and j < 4:
                        turn_before(n, j, 4)
                    chunk_t(ph["c"] + j, i * 8, ph["b"] + j // 4, j % 4, hn_ready=16 * n + 4 * (j % 4 + 1))

            gate_and_up(0, True)
            with pe.Fori(1, FI) as i:
                gate_and_up(i)
            layer = n // 2
            out_projection(pd, list(range(FF // P // 2)), lambda kt: pair(hid, kt),
                           lambda j: pe.wait_ge(s_hl, FI * layer + j + 1))

        pe.wait_ge(s_id, 16)
        pe.wait_ge(s_vrow, 64)
        R = 4 * KT + 9
        nc.tensor.transpose(mi[:, BX, 0:R], vrow[:, :], ident[0:R, 0:R]).then_inc(s_vecp, 1)
        pe.wait_ge(s_vec, 1)

        def bias_row(h):
            if h == 0:
                pe.wait_ge(s_relb, 32)
                pe.wait_ge(s_hnl, 16)
            if h >= 2:
                pe.wait_ge(s_bs, h - 1)
            nc.tensor.matmul(mi[:, h % 2, 0:SEG], relb[:, h:h + 1].broadcast_to([NB, P]), onehot[:, :],
                             start=True, stop=True).then_inc(s_bsp, 1)

        def turn_index_weights():
            pe.wait_ge(s_evac, 1)
            pe.wait_ge(s_hnl, 16)
            for t in range(NT):
                mm = nc.tensor.transpose(mi[:, BX, t * P:(t + 1) * P], kiw[:, t * P:(t + 1) * P], ident)
            mm.then_inc(s_wip, 1)

        def dots(ih):
            lo = DIH * (ih % 2)
            src = kiw if ih % 2 == 0 else kid
            pe.wait_ge(s_evac, 2 + ih // 4)
            if ih == 1:
                pe.wait_ge(s_kid, 16)
            if ih == 0:
                pe.wait_ge(s_bs, NH)
            if ih >= 2:
                pe.wait_ge(s_rel, ih - 1)
            for t in range(NT):
                w = P * (t + 1)
                mm = nc.tensor.matmul(mi[:, ih % 2, t * P:t * P + w],
                                      qiT[lo:lo + DIH, ih // 4 % 2, ih % 4 // 2, t * P:(t + 1) * P],
                                      src[lo:lo + DIH, 0:w], start=t == 0, stop=True, skip_group_check=True)
            mm.then_inc(s_dot, 1)

        def logits(h):
            pe.wait_ge(s_evac, end0.index(end0[5 + 3 * (h // 2) + 2]) + 1)
            if h >= 1:
                pe.wait_ge(s_lb, h)
            else:
                pe.wait_ge(s_rel, NIH)
            for t in range(NT):
                w = P * (t + 1)
                mm = nc.tensor.matmul(mi[:, 0, t * P:t * P + w], kqT[:, 1, h % 2, t * P:(t + 1) * P],
                                      kqT[:, 0, h % 2, 0:w], start=t == 0, stop=True, skip_group_check=True)
            mm.then_inc(s_lg, 1)

        def turn_probs(h):
            pe.wait_ge(s_pn, NT * (h + 1))
            if h >= 1:
                pe.wait_ge(s_pt, h)
            for n_, at_ in enumerate((0, P, 2 * P)):
                mm = nc.tensor.transpose(mi[:, 1, n_ * P:(n_ + 1) * P], prob[:, h % 2, at_:at_ + P], ident)
            mm.then_inc(s_ptp, 1)

        def attend(h):
            pe.wait_ge(s_pt, h + 1)
            if h >= 1:
                pe.wait_ge(s_ml, h)
            v = vtm[:, h // 2 % 2, :, (h % 2) * DH:(h % 2 + 1) * DH]
            nc.tensor.matmul(mi[:, 2, 0:P], v[:, 0, :], pT[:, 0:P], start=True, stop=True)
            nc.tensor.matmul(mi[:, 2, P:S], v[:, 0, :], pT[:, P:S], start=True, stop=False)
            nc.tensor.matmul(mi[:, 2, P:S], v[:, 1, :], pT[:, S:S + P], start=False, stop=True).then_inc(s_ov, 1)

        def mix_pool(k):
            gi = xp_order[k]
            pe.wait_ge(s_pd, 2 * (k + 1))
            if k == 0:
                pe.wait_ge(s_poolw, 16)
            else:
                pe.wait_ge(s_pl, k)
            for dt in range(2):
                for ct in range(2):
                    mm = nc.tensor.matmul(mi[:, 3, dt * S:(dt + 1) * S], poolw[:, gi, ct, dt * P:(dt + 1) * P],
                                          wina[:, ct, 16:16 + S], start=ct == 0, stop=ct == 1)
            mm.then_inc(s_mp, 1)

        def mix_ready(j):
            if j < NH // 2:
                pe.wait_ge(s_ml, 2 * (j + 1))
            else:
                pe.wait_ge(s_pl, j - NH // 2 + 1)

        out0 = (kmap0, lambda kt: pair(mix, kt), mix_ready)
        for s, (n, j) in enumerate(chunks0 + [(None, None)] * OVER0):
            if n is None:
                out_chunk(PH_OUT0, 0, 0, s - len(chunks0), *out0)
            else:
                kind = blocks0[n][0]
                if j == 0:
                    begin_block(n, 0)
                if kind == "kw":
                    turn_before(0, j, 2)
                    chunk_t(s, 0, n, j, kts=8, tiles=1, hn_ready=8 * (j + 1))
                elif kind == "v":
                    chunk_n(s, 0, n, j == 0, j == 3, [pair(hn, 4 * j + kk) for kk in range(4)], TW)
                else:
                    chunk_t(s, 0, n, j)
            if 2 <= s < 2 + NH // 2:
                bias_row(2 * (s - 2))
                bias_row(2 * (s - 2) + 1)
            if s == 3:
                turn_index_weights()
            if 7 <= s < 7 + NIH:
                dots(s - 7)
            if s in head_at:
                logits(head_at[s])
            if s - 2 in head_at:
                turn_probs(head_at[s - 2])
            if s - 3 in head_at:
                attend(head_at[s - 3])
            for k in range(4):
                if s == end0[17 + k] + 2:
                    mix_pool(k)

        out_projection(PH_OUT0, *out0, done=OVER0)
        feed_forward(1, PH_FF0, PH_DN0)
        begin_block(PH_BA["b"], 0)
        for j in range(2):
            turn_before(2, j, 2)
            chunk_t(PH_BA["c"] + j, 0, PH_BA["b"], j, kts=8, tiles=1, hn_ready=32 + 8 * (j + 1))
        pe.wait_ge(s_cwr, 16)
        for a in range(2):
            mm = nc.tensor.transpose(mi[:, BX, a * P:(a + 1) * P], cwrow[:, a, :], ident)
        mm.then_inc(s_cwp, 1)
        pe.wait_ge(s_evac, PH_IN1["b"])
        for t in range(NT):
            mm = nc.tensor.transpose(mi[:, BY, t * P:(t + 1) * P], conv_y[:, 0, t * P:(t + 1) * P], ident)
        mm.then_inc(s_bap, 1)

        def log_decay_sums():
            pe.wait_ge(s_g, 1)
            pe.wait_ge(s_cst, 16)
            for c in range(2):
                mm = nc.tensor.matmul(mi[:, BX, 256 + c * NVH:256 + (c + 1) * NVH], triu, sc4[:, 0, c, :],
                                      start=True, stop=True)
            mm.then_inc(s_gcp, 1)

        def decay_rows(g, c):
            pe.wait_ge(s_gch, g * 1 + 1)
            if c == 0 and looped(g):
                pe.wait_ge(s_xte, g * 12)
            if c == 1:
                pe.wait_ge(s_clamp, g * 2 + 1)
            for u in range(4):
                mm = nc.tensor.transpose(mi[:, BM, u * P:(u + 1) * P], gch[:, c, u:u + 1].broadcast_to([P, P]), ident)
            mm.then_inc(s_gb, 1)

        def norm_sums(g):
            pe.wait_ge(s_sqk, g * 1 + 1)
            if looped(g):
                pe.wait_ge(s_v1, g * 1)
            for n in range(8):
                mm = nc.tensor.matmul(mi[:, BY, n:n + 1], sqkq[:, n // 4, (n % 4) * P:(n % 4 + 1) * P],
                                      ones[:, 0:1], start=True, stop=True, skip_group_check=True)
            mm.then_inc(s_ss, 1)

        def norm_rows(g):
            pe.wait_ge(s_rc, g * 1 + 1)
            pe.wait_ge(s_clamp, g * 2 + 2)
            pe.wait_ge(s_eq, g * 1 + 1)
            for n in range(8):
                mm = nc.tensor.transpose(mi[:, (BM, BY)[n // 4], (n % 4) * P:(n % 4 + 1) * P],
                                         nrm[:, n:n + 1].broadcast_to([P, P]), ident)
                if n % 4 == 3:
                    mm.then_inc(s_nr, 1)

        def o_norm_sums(g):
            pe.wait_ge(s_osq, g * 2 + 2)
            for n in range(8):
                mm = nc.tensor.matmul(mi[:, BY, 8 + n:9 + n], osq[:, n // 4, (n % 4) * P:(n % 4 + 1) * P],
                                      ones[:, 0:1], start=True, stop=True, skip_group_check=True)
            mm.then_inc(s_og_ss, 1)

        def o_norm_rows(g, k):
            pe.wait_ge(s_on, g * 2 + (k + 1))
            for n in range(4):
                mm = nc.tensor.transpose(mi[:, (BX, BT)[k], n * P:(n + 1) * P],
                                         nrm[:, 8 + 4 * k + n:9 + 4 * k + n].broadcast_to([P, P]), ident)
            mm.then_inc(s_onr, 1)

        def products(g, c):
            pe.wait_ge(s_kqn, g * 2 + 2)
            if c == 1:
                pe.wait_ge(s_atr, g * 2 + 1)
                pe.wait_ge(s_inr, g * 2 + 1)
            tok = slice(c * P, (c + 1) * P)
            for kp in range(2):
                mm = nc.tensor.matmul(mi[:, BM, kp * 256:(kp + 1) * 256].rearrange("p (a b) -> p a b", a=2),
                                      kq[:, 0, kp, tok], kq[:, :, kp, tok], start=True, stop=True)
            mm.then_inc(s_gq, 1)

        def turn_v(g, half):
            pe.wait_ge(s_silu, g * 4 + (3 + half))
            if half == 0:
                pe.wait_ge(s_atr, g * 2 + 2)
                pe.wait_ge(s_inr, g * 2 + 2)
            else:
                pe.wait_ge(s_x1, g * 2 + 2)
            for c in range(2):
                for u in range(2):
                    mm = nc.tensor.transpose(mi[:, BM, (2 * c + u) * P:(2 * c + u + 1) * P],
                                             vfm[:, u, c * P:(c + 1) * P], ident)
            mm.then_inc(s_vtp, 1)

        def turn_x1(g, b):
            pe.wait_ge(s_x1t, g * 2 + (b + 1))
            if b == 0:
                pe.wait_ge(s_vt, g * 2 + 1)
            else:
                pe.wait_ge(s_x1, g * 2 + 1)
            for u in range(4):
                mm = nc.tensor.transpose(mi[:, BM, u * P:(u + 1) * P], xt[:, b, u, :], ident)
            mm.then_inc(s_x1p, 1)

        def turn_k(g):
            pe.wait_ge(s_vt, g * 2 + 2)
            for kp in range(2):
                mm = nc.tensor.transpose(mi[:, BM, kp * P:(kp + 1) * P], kq[:, 0, kp, 0:P], ident)
            mm.then_inc(s_ktp, 1)

        def times_a(g, b, lev):
            n = 2 * (lev - 1) + b
            if lev == 1:
                pe.wait_ge(s_x1, g * 2 + (b + 1))
                pe.wait_ge(s_atp, g * 2 + (b + 1))
            else:
                pe.wait_ge(s_xe, g * 12 + (2 * (lev - 2) + b + 1))
            if n >= 1:
                pe.wait_ge(s_w, g * 12 + n)
            half = P // 2
            if lev < NLEV:
                for p in range(2):
                    o = mi[:, BY, p * P:(p + 1) * P].rearrange("p (g s) -> p g s", s=2 ** lev)
                    xe = xi[:, b, p, :].rearrange("p (g t s) -> p g t s", t=2, s=2 ** lev)[:, :, 0, :]
                    mm = nc.tensor.matmul(o, atp[:, b, p, :], xe, start=True, stop=True)
            else:
                for u in range(4):
                    mm = nc.tensor.matmul(mi[:, BY, u * half:(u + 1) * half], at[:, b, u, :],
                                          xi[:, b, u // 2, (u % 2) * half:(u % 2 + 1) * half], start=True, stop=True)
            mm.then_inc(s_y, 1)

        def next_x(g, b, lev):
            n = 2 * (lev - 1) + b
            pe.wait_ge(s_w, g * 12 + (n + 1))
            if n >= 1:
                pe.wait_ge(s_xe, g * 12 + n)
            pe.wait_ge(s_xte, g * 12 + (n + 1))
            if lev == NLEV:
                pe.wait_ge(s_wid, g * 1 + 1)
            half = P // 2
            if lev < NLEV:
                for p in range(2):
                    mm = nc.tensor.matmul(mi[:, BX, p * P:(p + 1) * P].rearrange("p (h x) -> p h x", h=2),
                                          xt[:, b, p, :], wy[:, b, 2 * p:2 * p + 2, 0:half], start=True, stop=True)
            else:
                for u in range(4):
                    mm = nc.tensor.matmul(mi[:, BX, u * half:(u + 1) * half], wy[:, b, u, :], xt[:, b, u, half:P],
                                          start=True, stop=True)
            mm.then_inc(s_xx, 1)

        def turn_x(g, b, lev):
            n = 2 * lev + b
            if lev == 0:
                pe.wait_ge(s_x1, g * 2 + (b + 1))
                if b == 0 and looped(g):
                    pe.wait_ge(s_og, g * 2)
            else:
                pe.wait_ge(s_xe, g * 12 + (2 * (lev - 1) + b + 1))
            if n >= 1:
                pe.wait_ge(s_xte, g * 12 + n)
            half = P // 2
            for p in range(2):
                for q in range(2):
                    mm = nc.tensor.transpose(mi[:, BT, (2 * p + q) * P:(2 * p + q + 1) * P],
                                             xi[:, b, p, q * P:(q + 1) * P], ident)
                if lev == NLEV - 1:
                    if b == 0 and p == 0:
                        pe.wait_ge(s_kt, g * 1 + 1)
                    mm = nc.tensor.transpose(mi[:, BM, p * P:(p + 1) * P], xi[:, b, p, half:half + P], ident)
            mm.then_inc(s_xtu, 1)

        def solve(g, c):
            pe.wait_ge(s_xe, g * 12 + (11 + c))
            if c == 1:
                pe.wait_ge(s_r1, g * 1 + 1)
            for u in range(4):
                mm = nc.tensor.matmul(mi[:, BY, u * P:(u + 1) * P], xt[:, c, u, :], vtok[:, c, u, :],
                                      start=True, stop=True)
            mm.then_inc((s_y0, s_y1)[c], 1)

        def state(g):
            pe.wait_ge(s_v0, g * 1 + 1)
            for u in range(4):
                mm = nc.tensor.matmul(mi[:, BY, u * P:(u + 1) * P], kdec[:, u, :], vn[:, 0, u, :],
                                      start=True, stop=True)
            mm.then_inc(s_sp_, 1)

        def keys_times_state(g):
            pe.wait_ge(s_st, g * 1 + 1)
            for kp in range(2):
                mm = nc.tensor.matmul(mi[:, BY, kp * 256:(kp + 1) * 256], kq[:, 0, kp, P:S],
                                      st[:, 2 * kp:2 * kp + 2, :].rearrange("p a b -> p (a b)"),
                                      start=True, stop=True)
            mm.then_inc(s_ks, 1)

        def outputs(g, half):
            pe.wait_ge(s_v1, g * 1 + 1)
            pe.wait_ge(s_in, g * 2 + 2)
            for e in range(2):
                u = 2 * half + e
                o = mi[:, (BX, BT)[half], e * S:(e + 1) * S]
                nc.tensor.matmul(o[:, 0:P], vn[:, 0, u, :], intra[:, 0, u, :], start=True, stop=True)
                nc.tensor.matmul(o[:, P:S], vn[:, 1, u, :], intra[:, 1, u, :], start=True, stop=False)
                mm = nc.tensor.matmul(o[:, P:S], st[:, u, :], qd[:, u, :], start=False, stop=True)
            mm.then_inc(s_op, 1)

        def slot(n, g, cur_on, prev_on):
            if prev_on:
                h = g - 1
                m = n + GSLOT
                for b in range(2):
                    lev, odd = divmod(m - 20 - b, 2)
                    if odd == 1 and 1 <= lev + 1 <= NLEV:
                        next_x(h, b, lev + 1)
                for b in range(2):
                    lev, odd = divmod(m - 20 - b, 2)
                    if odd == 0 and 1 <= lev + 1 <= NLEV:
                        times_a(h, b, lev + 1)
                        turn_x(h, b, lev)
                if m == 32:
                    solve(h, 0)
                if m == 33:
                    state(h)
                if m == 34:
                    keys_times_state(h)
                if m == 35:
                    solve(h, 1)
                if m == 36:
                    outputs(h, 0)
                    outputs(h, 1)
            if cur_on:
                if n in (9, 10):
                    decay_rows(g, n - 9)
                if n == 12:
                    norm_sums(g)
            if prev_on and n == 13:
                o_norm_sums(g - 1)
            if cur_on and n == 15:
                norm_rows(g)
            if prev_on and n == 16:
                if not cur_on:
                    pe.wait_ge(s_rc, NG + 1)
                o_norm_rows(g - 1, 0)
                o_norm_rows(g - 1, 1)
            if cur_on:
                if n in (16, 17):
                    products(g, n - 16)
                if n == 18:
                    turn_v(g, 0)
                if n == 19:
                    turn_x1(g, 0)
                if n == 20:
                    turn_x1(g, 1)
                for b in range(2):
                    lev, odd = divmod(n - 20 - b, 2)
                    if odd == 1 and lev >= 0:
                        next_x(g, b, lev + 1)
                for b in range(2):
                    lev, odd = divmod(n - 20 - b, 2)
                    if odd == 0 and lev >= 0:
                        times_a(g, b, lev + 1)
                        turn_x(g, b, lev)
                if n == 21:
                    turn_v(g, 1)
                if n == 22:
                    turn_k(g)

        def group(g, d, prev_on):
            for n in range(GSLOT):
                b = n // 4
                if n % 4 == 0:
                    begin_block(PH_IN1["b"] + b, d * 6)
                chunk_t(PH_IN1["c"] + n, d * GSLOT, PH_IN1["b"] + b, n % 4)
                if n == 3 and not prev_on:
                    log_decay_sums()
                slot(n, g, True, prev_on)

        group(0, 0, False)
        with pe.Fori(1, NG) as g:
            group(g, g, True)
        out1 = (list(range(NVH // 2)), lambda kt: ((lambda k: ohi[:, kt, k]), (lambda k: olo[:, kt, k])),
                lambda j: pe.wait_ge(s_ol, j + 1))
        for n in range(17 + 1):
            if n < NFREE:
                out_chunk(PH_OUT1, 0, 0, n, *out1)
            slot(n, NG, False, True)
        out_projection(PH_OUT1, *out1, done=NFREE)
        feed_forward(3, PH_FF1, PH_DN1)

    @block.scalar
    def _(act):
        def split_hi(c, d):
            if c >= CHUNKS and not looped(d):
                return
            act.wait_ge(s_raw[c % RING], d * (16 // RING) + 16 * (c // RING + 1))
            if c >= RING or looped(d):
                act.wait_ge(s_used, d + (c - RING + 1))
            nc.scalar.activation(whi[:, c % RING, :], raw[:, c % RING, :], ACT.Copy).then_inc(s_hi, 1)

        def copy_half(c_last, dc, b, db, tiles=2):
            act.wait_ge(s_used, dc + (c_last + 1))
            if b >= 1:
                act.wait_ge(s_evac, db + b)
            b2 = 2 * (b % 2)
            nc.scalar.activation(halfa[:, 0:tiles, :], dn[:, b2:b2 + tiles, 0:S], ACT.Copy).then_inc(s_ca, 1)

        def square_x(n):
            for b in range(NCB):
                for t in range(NT):
                    if n == 0:
                        act.wait_ge(s_x[b], 16)
                    else:
                        act.wait_ge(s_xup, 8 * (n - 1) + NT * b + t + 1)
                    seq = 8 * n + NT * b + t
                    if n >= 1:
                        act.wait_ge(s_sqm, 8 * n)
                    if seq >= 1:
                        act.wait_ge(s_sqx, seq)
                    nc.scalar.activation(junk[:, :], x[:, t, b * NW:(b + 1) * NW], ACT.Square,
                                         accum_out=ssx[:, t, b:b + 1]).then_inc(s_sqx, 1)

        def norm(n):
            square_x(n)
            if n == 0:
                act.wait_ge(s_vecp, 1)
                nc.scalar.activation(vecT[:, :], mi[:, BX, 0:4 * KT + 9], ACT.Copy).then_inc(s_vec, 1)
            g0 = n // 2 * KT + (2 * KT if n % 2 else 0)
            act.wait_ge(s_rs, 2 * n + 1)

            def scale(kg):
                if kg >= 2:
                    act.wait_ge(s_xtp, 4 * n + kg - 1)
                at_ = (kg % 2) * NT * 512
                nc.scalar.activation(scr[:, at_:at_ + 512], x[:, 0, kg * 512:(kg + 1) * 512], ACT.Copy,
                                     scale=rstd[:, 0, 0:1]).then_inc(s_xs0, 1)

            scale(0)
            scale(1)
            if n == 0:
                for c in range(LEAD):
                    split_hi(c, 0)
                act.wait_ge(s_vec, 1)
            for kg in range(4):
                act.wait_ge(s_xtp, 4 * n + kg + 1)
                for q in range(4):
                    kt = 4 * kg + q
                    nc.scalar.activation(hn[:, kt, 0:S], mi[:, 2 * (kg % 2) + q // 2, (q % 2) * S:(q % 2 + 1) * S],
                                         ACT.Copy, scale=vecT[:, g0 + kt:g0 + kt + 1]).then_inc(s_hnh, 1)
                if kg + 2 < 4:
                    scale(kg + 2)

        def out_projection(ph, n, sq_base, final=False, done=0):
            def body(i, d, done=0):
                for u in range(2):
                    for j in range(0 if u else done, n):
                        c = ph["c"] + u * n + j
                        if not (final and c + LEAD + (d if isinstance(d, int) else 0) >= CHUNKS):
                            split_hi(c + LEAD, d)
                        if j == n - 1:
                            act.wait_ge(s_used, d + (c + 1))
                            act.wait_ge(s_sqx, sq_base + 8)
                            for t in range(NT):
                                act.wait_ge(s_sqm, i * 4 + (sq_base + 2 * u + t))
                                nc.scalar.activation(junk[:, :], dn[:, 2 * ((ph["b"] + u) % 2) + t, :], ACT.Square,
                                                     accum_out=ssm[:, t, i * 2 + u:i * 2 + u + 1] if isinstance(i, int)
                                                     else ssm[:, t, bass.ds(i * 2 + u, 1)]).then_inc(s_sqm, 1)
            if final:
                for i in range(NCB // 2):
                    body(i, i * 2 * n)
            else:
                if done:
                    body(0, 0, done)
                with act.Fori(1 if done else 0, NCB // 2) as i:
                    body(i, i * (2 * n))

        def feed_forward(layer, ph, pd, final):
            nc.scalar.activation(warm[:, :], epsc[:, 0:1], ACT.Tanh)
            with act.Fori(0, FI) as i:
                for j in range(8):
                    split_hi(ph["c"] + j + LEAD, i * 8)
                    if j == 3:
                        copy_half(ph["c"] + 3, i * 8, ph["b"], i * 2)
                    if j == 4:
                        act.wait_ge(s_evac, i * 2 + (ph["b"] + 1))
                        nc.scalar.activation(fth, fg, ACT.Tanh, scale=0.5).then_inc(s_th, 1)
                    if j == 7:
                        copy_half(ph["c"] + 7, i * 8, ph["b"] + 1, i * 2)
                        act.wait_ge(s_h, i + (FI * layer + 1))
                        nc.scalar.activation(hid[:, bass.ds(i * 2, 2), 0:S], fh, ACT.Copy).then_inc(s_hh, 1)
            out_projection(pd, FF // P // 2, 8 * (2 * layer + 1), final)

        norm(0)

        def exps(h):
            act.wait_ge(s_mx, NT * (h + 1))
            for t in range(NT):
                w = P * (t + 1)
                v = prob[:, h % 2, t * P:t * P + w]
                nc.scalar.activation(v, v, ACT.Exp, bias=mx[:, h, t:t + 1],
                                     accum_out=psm[:, h, t:t + 1]).then_inc(s_ex, 1)

        for s in range(len(chunks0) + OVER0):
            split_hi(s + LEAD, 0)
            if s in evac_at and blocks0[evac_at[s]][0] != "v":
                n = evac_at[s]
                copy_half(s - 1, 0, n, 0, tiles=1 if n == 0 else 2)
            if 2 <= s < 2 + NH // 2:
                for h in (2 * (s - 2), 2 * (s - 2) + 1):
                    act.wait_ge(s_bsp, h + 1)
                    nc.scalar.activation(bseg[:, h, :], mi[:, h % 2, 0:SEG], ACT.Copy).then_inc(s_bs, 1)
            if 7 <= s < 7 + NIH:
                ih = s - 7
                act.wait_ge(s_dot, ih + 1)
                if ih >= 2:
                    act.wait_ge(s_sc, NT * (ih - 1))
                nc.scalar.activation(rel[:, ih % 2, :], mi[:, ih % 2, 0:3 * P], ACT.Relu,
                                     scale=DIH ** -0.5).then_inc(s_rel, 1)
            if s - 1 in head_at:
                exps(head_at[s - 1])
            if s - 2 in head_at:
                h = head_at[s - 2]
                act.wait_ge(s_ptp, h + 1)
                if h >= 1:
                    act.wait_ge(s_ov, h)
                nc.scalar.activation(pT[:, :], mi[:, 1, 0:3 * P], ACT.Copy).then_inc(s_pt, 1)
            if s - 3 in head_at:
                h = head_at[s - 3]
                act.wait_ge(s_ov, h + 1)
                nc.scalar.activation(mix[:, h, 0:S], mi[:, 2, 0:S], ACT.Copy).then_inc(s_mh_, 1)
            for k in range(4):
                if s == end0[17 + k] + 2:
                    gi = xp_order[k]
                    act.wait_ge(s_mp, k + 1)
                    for dt in range(2):
                        col = 4 * KT + 2 * gi + dt
                        nc.scalar.activation(mix[:, NH + 2 * gi + dt, 0:S], mi[:, 3, dt * S:(dt + 1) * S], ACT.Copy,
                                             scale=vecT[:, col:col + 1]).then_inc(s_ph, 1)
        out_projection(PH_OUT0, KT // 2, 0, done=OVER0)
        norm(1)
        feed_forward(0, PH_FF0, PH_DN0, False)
        norm(2)
        split_hi(PH_BA["c"] + LEAD, 0)
        split_hi(PH_BA["c"] + 1 + LEAD, 0)
        act.wait_ge(s_cwp, 1)
        nc.scalar.activation(cwT[:, :, :].rearrange("p a b -> p (a b)"), mi[:, BX, 0:256], ACT.Copy,
                             scale=0.5).then_inc(s_cw, 1)
        copy_half(PH_BA["c"] + 1, 0, PH_BA["b"], 0, tiles=1)

        def gates(step):
            if step == 0:
                act.wait_ge(s_mn, 1)
                nc.scalar.activation(bat[:, 0, :, :], ba[:, :, 0:NVH], ACT.Exp, scale=-1.0).then_inc(s_ea, 1)
                nc.scalar.activation(bat[:, 2, :, :], bat[:, 2, :, :], ACT.Exp).then_inc(s_ea, 1)
                nc.scalar.activation(avec[:, 1, :], avec[:, 1, :], ACT.Exp).then_inc(s_ea, 1)
            if step == 1:
                act.wait_ge(s_ea, 2)
                nc.scalar.activation(bat[:, 3, :, :], bat[:, 2, :, :], ACT.Ln, bias=1.0).then_inc(s_el, 1)
            if step == 2:
                act.wait_ge(s_gc, 1)
                nc.scalar.activation(sc4[:, 2, :, :], sc4[:, 1, :, :], ACT.Exp).then_inc(s_eg, 1)

        def evac(g, b):
            copy_half(PH_IN1["c"] + 4 * b + 3, g * GSLOT, PH_IN1["b"] + b, g * 6)

        def tap0(g, b):
            act.wait_ge(s_evac, g * 6 + (PH_IN1["b"] + b + 1))
            act.wait_ge(s_cwc, g * 1 + 1)
            for f in range(2):
                k = 2 * b + f
                i = nc.scalar.activation(conv_y[:, f, :], cpad[:, f, 3:3 + S], ACT.Copy,
                                         scale=cwc[:, 3, k:k + 1])
            i.then_inc(s_tap0, 1)

        def tanh(g, k):
            if k < 4:
                act.wait_ge(s_tap, g * 24 + 6 * (k + 1))
                nc.scalar.activation(conv_th, conv_y, ACT.Tanh).then_inc(s_thc, 1)
            else:
                act.wait_ge(s_evac, g * 6 + (PH_IN1["b"] + k + 1))
                z = zs[:, 2 * (k - 4):2 * (k - 4) + 2, :]
                nc.scalar.activation(conv_th, z, ACT.Tanh, scale=0.5).then_inc(s_thc, 1)

        def decays(g, c):
            act.wait_ge(s_clamp, g * 2 + (c + 1))
            if c == 1:
                nc.scalar.activation(egc[:, :, :].rearrange("p a b -> p (a b)"), mi[:, BM, :], ACT.Exp).then_inc(s_eq, 1)
            nc.scalar.activation(dec[:, c, :, :], dec[:, c, :, :], ACT.Exp).then_inc(s_dec, 1)

        def squares(g):
            act.wait_ge(s_silu, g * 4 + 2)
            nc.scalar.activation(sqkq, kqr[:, :, :, :].rearrange("p a b c -> p a (b c)"), ACT.Square).then_inc(s_sqk, 1)

        def o_squares(g, k):
            act.wait_ge(s_op, g * 2 + (k + 1))
            nc.scalar.activation(osq[:, k, :], mi[:, (BX, BT)[k], :], ACT.Square).then_inc(s_osq, 1)

        def roots(g, kq_on, o_on):
            if kq_on:
                act.wait_ge(s_ss, g * 1 + 1)
            if o_on:
                act.wait_ge(s_og_ss, g * 1)
            if kq_on:
                for k in range(2):
                    i = nc.scalar.activation(nrm[:, 4 * k:4 * k + 4], mi[:, BY, 4 * k:4 * k + 4], ACT.Sqrt,
                                             scale=(1.0, float(DH))[k], bias=epsc[:, k:k + 1])
            if o_on:
                i = nc.scalar.activation(nrm[:, 8:16], mi[:, BY, 8:16], ACT.Sqrt, scale=1.0 / DH, bias=epsc[:, 0:1])
            i.then_inc(s_rt, 1)

        def copy_v(g, half):
            act.wait_ge(s_vtp, g * 2 + (half + 1))
            nc.scalar.activation(vtok[:, :, 2 * half:2 * half + 2, :],
                                 mi[:, BM, :].rearrange("p (a b c) -> p a b c", a=2, b=2), ACT.Copy).then_inc(s_vt, 1)

        def copy_x1(g, b):
            act.wait_ge(s_x1p, g * 2 + (b + 1))
            if b == 0 and not looped(g):
                act.wait_ge(s_pz, 2)
            half = P // 2
            src = mi[:, BM, :].rearrange("p (h a x) -> p h a x", h=2, a=2)
            nc.scalar.activation(xi[0:half, b, :, 0:P].rearrange("p h (a x) -> p h a x", a=2), src[0:half, :, :, 0:half],
                                 ACT.Copy)
            for a in range(2):
                i = nc.scalar.activation(xi[half:P, b, :, P + (1 - a) * half:P + (2 - a) * half],
                                         src[half:P, :, a, half:P], ACT.Copy)
            i.then_inc(s_x1, 1)

        def pair_a(g, c):
            half = P // 2
            if c == 0:
                act.wait_ge(s_qd, g * 1 + 1)
            act.wait_ge(s_at, g * 2 + (c + 1))
            src = at[:, c, :, :].rearrange("p (h a) x -> p h a x", h=2)
            nc.scalar.activation(atp[0:half, c, :, :].rearrange("p h (a x) -> p h a x", a=2), src[0:half, :, :, 0:half],
                                 ACT.Copy)
            for a in range(2):
                i = nc.scalar.activation(atp[half:P, c, :, (1 - a) * half:(2 - a) * half], src[half:P, :, a, half:P],
                                         ACT.Copy)
            i.then_inc(s_atp, 1)

        def copy_k(g):
            act.wait_ge(s_ktp, g * 1 + 1)
            nc.scalar.activation(ktok[:, :, :].rearrange("p a b -> p (a b)"), mi[:, BM, 0:256], ACT.Copy).then_inc(s_kt, 1)

        def copy_x(g, b, lev):
            act.wait_ge(s_xx, g * 12 + (2 * (lev - 1) + b + 1))
            src = mi[:, BX, 0:2 * P]
            if lev < NLEV:
                half = P // 2
                v = src.rearrange("p (h a x) -> p h a x", h=2, a=2)
                for a in range(2):
                    r = slice(a * half, (a + 1) * half)
                    dst = xi[r, b, :, a * P:(a + 1) * P].rearrange("p h (g t s) -> p h g t s", t=2, s=2 ** lev)[:, :, :, 0, :]
                    i = nc.scalar.activation(dst, v[r, :, a, :].rearrange("p h (g s) -> p h g s", s=2 ** lev), ACT.Copy)
                i.then_inc(s_xe, 1)
            else:
                nc.scalar.activation(xt[:, b, :, P // 2:P], src.rearrange("p (u s) -> p u s", u=4),
                                     ACT.Copy).then_inc(s_xe, 1)

        def copy_xt(g, b, lev):
            act.wait_ge(s_xtu, g * 12 + (2 * lev + b + 1))
            src = mi[:, BT, :].rearrange("p (h y) -> p h y", h=2)
            if lev < NLEV - 1:
                both = mi[:, BT, :].rearrange("p (h z x) -> p h z x", h=2, x=P // 2)[:, :, 0:4:3, :]
                nc.scalar.activation(xt[:, b, 0:2, :].rearrange("p h (z x) -> p h z x", z=2), both,
                                     ACT.Copy).then_inc(s_xte, 1)
                return
            heads = xt[:, b, :, :].rearrange("p (h a) s -> p h a s", h=2)
            half = P // 2
            lo, hi = slice(0, half), slice(half, P)
            nc.scalar.activation(heads[lo, :, 0, lo], src[lo, :, lo], ACT.Copy)
            nc.scalar.activation(heads[hi, :, 0, hi], src[hi, :, P + half:2 * P], ACT.Copy)
            nc.scalar.activation(heads[hi, :, 0, lo], xi[hi, b, :, lo], ACT.Copy)
            nc.scalar.activation(heads[lo, :, 0, hi], xi[lo, b, :, P:P + half], ACT.Copy)
            nc.scalar.activation(heads[:, :, 1, :], mi[:, BM, 0:2 * P].rearrange("p (h x) -> p h x", h=2),
                                 ACT.Copy).then_inc(s_xte, 1)

        def slot(n, g, cur_on, prev_on):
            if prev_on:
                h, m = g - 1, n + GSLOT
                for b in range(2):
                    lev, odd = divmod(m - 20 - b, 2)
                    if odd == 1 and 1 <= lev + 1 <= NLEV:
                        copy_x(h, b, lev + 1)
                    if odd == 0 and 1 <= lev < NLEV:
                        copy_xt(h, b, lev)
                if m == 33:
                    act.wait_ge(s_sp_, h * 1 + 1)
                    nc.scalar.activation(st[:, :, :].rearrange("p a b -> p (a b)"), mi[:, BY, :], ACT.Copy).then_inc(s_st, 1)
                if m == 24:
                    evac(h, 5)
                if m == 25:
                    tanh(h, 5)
            if cur_on:
                if n == 18:
                    copy_v(g, 0)
                if n == 19:
                    copy_x1(g, 0)
                if n == 20:
                    copy_x1(g, 1)
                if n in (19, 20):
                    pair_a(g, n - 19)
                for b in range(2):
                    lev, odd = divmod(n - 20 - b, 2)
                    if odd == 1 and lev >= 0:
                        copy_x(g, b, lev + 1)
                    if odd == 0 and lev >= 0:
                        copy_xt(g, b, lev)
                if n == 21:
                    copy_v(g, 1)
                if n == 22:
                    copy_k(g)
                if n % 4 == 0 and n > 0:
                    evac(g, n // 4 - 1)
                if n in (5, 9, 13, 17):
                    tap0(g, n // 4 - 1)
                if n in (6, 10, 14, 18):
                    tanh(g, n // 4 - 1)
                if n == 21:
                    tanh(g, 4)
                if n in (9, 10):
                    decays(g, n - 9)
                if n == 11:
                    squares(g)
            if prev_on and n == 12:
                o_squares(h, 0)
                o_squares(h, 1)
            if n == 13 and (prev_on or cur_on):
                roots(g, cur_on, prev_on)

        def group(g, d, prev_on):
            for n in range(GSLOT):
                split_hi(PH_IN1["c"] + n + LEAD, d * GSLOT)
                if not prev_on and n in (0, 1):
                    gates(n)
                if not prev_on and n == 4:
                    gates(2)
                slot(n, g, True, prev_on)

        group(0, 0, False)
        with act.Fori(1, NG) as g:
            group(g, g, True)
        def o_hi(j):
            if j == 0:
                act.wait_ge(s_used, PH_OUT1["c"])
            act.wait_ge(s_og, j + 1)
            nc.scalar.activation(ohi[:, 2 * j:2 * j + 2, :], o32[:, 2 * j:2 * j + 2, :], ACT.Copy).then_inc(s_oh, 1)

        o_hi(0)
        o_hi(1)
        for n in range(15 + 1):
            if n < NFREE:
                split_hi(PH_OUT1["c"] + n + LEAD, 0)
                if n + 2 < NFREE:
                    o_hi(n + 2)
            slot(n, NG, False, True)
        o_hi(NFREE)
        o_hi(NFREE + 1)
        out_projection(PH_OUT1, NVH // 2, 16, done=NFREE)
        norm(3)
        feed_forward(1, PH_FF1, PH_DN1, True)

    @block.vector
    def _(v):
        def split_lo(c, d):
            if c >= CHUNKS and not looped(d):
                return
            v.wait_ge(s_hi, d + (c + 1))
            nc.vector.tensor_tensor(wlo[:, c % RING, :], raw[:, c % RING, :], whi[:, c % RING, :].bitcast(F32),
                                    ALU.subtract).then_inc(s_lo, 1)

        def add_halves(out, b, t, dt, tiles=2):
            v.wait_ge(s_ca, dt + (t + 1))
            b2 = 2 * (b % 2)
            nc.vector.tensor_tensor(out, dn[:, b2:b2 + tiles, S:2 * S], halfa[:, 0:tiles, :], ALU.add).then_inc(s_evac, 1)

        def root_input(n, sums, cond):
            v.wait_ge(*cond)
            if n >= 2:
                v.wait_ge(s_rs, n - 1)
            nc.vector.tensor_reduce(tot[:, n % 2, :], sums[:, :, :], AX, ALU.add).then_inc(s_tot, 1)
            v.wait_ge(s_tot, n + 1)
            nc.vector.tensor_scalar(meansq[:, n % 2, :], tot[:, n % 2, :], 1.0 / D, EPS, ALU.mult, ALU.add).then_inc(s_ms, 1)

        def norm(n):
            root_input(2 * n, ssx, (s_sqx, 8 * (n + 1)))
            if n == 0:
                v.wait_ge(s_vec, 1)
                nc.vector.tensor_scalar(nwh[:, :], vecT[:, 4 * KT + 8:4 * KT + 9], 0.5, None, ALU.mult).then_inc(s_nwh, 1)
            v.wait_ge(s_rs, 2 * n + 1)
            g0 = n // 2 * KT + (2 * KT if n % 2 else 0)

            def scale(kg):
                if kg >= 2:
                    v.wait_ge(s_xtp, 4 * n + kg - 1)
                at_ = ((kg % 2) * NT + 1) * 512
                nc.vector.tensor_scalar(scr[:, at_:at_ + 512], x[:, 1, kg * 512:(kg + 1) * 512], rstd[:, 0, 1:2],
                                        None, ALU.mult).then_inc(s_xs1, 1)

            scale(0)
            scale(1)
            if n == 0:
                for c in range(LEAD):
                    split_lo(c, 0)
            for kg in range(4):
                for q in range(4):
                    kt = 4 * kg + q
                    v.wait_ge(s_hnh, 16 * n + 2 * (kt // 2) + 2)
                    nc.vector.scalar_tensor_tensor(out=hn[:, kt, S:2 * S],
                                                   in0=mi[:, 2 * (kg % 2) + q // 2, (q % 2) * S:(q % 2 + 1) * S],
                                                   scalar=vecT[:, g0 + kt:g0 + kt + 1], in1=hn[:, kt, 0:S].bitcast(F32),
                                                   op0=ALU.mult, op1=ALU.subtract).then_inc(s_hnl, 1)
                if kg + 2 < 4:
                    scale(kg + 2)

        def update_x(n, m):
            root_input(2 * n + 1, ssm, (s_sqm, 8 * (n + 1)))
            v.wait_ge(s_rs, 2 * n + 2)
            for b in range(NCB):
                for t in range(NT):
                    cs = slice(b * NW, (b + 1) * NW)
                    nc.vector.scalar_tensor_tensor(out=x[:, t, cs], in0=m[:, t, cs], scalar=rstd[:, 1, t:t + 1],
                                                   in1=x[:, t, cs], op0=ALU.mult, op1=ALU.add).then_inc(s_xup, 1)

        def out_projection(n_norm, ph, n, m, gn, final=False, done=0):
            def body(i, d, done=0):
                for u in range(2):
                    for j in range(0 if u else done, n):
                        c = ph["c"] + u * n + j
                        if not (final and c + LEAD + (d if isinstance(d, int) else 0) >= CHUNKS):
                            split_lo(c + LEAD, d)
                        if j == n - 1:
                            v.wait_ge(s_gain, 16 * (n_norm + 1))
                            cs = bass.ds(i * (2 * NW) + u * NW, NW)
                            for t in range(NT):
                                v.wait_ge(s_sqm, i * 4 + (8 * n_norm + 2 * u + t + 1))
                                e = nc.vector.tensor_tensor(m[:, t, cs], dn[:, 2 * ((ph["b"] + u) % 2) + t, :],
                                                            gn[:, cs], ALU.mult)
                            e.then_inc(s_evac, 1)
            if final:
                for i in range(NCB // 2):
                    body(i, i * 2 * n)
            else:
                if done:
                    body(0, 0, done)
                with v.Fori(1 if done else 0, NCB // 2) as i:
                    body(i, i * (2 * n))
            v.wait_ge(s_evac, ph["b"] + NCB)
            update_x(n_norm, m)

        def feed_forward(layer, ph, pd, final):
            with v.Fori(0, FI) as i:
                for j in range(8):
                    split_lo(ph["c"] + j + LEAD, i * 8)
                    if j == 3:
                        add_halves(fg, ph["b"], ph["t"], i * 2)
                    if j == 5:
                        v.wait_ge(s_th, i + (FI * layer + 1))
                        nc.vector.scalar_tensor_tensor(out=fth, in0=fth, scalar=1.0, in1=fg, op0=ALU.add,
                                                       op1=ALU.mult).then_inc(s_t1, 1)
                    if j == 7:
                        add_halves(fu, ph["b"] + 1, ph["t"] + 1, i * 2)
                        v.wait_ge(s_evac, i * 2 + (ph["b"] + 2))
                        v.wait_ge(s_t1, i + (FI * layer + 1))
                        nc.vector.scalar_tensor_tensor(out=fh, in0=fth, scalar=0.5, in1=fu, op0=ALU.mult,
                                                       op1=ALU.mult).then_inc(s_h, 1)
                        v.wait_ge(s_hh, i + (FI * layer + 1))
                        nc.vector.tensor_tensor(hid[:, bass.ds(i * 2, 2), S:2 * S], fh,
                                                hid[:, bass.ds(i * 2, 2), 0:S].bitcast(F32), ALU.subtract).then_inc(s_hl, 1)
            out_projection(2 * layer + 1, pd, FF // P // 2, m_a, gain, final)

        nc.vector.memset(epsc[:, 0:1], EPS).then_inc(s_eps, 1)
        nc.vector.memset(epsc[:, 1:2], EPS * DH).then_inc(s_eps, 1)
        norm(0)

        def score_add(ih):
            v.wait_ge(s_rel, ih + 1)
            for t in range(NT):
                w = P * (t + 1)
                cs = slice(t * P, t * P + w)
                if ih == 0:
                    nc.vector.tensor_scalar(score[:, cs], rel[:, 0, cs], wi[:, t, 0:1], None, ALU.mult).then_inc(s_sc, 1)
                else:
                    v.wait_ge(s_sc, NT * (ih - 1) + t + 1)
                    nc.vector.scalar_tensor_tensor(out=score[:, cs], in0=rel[:, ih % 2, cs], scalar=wi[:, t, ih:ih + 1],
                                                   in1=score[:, cs], op0=ALU.mult, op1=ALU.add).then_inc(s_sc, 1)

        def topk_round(r):
            if r == 0:
                v.wait_ge(s_causal, NT)
            for t in range(NT):
                w = P * (t + 1)
                if r >= 1:
                    v.wait_ge(s_repl, NT * (r - 1) + t + 1)
                nc.vector.max(top8[:, t, :], score[:, t * P:t * P + w]).then_inc(s_max8, 1)
            for t in range(NT):
                w = P * (t + 1)
                cs = slice(t * P, t * P + w)
                v.wait_ge(s_max8, NT * r + t + 1)
                nc.vector.match_replace(score[:, cs], top8[:, t, :], score[:, cs], TAKEN).then_inc(s_repl, 1)

        def soften(h):
            v.wait_ge(s_lg, h + 1)
            v.wait_ge(s_bm, h + 1)
            nc.vector.scalar_tensor_tensor(out=prob[:, h % 2, :], in0=mi[:, 0, 0:3 * P], scalar=float(DH) ** -0.5,
                                           in1=bm[:, h, :], op0=ALU.mult, op1=ALU.add).then_inc(s_lb, 1)
            v.wait_ge(s_lb, h + 1)
            for t in range(NT):
                w = P * (t + 1)
                nc.vector.tensor_reduce(mx[:, h, t:t + 1], prob[:, h % 2, t * P:t * P + w], AX, ALU.max,
                                        negate=True).then_inc(s_mx, 1)

        def scale_probs(h):
            v.wait_ge(s_ex, NT * (h + 1))
            nc.vector.reciprocal(rps[:, h, :], psm[:, h, :]).then_inc(s_rp, 1)
            v.wait_ge(s_rp, h + 1)
            for t in range(NT):
                w = P * (t + 1)
                pv = prob[:, h % 2, t * P:t * P + w]
                nc.vector.tensor_scalar(pv, pv, rps[:, h, t:t + 1], None, ALU.mult).then_inc(s_pn, 1)

        wins = [0]

        def pool_window(k):
            gi = xp_order[k]
            n = len(blocks0) - 4 + k
            v.wait_ge(s_evac, n + 1)
            if k >= 1:
                v.wait_ge(s_mp, k)
            src, step = xpad, 1
            for lev in range(gi + 1):
                dst = winb if (gi - lev) % 2 == 0 else wina
                lo = 2 * step - 1
                if wins[0]:
                    v.wait_ge(s_win, wins[0])
                nc.vector.tensor_tensor(dst[:, :, lo:16 + S], src[:, :, lo:16 + S], src[:, :, lo - step:16 + S - step],
                                        ALU.add).then_inc(s_win, 1)
                wins[0] += 1
                src, step = dst, 2 * step
            v.wait_ge(s_win, wins[0])
            if k == 0:
                v.wait_ge(s_cst, 16)
            inv = cst[:, K_INV + 16 * gi:K_INV + 16 * gi + 16].unsqueeze(1).broadcast_to([P, 2, 16])
            nc.vector.tensor_tensor(wina[:, :, 16:32], winb[:, :, 16:32], inv, ALU.mult).then_inc(s_win, 1)
            wins[0] += 1
            v.wait_ge(s_win, wins[0])
            nc.vector.tensor_tensor(wina[:, :, 16:32], wina[:, :, 16:32], xpad[:, :, 16:32], ALU.subtract).then_inc(s_pd, 1)
            nc.vector.scalar_tensor_tensor(out=wina[:, :, 32:16 + S], in0=winb[:, :, 32:16 + S], scalar=1.0 / WINDOWS[gi],
                                           in1=xpad[:, :, 32:16 + S], op0=ALU.mult, op1=ALU.subtract).then_inc(s_pd, 1)

        for s in range(len(chunks0) + OVER0):
            split_lo(s + LEAD, 0)
            if s in evac_at:
                n = evac_at[s]
                kind, idx, _, _ = blocks0[n]
                if kind == "kw":
                    add_halves(kiw[:, :].unsqueeze(1), n, tidx0[n], 0, tiles=1)
                elif kind == "qi":
                    add_halves(qiT[:, idx % 2, :, :], n, tidx0[n], 0)
                elif kind == "v":
                    v.wait_ge(s_used, s)
                    b2 = 2 * (n % 2)
                    nc.vector.tensor_copy(vtm[:, idx % 2, :, :], dn[:, b2:b2 + 2, 0:TW]).then_inc(s_evac, 1)
                elif kind == "k":
                    add_halves(kqT[:, 0, :, :], n, tidx0[n], 0)
                elif kind == "q":
                    add_halves(kqT[:, 1, :, :], n, tidx0[n], 0)
                else:
                    if n == len(blocks0) - 4:
                        v.wait_ge(s_pad, 3)
                    else:
                        v.wait_ge(s_pd, 2 * (n - len(blocks0) + 4))
                    add_halves(xpad[:, :, 16:16 + S], n, tidx0[n], 0)
            if s == 4:
                v.wait_ge(s_wip, 1)
                nc.vector.tensor_scalar(wi[:, :, :], mi[:, BX, 0:2 * P].rearrange("p (t f) -> p t f", t=2)[:, :, DIH:DIH + NIH],
                                        NIH ** -0.5, None, ALU.mult).then_inc(s_wi, 1)
                v.wait_ge(s_wi, 1)
            if 7 <= s < 7 + NIH:
                score_add(s - 7)
            if SC0 < s <= SC0 + NR:
                topk_round(s - SC0 - 1)
            if s == SC0 + NR + 1:
                v.wait_ge(s_repl, NT * NR)
                nc.vector.tensor_scalar(score[:, :], score[:, :], TAKEN / 3, NEG, ALU.is_gt, ALU.mult).then_inc(s_seln, 1)
            if s in head_at:
                soften(head_at[s])
            if s - 1 in head_at:
                scale_probs(head_at[s - 1])
            if s - 3 in head_at:
                h = head_at[s - 3]
                v.wait_ge(s_mh_, h + 1)
                nc.vector.tensor_tensor(mix[:, h, S:2 * S], mi[:, 2, 0:S], mix[:, h, 0:S].bitcast(F32),
                                        ALU.subtract).then_inc(s_ml, 1)
            for k in range(4):
                if s == end0[17 + k] + 1:
                    pool_window(k)
                if s == end0[17 + k] + 2:
                    gi = xp_order[k]
                    v.wait_ge(s_ph, 2 * (k + 1))
                    for dt in range(2):
                        col = 4 * KT + 2 * gi + dt
                        i = nc.vector.scalar_tensor_tensor(out=mix[:, NH + 2 * gi + dt, S:2 * S], in0=mi[:, 3, dt * S:(dt + 1) * S],
                                                           scalar=vecT[:, col:col + 1], in1=mix[:, NH + 2 * gi + dt, 0:S].bitcast(F32),
                                                           op0=ALU.mult, op1=ALU.subtract)
                    i.then_inc(s_pl, 1)
        out_projection(0, PH_OUT0, KT // 2, m_a, gain, done=OVER0)
        norm(1)
        feed_forward(0, PH_FF0, PH_DN0, False)
        norm(2)
        split_lo(PH_BA["c"] + LEAD, 0)
        split_lo(PH_BA["c"] + 1 + LEAD, 0)
        add_halves(conv_y[:, 0:1, :], PH_BA["b"], PH_BA["t"], 0, tiles=1)

        def gates(step):
            if step == 0:
                v.wait_ge(s_bap, 1)
                nc.vector.tensor_copy(ba[:, :, :], mi[:, BY, 0:2 * P].rearrange("p (t f) -> p t f", t=2)[:, :, P - 2 * NVH:P]).then_inc(s_ba, 1)
                v.wait_ge(s_ba, 1)
                v.wait_ge(s_av, 32)
                nc.vector.tensor_tensor(bat[:, 1, :, :], ba[:, :, NVH:2 * NVH],
                                        avec[:, 0:1, :].broadcast_to([P, 2, NVH]), ALU.add).then_inc(s_t, 1)
                v.wait_ge(s_t, 1)
                nc.vector.scalar_tensor_tensor(out=bat[:, 2, :, :], in0=bat[:, 1, :, :], scalar=-1.0,
                                               in1=bat[:, 1, :, :], op0=ALU.mult, op1=ALU.min).then_inc(s_mn, 1)
            if step == 1:
                v.wait_ge(s_ea, 3)
                nc.vector.tensor_scalar(bat[:, 0, :, :], bat[:, 0, :, :], 1.0, None, ALU.add).then_inc(s_t, 1)
                v.wait_ge(s_t, 2)
                nc.vector.reciprocal(sc4[:, 3, :, :], bat[:, 0, :, :]).then_inc(s_t, 1)
            if step == 2:
                v.wait_ge(s_el, 1)
                nc.vector.scalar_tensor_tensor(out=bat[:, 1, :, :], in0=bat[:, 1, :, :], scalar=0.0,
                                               in1=bat[:, 3, :, :], op0=ALU.max, op1=ALU.add).then_inc(s_sp, 1)
                v.wait_ge(s_sp, 1)
                nc.vector.scalar_tensor_tensor(out=sc4[:, 0, :, :], in0=bat[:, 1, :, :], scalar=-1.0,
                                               in1=avec[:, 1:2, :].broadcast_to([P, 2, NVH]), op0=ALU.mult,
                                               op1=ALU.mult).then_inc(s_g, 1)
            if step == 3:
                v.wait_ge(s_gcp, 1)
                nc.vector.tensor_copy(sc4[:, 1, :, :], mi[:, BX, 256:256 + 2 * NVH].rearrange("p (a b) -> p a b", a=2)).then_inc(s_gc, 1)
            if step == 4:
                v.wait_ge(s_eg, 1)
                nc.vector.tensor_scalar(sc4[:, 2, :, :], sc4[:, 2, :, :], -1.0, None, ALU.mult).then_inc(s_sc4, 1)

        def take_scalars(g):
            if not looped(g):
                v.wait_ge(s_sc4, 1)
                v.wait_ge(s_t, 3)
            else:
                v.wait_ge(s_v1, g * 1)
            nc.vector.tensor_copy(cur[:, :, :, :], sc4[:, :, :, bass.ds(g * 4, 4)]).then_inc(s_cur, 1)

        def take_gc(g):
            if not looped(g):
                v.wait_ge(s_sc4, 1)
            else:
                v.wait_ge(s_clamp, g * 2)
            nc.vector.tensor_copy(gch[:, :, :], sc4[:, 1, :, bass.ds(g * 4, 4)]).then_inc(s_gch, 1)

        def take_taps(g):
            if not looped(g):
                v.wait_ge(s_cw, 1)
            for at_, w, base, step in ((0, 2, NKH, 2), (2, 2, 0, 2), (4, 4, 2 * NKH, 4)):
                i = nc.vector.tensor_copy(cwc[:, :, at_:at_ + w], cwT[:, :, bass.ds(g * step + base, w)])
            i.then_inc(s_cwc, 1)

        def evac(g, b):
            out = cpad[:, :, 3:3 + S] if b < 4 else zs[:, 2 * (b - 4):2 * (b - 4) + 2, :]
            add_halves(out, PH_IN1["b"] + b, PH_IN1["t"] + b, g * 6)

        def taps(g, b):
            v.wait_ge(s_tap0, g * 4 + (b + 1))
            for k in range(3):
                for f in range(2):
                    if k >= 1:
                        v.wait_ge(s_tap, g * 24 + (6 * b + 2 * (k - 1) + f + 1))
                    nc.vector.scalar_tensor_tensor(out=conv_y[:, f, :], in0=cpad[:, f, 2 - k:2 - k + S],
                                                   scalar=cwc[:, 2 - k, 2 * b + f:2 * b + f + 1], in1=conv_y[:, f, :],
                                                   op0=ALU.mult, op1=ALU.add).then_inc(s_tap, 1)

        def silu(g, b):
            v.wait_ge(s_thc, g * 6 + (b + 1))
            out = kqr[:, b, :, :] if b < 2 else vfm[:, :, :]
            if b == 3:
                v.wait_ge(s_vtp, g * 2 + 1)
            nc.vector.scalar_tensor_tensor(out=out, in0=conv_th, scalar=1.0, in1=conv_y, op0=ALU.add,
                                           op1=ALU.mult).then_inc(s_silu, 1)

        def gate_z(g, k):
            v.wait_ge(s_thc, g * 6 + (5 + k))
            z = zs[:, 2 * k:2 * k + 2, :]
            nc.vector.scalar_tensor_tensor(out=z, in0=conv_th, scalar=1.0, in1=z, op0=ALU.add,
                                           op1=ALU.mult).then_inc(s_zg, 1)

        def clamp(g, c):
            v.wait_ge(s_gb, g * 2 + (c + 1))
            for u in range(4):
                i = nc.vector.tensor_scalar(dec[:, c, u, :], mi[:, BM, u * P:(u + 1) * P], gch[:, c, u:u + 1], 0.0,
                                            ALU.subtract, ALU.min)
            i.then_inc(s_clamp, 1)

        def invert_norms(g, kq_on, o_on):
            v.wait_ge(s_rt, g * 1 + 1)
            cs = slice(0 if kq_on else 8, 16 if o_on else 8)
            nc.vector.reciprocal(nrm[:, cs], nrm[:, cs]).then_inc(s_rc, 1)

        def norm_kq(g):
            for k in range(2):
                v.wait_ge(s_nr, g * 2 + (k + 1))
                nc.vector.tensor_tensor(kq[:, k, :, :].rearrange("p b c -> p (b c)"),
                                        kqr[:, k, :, :].rearrange("p b c -> p (b c)"), mi[:, (BM, BY)[k], :],
                                        ALU.mult).then_inc(s_kqn, 1)

        def o_heads(g, k):
            return o32[:, bass.ds(g * 4 + 2 * k, 2), :]

        def gate_o(g, k):
            v.wait_ge(s_osq, g * 2 + (k + 1))
            v.wait_ge(s_zg, g * 2 + (k + 1))
            nc.vector.scalar_tensor_tensor(out=o_heads(g, k), in0=mi[:, (BX, BT)[k], :].rearrange("p (a b) -> p a b", a=2),
                                           scalar=nwh[:, 0:1], in1=zs[:, 2 * k:2 * k + 2, :], op0=ALU.mult,
                                           op1=ALU.mult).then_inc(s_on, 1)

        def norm_o(g, k):
            v.wait_ge(s_onr, g * 2 + (k + 1))
            v.wait_ge(s_on, g * 2 + (k + 1))
            nc.vector.tensor_tensor(o_heads(g, k), o_heads(g, k), mi[:, (BX, BT)[k], :].rearrange("p (a b) -> p a b", a=2),
                                    ALU.mult).then_inc(s_og, 1)

        def weigh(g, c):
            v.wait_ge(s_gq, g * 2 + (c + 1))
            v.wait_ge(s_dec, g * 2 + (c + 1))
            for u in range(4):
                kp = u // 2
                i = nc.vector.scalar_tensor_tensor(out=at[:, c, u, :], in0=mi[:, BM, kp * 256:kp * 256 + P],
                                                   scalar=cur[:, 3, c, u:u + 1], in1=dec[:, c, u, :], op0=ALU.mult,
                                                   op1=ALU.mult)
            i.then_inc(s_atr, 1)
            for kp in range(2):
                i = nc.vector.tensor_tensor(intra[:, c, 2 * kp:2 * kp + 2, :],
                                            mi[:, BM, kp * 256 + P:kp * 256 + 2 * P].unsqueeze(1).broadcast_to([P, 2, P]),
                                            dec[:, c, 2 * kp:2 * kp + 2, :], ALU.mult)
            i.then_inc(s_inr, 1)

        def first_x(g, b):
            v.wait_ge(s_at, g * 2 + (b + 1))
            nc.vector.tensor_tensor(xt[:, b, :, :], at[:, b, :, :],
                                    cst[:, K_M0:K_M0 + P].unsqueeze(1).broadcast_to([P, 4, P]), ALU.mult).then_inc(s_x1t, 1)

        def mask_w(g, b, lev):
            v.wait_ge(s_y, g * 12 + (2 * (lev - 1) + b + 1))
            half = P // 2
            src = mi[:, BY, 0:2 * P]
            if lev < NLEV:
                mk = cst[:, K_MT + (lev - 1) * P:K_MT + lev * P].rearrange("p (a x) -> p a x", a=2)
                nc.vector.tensor_tensor(wy[:, b, :, 0:half].rearrange("p (h a) x -> p h a x", h=2),
                                        src.rearrange("p (h a x) -> p h a x", h=2, a=2),
                                        mk.unsqueeze(1).broadcast_to([P, 2, 2, half]), ALU.mult).then_inc(s_w, 1)
            else:
                mk = cst[:, K_MT + (lev - 1) * P:K_MT + (lev - 1) * P + half].unsqueeze(1).broadcast_to([P, 4, half])
                nc.vector.tensor_tensor(wy[:, b, :, 0:half], src.rearrange("p (u s) -> p u s", u=4), mk,
                                        ALU.mult).then_inc(s_w, 1)

        def decay_q(g):
            v.wait_ge(s_eq, g * 1 + 1)
            v.wait_ge(s_kqn, g * 2 + 2)
            for kp in range(2):
                i = nc.vector.tensor_tensor(qd[:, 2 * kp:2 * kp + 2, :], egc[:, 2 * kp:2 * kp + 2, :],
                                            kq[:, 1, kp:kp + 1, P:S].broadcast_to([P, 2, P]), ALU.mult)
            i.then_inc(s_qd, 1)

        def decay_k(g):
            v.wait_ge(s_kt, g * 1 + 1)
            for u in range(4):
                i = nc.vector.tensor_scalar(kdec[:, u, :], ktok[:, u // 2, :], dec[:, 0, u, P - 1:P], None, ALU.mult)
            i.then_inc(s_kd, 1)

        def times_beta(g, c):
            v.wait_ge((s_y0, s_y1)[c], g * 1 + 1)
            for u in range(4):
                i = nc.vector.tensor_scalar(vn[:, c, u, :], mi[:, BY, u * P:(u + 1) * P], cur[:, 3, c, u:u + 1], None,
                                            ALU.mult)
            i.then_inc((s_v0, s_v1)[c], 1)

        def rhs1(g):
            v.wait_ge(s_ks, g * 1 + 1)
            for u in range(4):
                i = nc.vector.scalar_tensor_tensor(out=vtok[:, 1, u, :], in0=mi[:, BY, u * P:(u + 1) * P],
                                                   scalar=cur[:, 2, 1, u:u + 1], in1=vtok[:, 1, u, :], op0=ALU.mult,
                                                   op1=ALU.add)
            i.then_inc(s_r1, 1)

        def urgent(n, g, cur_on, prev_on):
            if prev_on and n + GSLOT == 35:
                times_beta(g - 1, 1)
            if cur_on:
                if n == 15:
                    norm_kq(g)
                if n in (16, 17):
                    weigh(g, n - 16)
                if n in (17, 18):
                    first_x(g, n - 17)

        def slot(n, g, cur_on, prev_on):
            if prev_on:
                h, m = g - 1, n + GSLOT
                if m == 24:
                    evac(h, 5)
                if m == 26:
                    gate_z(h, 1)
                for b in range(2):
                    lev, odd = divmod(m - 20 - b, 2)
                    if odd == 0 and 1 <= lev + 1 <= NLEV:
                        mask_w(h, b, lev + 1)
                if m == 32:
                    times_beta(h, 0)
                if m == 34:
                    rhs1(h)
            if cur_on:
                if n == 3:
                    take_taps(g)
                if n == 8:
                    take_gc(g)
                if n in (9, 10):
                    clamp(g, n - 9)
                if n == 11:
                    take_scalars(g)
            if n == 13 and (cur_on or prev_on):
                invert_norms(g, cur_on, prev_on)
            if prev_on and n == 13:
                gate_o(h, 0)
                gate_o(h, 1)
            if cur_on:
                if n == 18:
                    decay_q(g)
                for b in range(2):
                    lev, odd = divmod(n - 20 - b, 2)
                    if odd == 0 and lev >= 0:
                        mask_w(g, b, lev + 1)
                if n % 4 == 0 and n > 0:
                    evac(g, n // 4 - 1)
                if n in (7, 11, 15, 19):
                    silu(g, n // 4 - 1)
                if n in (5, 9, 13, 17):
                    taps(g, n // 4 - 1)
                if n == 22:
                    gate_z(g, 0)
                if n == 23:
                    decay_k(g)
            if prev_on and n in (18, 19):
                norm_o(h, n - 18)

        def group(g, d, prev_on):
            for n in range(GSLOT):
                urgent(n, g, True, prev_on)
                split_lo(PH_IN1["c"] + n + LEAD, d * GSLOT)
                if not prev_on and n < 5:
                    gates(n)
                slot(n, g, True, prev_on)

        v.wait_ge(s_pz, 1)
        group(0, 0, False)
        with v.Fori(1, NG) as g:
            group(g, g, True)
        def o_lo(j):
            v.wait_ge(s_oh, j + 1)
            nc.vector.tensor_tensor(olo[:, 2 * j:2 * j + 2, :], o32[:, 2 * j:2 * j + 2, :],
                                    ohi[:, 2 * j:2 * j + 2, :].bitcast(F32), ALU.subtract).then_inc(s_ol, 1)

        o_lo(0)
        o_lo(1)
        for n in range(19 + 1):
            urgent(n, NG, False, True)
            if n < NFREE:
                split_lo(PH_OUT1["c"] + n + LEAD, 0)
                if n + 2 < NFREE:
                    o_lo(n + 2)
            slot(n, NG, False, True)
        o_lo(NFREE)
        o_lo(NFREE + 1)
        out_projection(2, PH_OUT1, NVH // 2, m_b, gain_b, done=NFREE)
        norm(3)
        feed_forward(1, PH_FF1, PH_DN1, True)


_INS = ["x", "rel_bias", "even_w_in", "even_w_o", "pool_w", "pool_scale", "odd_w_in", "conv_w", "a_log", "dt_bias",
        "gdn_norm_w", "odd_w_o", "ffn_w_gate", "ffn_w_up", "ffn_w_down", "mix_pre_g", "mix_post_g", "ffn_pre_g",
        "ffn_post_g"]


def kernel(**inputs):
    import numpy as _np
    import concourse.bacc as _bacc
    from concourse.bass_utils import run_bass_kernel_spmd as _run

    nc = _bacc.Bacc("TRN2", target_bir_lowering=False, num_devices=1)
    arrays, io = {}, {}
    given = {n: _np.ascontiguousarray(inputs[n]) for n in _INS}
    given["consts"] = constants()
    given["onehot"] = bucket_onehot()
    for name, a in given.items():
        arrays[f"in_{name}"] = a
        io[name] = nc.dram_tensor(f"in_{name}", a.shape, F32, kind="ExternalInput").ap()
    io["out"] = nc.dram_tensor("out_x", (1, S, D), F32, kind="ExternalOutput").ap()
    trunk(nc, io)
    r = _run(nc, [arrays], core_ids=[0])
    return r.results[0]["out_x"]
```

```python
from contextlib import ExitStack
import math

import numpy as np

import concourse.bass as bass
from concourse import mybir

F32 = mybir.dt.float32
F32R = mybir.dt.float32r
ALU = mybir.AluOpType
ACT = mybir.ActivationFunctionType
AX = mybir.AxisListType.X

P = 128
D = 2048
S = 256
NT = S // P
KT = D // P
AW = D // 2
DH = 128
NH = AW // DH
NIH, DIH = 16, 64
TOPK = min(256, S // 4)
NEG = -1e30
TAKEN = -3e38
WINDOWS = (2, 4, 8, 16)
PGW = D // 8
NB = 32
EVEN_IN = 3 * AW + NIH * DIH + DIH + NIH + len(WINDOWS) * PGW
C_QI, C_KI, C_XP = 3 * AW, 3 * AW + NIH * DIH, 3 * AW + NIH * DIH + DIH + NIH
NKH = D // 128
NVH = 2 * NKH
QKW, VW = NKH * 128, NVH * 128
CONVW = 2 * QKW + VW
NTAP = 4
ODD_IN = CONVW + VW + 2 * NVH
FF = -(-8 * D // (3 * 256)) * 256
EPS = 1e-6
NSEG = P + S - 1
SEG = S + P

CH = 1024
RING = 4
LEAD = 3
TW, NW = 256, 512
NCB = D // NW
FI = FF // TW
NG = NKH // 2
GSLOT = 24
OVER0 = 3
NFREE = NKH - 2
NLEV = 6

PH_IN0 = dict(c=0, b=0, t=0)
PH_OUT0 = dict(c=82, b=21, t=17)


def _after(ph, c, b, t):
    return dict(c=ph["c"] + c, b=ph["b"] + b, t=ph["t"] + t)


PH_FF0 = _after(PH_OUT0, NCB * KT // 2, NCB, 0)
PH_DN0 = _after(PH_FF0, 8 * FI, 2 * FI, 2 * FI)
PH_BA = _after(PH_DN0, NCB * FF // P // 2, NCB, 0)
PH_IN1 = _after(PH_BA, 2, 1, 1)
PH_OUT1 = _after(PH_IN1, GSLOT * NG, 6 * NG, 6 * NG)
PH_FF1 = _after(PH_OUT1, NCB * NVH // 2, NCB, 0)
PH_DN1 = _after(PH_FF1, 8 * FI, 2 * FI, 2 * FI)
CHUNKS = PH_DN1["c"] + NCB * FF // P // 2

K_ID, K_ONE, K_U, K_M0 = 0, P, 2 * P, 3 * P
K_MT = 4 * P
K_INV = K_MT + (NLEV - 1) * P + P // 2
K_END = K_INV + len(WINDOWS) * 16


def constants():
    k = np.zeros((P, K_END), np.float32)
    i, j = np.arange(P)[:, None], np.arange(P)[None, :]
    k[:, K_ID:K_ID + P] = np.eye(P)
    k[:, K_ONE:K_ONE + P] = 1
    k[:, K_U:K_U + P] = i <= j
    hf = P // 2
    for lev in range(NLEV + 1):
        s = 2 ** lev
        off = (i // (2 * s) == j // (2 * s)) & (i // s % 2 == 1) & (j // s % 2 == 0)
        m = np.eye(P) - off
        if lev == 0:
            k[:, K_M0:K_M0 + P] = m.T
        else:
            even = m[:, j[0] // s % 2 == 0]
            at = K_MT + (lev - 1) * P
            if lev == NLEV:
                k[:, at:at + hf] = even
            else:
                q = even[:hf, :hf // 2]
                for seg in range(4):
                    r = (0, hf, 0, hf)[seg]
                    k[r:r + hf, at + seg * hf // 2:at + (seg + 1) * hf // 2] = q
    for n, w in enumerate(WINDOWS):
        k[:, K_INV + 16 * n:K_INV + 16 * n + 16] = 1.0 / np.minimum(np.arange(16) + 1, w)
    return k


def bucket_onehot():
    d = np.maximum(S - 1 - np.arange(SEG), 0)
    half = NB // 2
    ratio = np.log(np.maximum(d, 1).astype(np.float32) / half) / math.log(128 / half)
    large = np.minimum(half + (ratio.astype(np.float32) * (NB - half)).astype(np.int32), NB - 1)
    b = np.where(d < half, d, large)
    return (np.arange(NB)[:, None] == b[None, :]).astype(np.float32)


def level_half(ap, lev, odd):
    s = 2 ** lev
    return ap.rearrange("p u (g t s) -> p u g t s", t=2, s=s)[:, :, :, odd, :]


def looped(d):
    return not isinstance(d, int)


def trunk(nc, io):
    with ExitStack() as ctx:
        program(nc, io, ctx)


def program(nc, io, ctx):
    names = set()

    def sb(name, shape, dt=F32, at=ctx):
        return at.enter_context(nc.sbuf_tensor(name, shape, dt))

    def sem(name):
        assert name not in names
        names.add(name)
        return ctx.enter_context(nc.semaphore(name))

    x = sb("x_res", [P, NT, D])
    raw = sb("w_raw", [P, RING, CH])
    whi = sb("w_hi", [P, RING, CH], F32R)
    wlo = sb("w_lo", [P, RING, CH], F32R)
    halfa = sb("halfa", [P, 2, S])
    scr = sb("scr", [P, D])
    cst = sb("cst", [P, K_END])
    nrm = sb("nrm", [P, 16])
    vecT = sb("vecT", [P, 4 * KT + 8 + 1])
    junk = sb("junk", [P, NW])
    ssx = sb("ssx", [P, NT, NCB])
    ssm = sb("ssm", [P, NT, NCB])
    tot = sb("tot", [P, 2, NT])
    meansq = sb("meansq", [P, 2, NT])
    rstd = sb("rstd", [P, 2, NT])
    mhalf = sb("mhalf", [P, NT])
    nwh = sb("nwh", [P, 1])
    epsc = sb("epsc", [P, 2])
    warm = sb("warm", [P, 1])
    ident = cst[:, K_ID:K_ID + P]
    ones = cst[:, K_ONE:K_ONE + P]
    triu = cst[:, K_U:K_U + P]

    with ExitStack() as a1:
        hn = sb("hn", [P, KT, 2 * S], F32R, a1)
    with ExitStack() as a2:
        m_a = sb("m_a", [P, NT, D], F32, a2)
        gain = sb("gain", [P, D], F32, a2)
    with ExitStack() as a3:
        ohi = sb("ohi", [P, NVH, S], F32R, a3)
    sb("region_a", [P, KT * 2 * S])

    with ExitStack() as b1:
        mix = sb("mix", [P, KT, 2 * S], F32R, b1)
        qiT = sb("qiT", [P, 2, 2, S], F32, b1)
        kiw = sb("kiw", [P, S], F32, b1)
        kid = sb("kid", [P, S], F32, b1)
        wi = sb("wi", [P, NT, NIH], F32, b1)
        rel = sb("rel", [P, 2, 3 * P], F32, b1)
        score = sb("score", [P, 3 * P], F32, b1)
        top8 = sb("top8", [P, NT, 8], F32, b1)
        bm = sb("bm", [P, NH, 3 * P], F32, b1)
        kqT = sb("kqT", [P, 2, 2, S], F32, b1)
        vtm = sb("vtm", [P, 2, NT, TW], F32, b1)
        prob = sb("prob", [P, 2, 3 * P], F32, b1)
        pT = sb("pT", [P, 3 * P], F32, b1)
        mx = sb("mx", [P, NH, NT], F32, b1)
        psm = sb("psm", [P, NH, NT], F32, b1)
        rps = sb("rps", [P, NH, NT], F32, b1)
        xpad = sb("xpad", [P, 2, 16 + S], F32, b1)
        wina = sb("wina", [P, 2, 16 + S], F32, b1)
        winb = sb("winb", [P, 2, 16 + S], F32, b1)
        poolw = sb("poolw", [P, len(WINDOWS), 2, PGW], F32, b1)
        onehot = sb("onehot", [NB, SEG], F32, b1)
        relb = sb("relb", [NB, NH], F32, b1)
        vrow = sb("vrow", [4 * KT + 8 + 1, P], F32, b1)
    with ExitStack() as b1b:
        bseg = sb("bseg", [P, NH, SEG], F32, b1b)
    with ExitStack() as b2:
        hid = sb("hid", [P, FF // P, 2 * S], F32R, b2)
    with ExitStack() as b3:
        o32 = sb("o32", [P, NVH, S], F32, b3)
        kqr = sb("kqr", [P, 2, 2, S], F32, b3)
        vfm = sb("vfm", [P, 2, S], F32, b3)
        cpad = sb("cpad", [P, 2, 3 + S + 1], F32, b3)
        kq = sb("kq", [P, 2, 2, S], F32, b3)
        vtok = sb("vtok", [P, 2, 4, P], F32, b3)
        zs = sb("zs", [P, 4, S], F32, b3)
        dec = sb("dec", [P, 2, 4, P], F32, b3)
        at = sb("at", [P, 2, 4, P], F32, b3)
        intra = sb("intra", [P, 2, 4, P], F32, b3)
        xi = sb("xi", [P, 2, 2, 2 * P], F32, b3)
        xt = sb("xt", [P, 2, 4, P], F32, b3)
        wy = sb("wy", [P, 2, 4, P], F32, b3)
        qd = sb("qd", [P, 4, P], F32, b3)
        egc = sb("egc", [P, 4, P], F32, b3)
        gch = sb("gch", [P, 2, 4], F32, b3)
        ktok = sb("ktok", [P, 2, P], F32, b3)
        kdec = sb("kdec", [P, 4, P], F32, b3)
        vn = sb("vn", [P, 2, 4, P], F32, b3)
        st = sb("st", [P, 4, P], F32, b3)
        ba = sb("ba", [P, 2, 2 * NVH], F32, b3)
        sc4 = sb("sc4", [P, 4, 2, NVH], F32, b3)
        cur = sb("cur", [P, 4, 2, 4], F32, b3)
        bat = sb("bat", [P, 4, 2, NVH], F32, b3)
        avec = sb("avec", [P, 2, NVH], F32, b3)
        cwT = sb("cwT", [P, NTAP, 64], F32, b3)
        cwc = sb("cwc", [P, NTAP, 8], F32, b3)
    with ExitStack() as b4:
        olo = sb("olo", [P, NVH, S], F32R, b4)
        gain_b = sb("gain_b", [P, D], F32, b4)
        m_b = sb("m_b", [P, NT, D], F32, b4)
    cwrow = vfm[:, :, 0:P]
    conv_y, conv_th = (scr[:, i * 512:(i + 1) * 512].rearrange("p (a b) -> p a b", a=2) for i in (0, 1))
    sqkq = scr[:, 1024:2048].rearrange("p (a b) -> p a b", a=2)
    atp = egc[:, :, :].rearrange("p (c h) x -> p c h x", c=2)
    osq = wy[:, :, :, :].rearrange("p a b c -> p a (b c)")
    fg, fth, fu, fh = (scr[:, i * 512:(i + 1) * 512].rearrange("p (a b) -> p a b", a=2) for i in range(4))

    dn = ctx.enter_context(nc.psum_tensor("dense", [P, 4, 512], F32))
    mi = ctx.enter_context(nc.psum_tensor("misc", [P, 4, 512], F32))
    BM, BY, BX, BT = range(4)
    seg_dram = nc.dram_tensor("bias_segments", (P, NH * SEG), F32).ap()

    s_raw_loaded = [sem(f"raw_loaded{i}") for i in range(RING)]
    s_hi_made = sem("hi_made")
    s_lo_made = sem("lo_made")
    s_chunk_used = sem("chunk_used")
    s_half_copied = sem("half_copied")
    s_block_evacuated = sem("block_evacuated")
    s_out_squared = sem("out_squared")
    s_x_loaded = [sem(f"x_loaded{b}") for b in range(NCB)]
    s_ident_loaded = sem("ident_loaded")
    s_cst_loaded = sem("cst_loaded")
    s_vrow_loaded = sem("vrow_loaded")
    s_relb_loaded = sem("relb_loaded")
    s_poolw_loaded = sem("poolw_loaded")
    s_vec_turned = sem("vec_turned")
    s_vec_ready = sem("vec_ready")
    s_mhalf_set = sem("mhalf_set")
    s_x_squared = sem("x_squared")
    s_squares_summed = sem("squares_summed")
    s_meansq_ready = sem("meansq_ready")
    s_rstd_ready = sem("rstd_ready")
    s_x_scaled_act = sem("x_scaled_act")
    s_x_scaled_dve = sem("x_scaled_dve")
    s_x_turned = sem("x_turned")
    s_hn_hi = sem("hn_hi")
    s_hn_lo = sem("hn_lo")
    s_gain_loaded = sem("gain_loaded")
    s_x_updated = sem("x_updated")
    s_out_stored = sem("out_stored")
    s_bias_row_psum = sem("bias_row_psum")
    s_bias_row = sem("bias_row")
    s_bias_rows_stored = sem("bias_rows_stored")
    s_bias_read = sem("bias_read")
    s_bias_masked = sem("bias_masked")
    s_ki_copied = sem("ki_copied")
    s_wi_turned = sem("wi_turned")
    s_wi_ready = sem("wi_ready")
    s_dots = sem("dots")
    s_relu_dots = sem("relu_dots")
    s_score_added = sem("score_added")
    s_score_masked = sem("score_masked")
    s_max8 = sem("max8")
    s_replaced = sem("replaced")
    s_selection = sem("selection")
    s_selection_masked = sem("selection_masked")
    s_logits = sem("logits")
    s_logits_biased = sem("logits_biased")
    s_logits_max = sem("logits_max")
    s_probs = sem("probs")
    s_probs_sum_inv = sem("probs_sum_inv")
    s_probs_scaled = sem("probs_scaled")
    s_probs_turned = sem("probs_turned")
    s_probsT = sem("probsT")
    s_attn_out = sem("attn_out")
    s_attn_hi = sem("attn_hi")
    s_attn_lo = sem("attn_lo")
    s_pads_zeroed = sem("pads_zeroed")
    s_window_sum = sem("window_sum")
    s_pooled = sem("pooled")
    s_pool_mixed = sem("pool_mixed")
    s_pool_hi = sem("pool_hi")
    s_pool_lo = sem("pool_lo")
    s_ff_tanh = sem("ff_tanh")
    s_ff_gate = sem("ff_gate")
    s_ff_hidden = sem("ff_hidden")
    s_ff_hi = sem("ff_hi")
    s_ff_lo = sem("ff_lo")
    s_nwh_ready = sem("nwh_ready")
    s_cw_loaded = sem("cw_loaded")
    s_cw_turned = sem("cw_turned")
    s_cw_ready = sem("cw_ready")
    s_avec_loaded = sem("avec_loaded")
    s_cpad_zeroed = sem("cpad_zeroed")
    s_ba_turned = sem("ba_turned")
    s_ba_ready = sem("ba_ready")
    s_a_biased = sem("a_biased")
    s_a_folded = sem("a_folded")
    s_ba_exps = sem("ba_exps")
    s_a_log1p = sem("a_log1p")
    s_softplus = sem("softplus")
    s_g_ready = sem("g_ready")
    s_gc_psum = sem("gc_psum")
    s_gc_ready = sem("gc_ready")
    s_gc_exp = sem("gc_exp")
    s_scalars_ready = sem("scalars_ready")
    s_cur_ready = sem("cur_ready")
    s_cwc_ready = sem("cwc_ready")
    s_tap0 = sem("tap0")
    s_taps = sem("taps")
    s_conv_tanh = sem("conv_tanh")
    s_silu_done = sem("silu_done")
    s_z_gated = sem("z_gated")
    s_gc_rows = sem("gc_rows")
    s_decay_clamped = sem("decay_clamped")
    s_decay_ready = sem("decay_ready")
    s_exp_gc_row = sem("exp_gc_row")
    s_q_decayed = sem("q_decayed")
    s_kq_squared = sem("kq_squared")
    s_norm_sums = sem("norm_sums")
    s_norm_roots = sem("norm_roots")
    s_norm_inverses = sem("norm_inverses")
    s_kq_normed = sem("kq_normed")
    s_kk_qk = sem("kk_qk")
    s_a_raw = sem("a_raw")
    s_intra_raw = sem("intra_raw")
    s_a_strict = sem("a_strict")
    s_a_ready = sem("a_ready")
    s_intra_ready = sem("intra_ready")
    s_v_turned = sem("v_turned")
    s_v_tok = sem("v_tok")
    s_k_turned = sem("k_turned")
    s_k_tok = sem("k_tok")
    s_k_decayed = sem("k_decayed")
    s_x1T = sem("x1T")
    s_x1_turned = sem("x1_turned")
    s_x1 = sem("x1")
    s_ax_psum = sem("ax_psum")
    s_w_ready = sem("w_ready")
    s_x_psum = sem("x_psum")
    s_x_evacuated = sem("x_evacuated")
    s_y0 = sem("y0")
    s_vnew0 = sem("vnew0")
    s_state_psum = sem("state_psum")
    s_state = sem("state")
    s_k_state = sem("k_state")
    s_rhs1 = sem("rhs1")
    s_y1 = sem("y1")
    s_vnew1 = sem("vnew1")
    s_o_psum = sem("o_psum")
    s_o_squared = sem("o_squared")
    s_o_normed = sem("o_normed")
    s_o_gated = sem("o_gated")
    s_o_norm_sums = sem("o_norm_sums")
    s_a_paired = sem("a_paired")
    s_x_turned_level = sem("x_turned_level")
    s_xT_evacuated = sem("xT_evacuated")
    s_gc_taken = sem("gc_taken")
    s_norm_rows = sem("norm_rows")
    s_o_norm_rows = sem("o_norm_rows")
    s_w_identity_part = sem("w_identity_part")
    s_o_hi = sem("o_hi")
    s_o_lo = sem("o_lo")
    s_eps_set = sem("eps_set")

    kmap0 = list(range(NH // 2)) + [NH // 2 + gi for gi in (3, 2, 1, 0)]
    xp_order = (3, 2, 1, 0)

    blocks0 = [("kw", 0, C_KI, 2)] + [("qi", b, C_QI + b * TW, 4) for b in range(4)]
    for p in range(NH // 2):
        blocks0 += [("v", p, 2 * AW + p * TW, 4), ("k", p, AW + p * TW, 4), ("q", p, p * TW, 4)]
    blocks0 += [("xp", gi, C_XP + gi * PGW, 4) for gi in xp_order]
    chunks0 = [(n, j) for n, blk in enumerate(blocks0) for j in range(blk[3])]
    end0 = np.cumsum([blk[3] for blk in blocks0]).tolist()
    tidx0 = np.cumsum([0] + [blk[0] != "v" for blk in blocks0]).tolist()
    assert len(chunks0) == PH_OUT0["c"] and len(blocks0) == PH_OUT0["b"] and tidx0[-1] == PH_OUT0["t"]
    evac_at = {e: n for n, e in enumerate(end0)}
    SC0 = 23
    NR = TOPK // 8
    ATT = [SC0 + NR + 3 + 12 * p for p in range(NH // 2)]
    head_at = {ATT[h // 2] + 2 * (h % 2): h for h in range(NH)}
    GB_COL = {0: QKW, 1: 0, 2: 2 * QKW, 3: 2 * QKW + TW, 4: CONVW, 5: CONVW + TW}
    GB_STEP = {0: TW, 1: TW, 2: 2 * TW, 3: 2 * TW, 4: 2 * TW, 5: 2 * TW}
    w_in0, w_in1 = io["even_w_in"][0], io["odd_w_in"][0]

    block = ctx.enter_context(nc.Block())

    @block.sync
    def _(sp):
        def load(c, d, view, src):
            if c >= RING or looped(d):
                sp.wait_ge(s_lo_made, d + (c - RING + 1))
            sp.dma_start(view, src).then_inc(s_raw_loaded[c % RING], 16)

        def slot(c, k):
            return raw[:, c % RING, :].rearrange("p (k n) -> p k n", k=k)

        def load_t(c, d, w, j, col):
            load(c, d, slot(c, 4), w[4 * j * P:(4 * j + 4) * P, bass.ds(col, TW)].rearrange("(k p) n -> p k n", p=P))

        def load_n(c, d, w, kp, col):
            load(c, d, slot(c, 2), w[2 * kp * P:(2 * kp + 2) * P, bass.ds(col, NW)].rearrange("(k p) n -> p k n", p=P))

        def load_w128(c, w, j, col):
            load(c, 0, slot(c, 8), w[8 * j * P:(8 * j + 8) * P, bass.ds(col, P)].rearrange("(k p) n -> p k n", p=P))

        def out_projection(ph, w, kmap):
            n = len(kmap)
            with sp.Fori(0, NCB // 2) as i:
                for u in range(2):
                    for j in range(n):
                        load_n(ph["c"] + u * n + j, i * (2 * n), w, kmap[j], i * (2 * NW) + u * NW)

        def feed_forward(layer, ph, pd):
            wg, wu, wd = io["ffn_w_gate"][layer], io["ffn_w_up"][layer], io["ffn_w_down"][layer]
            with sp.Fori(0, FI) as i:
                for j in range(8):
                    load_t(ph["c"] + j, i * 8, wg if j < 4 else wu, j % 4, i * TW)
            out_projection(pd, wd, list(range(FF // P // 2)))

        sp.dma_start(cst[:, 0:P], io["consts"][:, 0:P]).then_inc(s_ident_loaded, 16)
        rows = 0
        for nm, n in (("mix_pre_g", 2 * KT), ("ffn_pre_g", 2 * KT), ("pool_scale", 8), ("gdn_norm_w", 1)):
            a = io[nm]
            sp.dma_start(vrow[rows:rows + n, :],
                         a if n == 1 else a.rearrange("a (k p) -> (a k) p", p=P)).then_inc(s_vrow_loaded, 16)
            rows += n
        for b in range(NCB):
            sp.dma_start(x[:, :, b * NW:(b + 1) * NW],
                         io["x"][0, :, b * NW:(b + 1) * NW].rearrange("(t p) d -> p t d", p=P)).then_inc(s_x_loaded[b], 16)
        for c, (n, j) in enumerate(chunks0):
            kind, _, col, _ = blocks0[n]
            if kind == "kw":
                load_w128(c, w_in0, j, col)
            else:
                load_t(c, 0, w_in0, j, col)
        out_projection(PH_OUT0, io["even_w_o"][0], kmap0)
        feed_forward(0, PH_FF0, PH_DN0)
        for j in range(2):
            load_w128(PH_BA["c"] + j, w_in1, j, ODD_IN - P)
        with sp.Fori(0, NG) as g:
            for b in range(GSLOT // 4):
                col = (g * (GB_STEP[b] // P) * P + GB_COL[b]) if GB_COL[b] == 0 else g * GB_STEP[b] + GB_COL[b]
                for j in range(4):
                    load_t(PH_IN1["c"] + 4 * b + j, g * GSLOT, w_in1, j, col)
        out_projection(PH_OUT1, io["odd_w_o"][0], list(range(NVH // 2)))
        feed_forward(1, PH_FF1, PH_DN1)
        for b in range(NCB):
            sp.wait_ge(s_x_updated, 8 * 3 + NT * (b + 1))
            sp.dma_start(io["out"][0, :, b * NW:(b + 1) * NW].rearrange("(t p) d -> p t d", p=P),
                         x[:, :, b * NW:(b + 1) * NW]).then_inc(s_out_stored, 16)
        sp.wait_ge(s_out_stored, 16 * NCB)

    @block.gpsimd
    def _(pool):
        pool.dma_start(cst[:, P:K_END], io["consts"][:, P:K_END]).then_inc(s_cst_loaded, 16)
        pool.dma_start(onehot[:, :], io["onehot"]).then_inc(s_relb_loaded, 16)
        pool.dma_start(relb[:, :], io["rel_bias"]).then_inc(s_relb_loaded, 16)
        pool.memset(mhalf[:, :], -0.5).then_inc(s_mhalf_set, 1)
        pool.wait_ge(s_mhalf_set, 1)

        def inverse_root(n):
            pool.wait_ge(s_meansq_ready, n + 1)
            pool.tensor_tensor(rstd[:, n % 2, :], meansq[:, n % 2, :], mhalf[:, :], ALU.pow).then_inc(s_rstd_ready, 1)

        def load_gain(n, dst, src, free_sem, free_val):
            pool.wait_ge(free_sem, free_val)
            pool.dma_start(dst[:, :], src.partition_broadcast(P)).then_inc(s_gain_loaded, 16)

        inverse_root(0)
        pool.wait_ge(s_block_evacuated, 1)
        pool.dma_start(kid[DIH:2 * DIH, :], kiw[0:DIH, :]).then_inc(s_ki_copied, 16)
        pool.wait_ge(s_bias_row, NH)
        pool.dma_start(seg_dram, bseg[:, :, :].rearrange("p h s -> p (h s)")).then_inc(s_bias_rows_stored, 16)
        pool.wait_ge(s_bias_rows_stored, 16)
        for t in range(NT):
            w = P * (t + 1)
            src = bass.AP(seg_dram.tensor, S - 1 - P * t, [[NH * SEG - 1, P], [SEG, NH], [1, w]])
            pool.dma_start(bm[:, :, t * P:t * P + w], src).then_inc(s_bias_read, 16)
        pool.dma_start(poolw[:, :, :, :], io["pool_w"][0].rearrange("g (c p) d -> p g c d", p=P)).then_inc(s_poolw_loaded, 16)
        pool.memset(xpad[:, :, 0:16], 0.0).then_inc(s_pads_zeroed, 1)
        pool.memset(wina[:, :, 0:16], 0.0).then_inc(s_pads_zeroed, 1)
        pool.memset(winb[:, :, 0:16], 0.0).then_inc(s_pads_zeroed, 1)
        pool.wait_ge(s_score_added, NIH * NT)
        for t in range(NT):
            w = P * (t + 1)
            v = score[:, t * P:t * P + w]
            pool.affine_select(out=v, in_=v, compare_op=ALU.is_ge, fill=NEG, base=t * P,
                               pattern=[[-1, w]], channel_multiplier=1).then_inc(s_score_masked, 1)
        pool.wait_ge(s_selection, 1)
        for t in range(NT):
            w = P * (t + 1)
            v = score[:, t * P:t * P + w]
            pool.affine_select(out=v, in_=v, compare_op=ALU.is_ge, fill=NEG, base=t * P,
                               pattern=[[-1, w]], channel_multiplier=1).then_inc(s_selection_masked, 1)
        pool.wait_ge(s_selection_masked, 2)
        pool.wait_ge(s_bias_read, 32)
        for h in range(NH):
            pool.tensor_tensor(bm[:, h, :], bm[:, h, :], score[:, :], ALU.add).then_inc(s_bias_masked, 1)
        load_gain(0, gain, io["mix_post_g"][0], s_chunk_used, PH_OUT0["c"])
        inverse_root(1)
        inverse_root(2)
        load_gain(1, gain, io["ffn_post_g"][0], s_chunk_used, PH_DN0["c"])
        inverse_root(3)
        inverse_root(4)
        pool.dma_start(cwrow[:, :, :], io["conv_w"][0].rearrange("k (t p) -> (k t) p", p=P)
                       .rearrange("(a r) p -> r a p", a=2)).then_inc(s_cw_loaded, 16)
        pool.dma_start(avec[:, 0, :], io["dt_bias"][0].partition_broadcast(P)).then_inc(s_avec_loaded, 16)
        pool.dma_start(avec[:, 1, :], io["a_log"][0].partition_broadcast(P)).then_inc(s_avec_loaded, 16)
        pool.memset(cpad[:, :, 0:3], 0.0).then_inc(s_cpad_zeroed, 1)
        pool.memset(xi[:, :, :, :].rearrange("p a b c -> p (a b c)"), 0.0).then_inc(s_cpad_zeroed, 1)

        def masks(c, g):
            v, w = at[:, c, :, :], intra[:, c, :, :]
            pool.wait_ge(s_a_raw, g * 2 + (c + 1))
            pool.affine_select(out=v, in_=v, compare_op=ALU.is_ge, fill=0.0, base=-1,
                               pattern=[[0, 4], [1, P]], channel_multiplier=-1).then_inc(s_a_strict, 1)
            pool.wait_ge(s_a_strict, g * 2 + (c + 1))
            pool.affine_select(out=v, in_=v, compare_op=ALU.not_equal, fill=1.0, base=0,
                               pattern=[[0, 4], [1, P]], channel_multiplier=-1).then_inc(s_a_ready, 1)
            pool.wait_ge(s_intra_raw, g * 2 + (c + 1))
            pool.affine_select(out=w, in_=w, compare_op=ALU.is_ge, fill=0.0, base=0,
                               pattern=[[0, 4], [1, P]], channel_multiplier=-1).then_inc(s_intra_ready, 1)

        def identity_part(g):
            if g > 0:
                pool.wait_ge(s_o_norm_sums, g)
            half = P // 2
            pool.tensor_copy(wy[:, :, :, half:P].rearrange("p a b c -> p (a b) c"),
                             ident[:, half:P].unsqueeze(1).broadcast_to([P, 8, half])).then_inc(s_w_identity_part, 1)

        for g in range(NG):
            for c in range(2):
                masks(c, g)
            identity_part(g)
        load_gain(2, gain_b, io["mix_post_g"][1], s_v_turned, 2 * NG)
        inverse_root(5)
        inverse_root(6)
        load_gain(3, gain, io["ffn_post_g"][1], s_chunk_used, PH_DN1["c"])
        inverse_root(7)

    @block.tensor
    def _(pe):
        def begin_block(b, d):
            if b >= 2:
                pe.wait_ge(s_block_evacuated, d + (b - 1))

        def chunk_t(c, dc, b, j, kts=4, tiles=2, hn_ready=None):
            pe.wait_ge(s_lo_made, dc + (c + 1))
            if hn_ready is not None:
                pe.wait_ge(s_hn_lo, hn_ready)
            sl = c % RING
            w = tiles * P
            for f in range(tiles):
                bank = 2 * (b % 2) + f
                for kk in range(kts):
                    kt = kts * j + kk
                    at_ = slice(kk * w + f * P, kk * w + f * P + P)
                    if kt == 0:
                        nc.tensor.matmul(dn[:, bank, :], whi[:, sl, at_], hn[:, kt, :], start=True, stop=False)
                    mm = nc.tensor.matmul(dn[:, bank, 0:S], wlo[:, sl, at_], hn[:, kt, 0:S], start=False, stop=False)
                    if kt > 0:
                        mm = nc.tensor.matmul(dn[:, bank, :], whi[:, sl, at_], hn[:, kt, :], start=False,
                                              stop=kt == KT - 1)
            mm.then_inc(s_chunk_used, 1)

        def chunk_n(c, dc, b, first, last, lhs, width):
            pe.wait_ge(s_lo_made, dc + (c + 1))
            sl = c % RING
            for t in range(NT):
                bank = 2 * (b % 2) + t
                for kk, (hi, lo) in enumerate(lhs):
                    tok = slice(t * P, (t + 1) * P)
                    ws = slice(kk * width, (kk + 1) * width)
                    o = dn[:, bank, 0:width]
                    nc.tensor.matmul(o, hi(tok), whi[:, sl, ws], start=first and kk == 0, stop=False)
                    nc.tensor.matmul(o, hi(tok), wlo[:, sl, ws], start=False, stop=False)
                    mm = nc.tensor.matmul(o, lo(tok), whi[:, sl, ws], start=False,
                                          stop=last and kk == len(lhs) - 1)
            mm.then_inc(s_chunk_used, 1)

        def pair(t, kt, lo_at=S):
            return (lambda k: t[:, kt, k]), (lambda k: t[:, kt, lo_at + k.start:lo_at + k.stop])

        def turn(n, kg):
            pe.wait_ge(s_x_scaled_act, 4 * n + kg + 1)
            pe.wait_ge(s_x_scaled_dve, 4 * n + kg + 1)
            if kg >= 2:
                pe.wait_ge(s_hn_lo, 16 * n + 4 * (kg - 1))
            for q in range(4):
                for t in range(NT):
                    at_ = ((kg % 2) * NT + t) * 512 + q * P
                    mm = nc.tensor.transpose(mi[:, 2 * (kg % 2) + q // 2, (q % 2) * S + t * P:(q % 2) * S + (t + 1) * P],
                                             scr[:, at_:at_ + P], ident)
            mm.then_inc(s_x_turned, 1)

        def idle_products(k, out=mi[:, BT, 0:P]):
            for _ in range(k):
                nc.tensor.matmul(out, ident, ident, start=True, stop=True)

        def keep_warm(n):
            if n == 0:
                pe.wait_ge(s_ident_loaded, 16)
                for k in range(1, 9, 2):
                    pe.wait_ge(s_x_squared, k)
                    idle_products(5)
                pe.wait_ge(s_vec_ready, 1)
            else:
                idle_products(14)
                pe.wait_ge(s_rstd_ready, 2 * n)
                idle_products(17)
                pe.wait_ge(s_x_updated, 8 * (n - 1) + 6)
                idle_products(18)

        def turn_before(n, j, chunks, b):
            other = dn[:, 2 * ((b + 1) % 2), 0:P]
            if j == 0:
                keep_warm(n)
                turn(n, 0)
                turn(n, 1)
                idle_products(8, other)
                if chunks == 2:
                    turn(n, 2)
            elif chunks == 2:
                turn(n, 3)
                idle_products(12, other)
            elif j < 3:
                turn(n, j + 1)

        def out_chunk(ph, i, u, j, kmap, lhs_of, ready):
            n = len(kmap)
            if j == 0:
                begin_block(ph["b"] + u, i * 2)
            ready(j)
            kt = 2 * kmap[j]
            chunk_n(ph["c"] + u * n + j, i * (2 * n), ph["b"] + u, j == 0, j == n - 1, [lhs_of(kt), lhs_of(kt + 1)], NW)

        def out_projection(ph, kmap, lhs_of, ready, done=0):
            def blocks(i, done):
                for u in range(2):
                    for j in range(0 if u else done, len(kmap)):
                        out_chunk(ph, i, u, j, kmap, lhs_of, ready)
            if done:
                blocks(0, done)
            with pe.Fori(1 if done else 0, NCB // 2) as i:
                blocks(i, 0)

        def feed_forward(n, ph, pd):
            def gate_and_up(i, first=False):
                for j in range(8):
                    if j % 4 == 0:
                        begin_block(ph["b"] + j // 4, i * 2)
                    if first and j < 4:
                        turn_before(n, j, 4, ph["b"])
                    chunk_t(ph["c"] + j, i * 8, ph["b"] + j // 4, j % 4, hn_ready=16 * n + 4 * (j % 4 + 1))

            gate_and_up(0, True)
            with pe.Fori(1, FI) as i:
                gate_and_up(i)
            layer = n // 2
            out_projection(pd, list(range(FF // P // 2)), lambda kt: pair(hid, kt),
                           lambda j: pe.wait_ge(s_ff_lo, FI * layer + j + 1))

        pe.wait_ge(s_ident_loaded, 16)
        pe.wait_ge(s_vrow_loaded, 64)
        R = 4 * KT + 9
        nc.tensor.transpose(mi[:, BX, 0:R], vrow[:, :], ident[0:R, 0:R]).then_inc(s_vec_turned, 1)

        def bias_row(h):
            if h == 0:
                pe.wait_ge(s_relb_loaded, 32)
                pe.wait_ge(s_hn_lo, 16)
            if h >= 2:
                pe.wait_ge(s_bias_row, h - 1)
            nc.tensor.matmul(mi[:, h % 2, 0:SEG], relb[:, h:h + 1].broadcast_to([NB, P]), onehot[:, :],
                             start=True, stop=True).then_inc(s_bias_row_psum, 1)

        def turn_index_weights():
            pe.wait_ge(s_block_evacuated, 1)
            pe.wait_ge(s_hn_lo, 16)
            for t in range(NT):
                mm = nc.tensor.transpose(mi[:, BX, t * P:(t + 1) * P], kiw[:, t * P:(t + 1) * P], ident)
            mm.then_inc(s_wi_turned, 1)

        def dots(ih):
            lo = DIH * (ih % 2)
            src = kiw if ih % 2 == 0 else kid
            pe.wait_ge(s_block_evacuated, 2 + ih // 4)
            if ih == 1:
                pe.wait_ge(s_ki_copied, 16)
            if ih == 0:
                pe.wait_ge(s_bias_row, NH)
            if ih >= 2:
                pe.wait_ge(s_relu_dots, ih - 1)
            for t in range(NT):
                w = P * (t + 1)
                mm = nc.tensor.matmul(mi[:, ih % 2, t * P:t * P + w],
                                      qiT[lo:lo + DIH, ih // 4 % 2, ih % 4 // 2, t * P:(t + 1) * P],
                                      src[lo:lo + DIH, 0:w], start=t == 0, stop=True, skip_group_check=True)
            mm.then_inc(s_dots, 1)

        def logits(h):
            pe.wait_ge(s_block_evacuated, end0.index(end0[5 + 3 * (h // 2) + 2]) + 1)
            if h >= 1:
                pe.wait_ge(s_logits_biased, h)
            else:
                pe.wait_ge(s_relu_dots, NIH)
            for t in range(NT):
                w = P * (t + 1)
                mm = nc.tensor.matmul(mi[:, 0, t * P:t * P + w], kqT[:, 1, h % 2, t * P:(t + 1) * P],
                                      kqT[:, 0, h % 2, 0:w], start=t == 0, stop=True, skip_group_check=True)
            mm.then_inc(s_logits, 1)

        def turn_probs(h):
            pe.wait_ge(s_probs_scaled, NT * (h + 1))
            if h >= 1:
                pe.wait_ge(s_probsT, h)
            for n_, at_ in enumerate((0, P, 2 * P)):
                mm = nc.tensor.transpose(mi[:, 1, n_ * P:(n_ + 1) * P], prob[:, h % 2, at_:at_ + P], ident)
            mm.then_inc(s_probs_turned, 1)

        def attend(h):
            pe.wait_ge(s_probsT, h + 1)
            if h >= 1:
                pe.wait_ge(s_attn_lo, h)
            v = vtm[:, h // 2 % 2, :, (h % 2) * DH:(h % 2 + 1) * DH]
            nc.tensor.matmul(mi[:, 2, 0:P], v[:, 0, :], pT[:, 0:P], start=True, stop=True)
            nc.tensor.matmul(mi[:, 2, P:S], v[:, 0, :], pT[:, P:S], start=True, stop=False)
            nc.tensor.matmul(mi[:, 2, P:S], v[:, 1, :], pT[:, S:S + P], start=False, stop=True).then_inc(s_attn_out, 1)

        def mix_pool(k):
            gi = xp_order[k]
            pe.wait_ge(s_pooled, 2 * (k + 1))
            if k == 0:
                pe.wait_ge(s_poolw_loaded, 16)
            else:
                pe.wait_ge(s_pool_lo, k)
            for dt in range(2):
                for ct in range(2):
                    mm = nc.tensor.matmul(mi[:, 3, dt * S:(dt + 1) * S], poolw[:, gi, ct, dt * P:(dt + 1) * P],
                                          wina[:, ct, 16:16 + S], start=ct == 0, stop=ct == 1)
            mm.then_inc(s_pool_mixed, 1)

        def mix_ready(j):
            if j < NH // 2:
                pe.wait_ge(s_attn_lo, 2 * (j + 1))
            else:
                pe.wait_ge(s_pool_lo, j - NH // 2 + 1)

        out0 = (kmap0, lambda kt: pair(mix, kt), mix_ready)
        for s, (n, j) in enumerate(chunks0 + [(None, None)] * OVER0):
            if n is None:
                out_chunk(PH_OUT0, 0, 0, s - len(chunks0), *out0)
            else:
                kind = blocks0[n][0]
                if j == 0:
                    begin_block(n, 0)
                if kind == "kw":
                    turn_before(0, j, 2, n)
                    chunk_t(s, 0, n, j, kts=8, tiles=1, hn_ready=8 * (j + 1))
                elif kind == "v":
                    chunk_n(s, 0, n, j == 0, j == 3, [pair(hn, 4 * j + kk) for kk in range(4)], TW)
                else:
                    chunk_t(s, 0, n, j)
            if 2 <= s < 2 + NH // 2:
                bias_row(2 * (s - 2))
                bias_row(2 * (s - 2) + 1)
            if s == 3:
                turn_index_weights()
            if 7 <= s < 7 + NIH:
                dots(s - 7)
            if s in head_at:
                logits(head_at[s])
            if s - 2 in head_at:
                turn_probs(head_at[s - 2])
            if s - 3 in head_at:
                attend(head_at[s - 3])
            for k in range(4):
                if s == end0[17 + k] + 2:
                    mix_pool(k)

        out_projection(PH_OUT0, *out0, done=OVER0)
        feed_forward(1, PH_FF0, PH_DN0)
        begin_block(PH_BA["b"], 0)
        for j in range(2):
            turn_before(2, j, 2, PH_BA["b"])
            chunk_t(PH_BA["c"] + j, 0, PH_BA["b"], j, kts=8, tiles=1, hn_ready=32 + 8 * (j + 1))
        pe.wait_ge(s_cw_loaded, 16)
        for a in range(2):
            mm = nc.tensor.transpose(mi[:, BX, a * P:(a + 1) * P], cwrow[:, a, :], ident)
        mm.then_inc(s_cw_turned, 1)
        pe.wait_ge(s_block_evacuated, PH_IN1["b"])
        for t in range(NT):
            mm = nc.tensor.transpose(mi[:, BY, t * P:(t + 1) * P], conv_y[:, 0, t * P:(t + 1) * P], ident)
        mm.then_inc(s_ba_turned, 1)

        def log_decay_sums():
            pe.wait_ge(s_g_ready, 1)
            pe.wait_ge(s_cst_loaded, 16)
            for c in range(2):
                mm = nc.tensor.matmul(mi[:, BX, 256 + c * NVH:256 + (c + 1) * NVH], triu, sc4[:, 0, c, :],
                                      start=True, stop=True)
            mm.then_inc(s_gc_psum, 1)

        def decay_rows(g, c):
            pe.wait_ge(s_gc_taken, g * 1 + 1)
            if c == 0 and looped(g):
                pe.wait_ge(s_xT_evacuated, g * 12)
            if c == 1:
                pe.wait_ge(s_decay_clamped, g * 2 + 1)
            for u in range(4):
                mm = nc.tensor.transpose(mi[:, BM, u * P:(u + 1) * P], gch[:, c, u:u + 1].broadcast_to([P, P]), ident)
            mm.then_inc(s_gc_rows, 1)

        def norm_sums(g):
            pe.wait_ge(s_kq_squared, g * 1 + 1)
            if looped(g):
                pe.wait_ge(s_vnew1, g * 1)
            for n in range(8):
                mm = nc.tensor.matmul(mi[:, BY, n:n + 1], sqkq[:, n // 4, (n % 4) * P:(n % 4 + 1) * P],
                                      ones[:, 0:1], start=True, stop=True, skip_group_check=True)
            mm.then_inc(s_norm_sums, 1)

        def norm_rows(g):
            pe.wait_ge(s_norm_inverses, g * 1 + 1)
            pe.wait_ge(s_decay_clamped, g * 2 + 2)
            pe.wait_ge(s_exp_gc_row, g * 1 + 1)
            for n in range(8):
                mm = nc.tensor.transpose(mi[:, (BM, BY)[n // 4], (n % 4) * P:(n % 4 + 1) * P],
                                         nrm[:, n:n + 1].broadcast_to([P, P]), ident)
                if n % 4 == 3:
                    mm.then_inc(s_norm_rows, 1)

        def o_norm_sums(g):
            pe.wait_ge(s_o_squared, g * 2 + 2)
            for n in range(8):
                mm = nc.tensor.matmul(mi[:, BY, 8 + n:9 + n], osq[:, n // 4, (n % 4) * P:(n % 4 + 1) * P],
                                      ones[:, 0:1], start=True, stop=True, skip_group_check=True)
            mm.then_inc(s_o_norm_sums, 1)

        def o_norm_rows(g, k):
            pe.wait_ge(s_o_normed, g * 2 + (k + 1))
            for n in range(4):
                mm = nc.tensor.transpose(mi[:, (BX, BT)[k], n * P:(n + 1) * P],
                                         nrm[:, 8 + 4 * k + n:9 + 4 * k + n].broadcast_to([P, P]), ident)
            mm.then_inc(s_o_norm_rows, 1)

        def products(g, c):
            pe.wait_ge(s_kq_normed, g * 2 + 2)
            if c == 1:
                pe.wait_ge(s_a_raw, g * 2 + 1)
                pe.wait_ge(s_intra_raw, g * 2 + 1)
            tok = slice(c * P, (c + 1) * P)
            for kp in range(2):
                mm = nc.tensor.matmul(mi[:, BM, kp * 256:(kp + 1) * 256].rearrange("p (a b) -> p a b", a=2),
                                      kq[:, 0, kp, tok], kq[:, :, kp, tok], start=True, stop=True)
            mm.then_inc(s_kk_qk, 1)

        def turn_v(g, half):
            pe.wait_ge(s_silu_done, g * 4 + (3 + half))
            if half == 0:
                pe.wait_ge(s_a_raw, g * 2 + 2)
                pe.wait_ge(s_intra_raw, g * 2 + 2)
            else:
                pe.wait_ge(s_x1, g * 2 + 2)
            for c in range(2):
                for u in range(2):
                    mm = nc.tensor.transpose(mi[:, BM, (2 * c + u) * P:(2 * c + u + 1) * P],
                                             vfm[:, u, c * P:(c + 1) * P], ident)
            mm.then_inc(s_v_turned, 1)

        def turn_x1(g, b):
            pe.wait_ge(s_x1T, g * 2 + (b + 1))
            if b == 0:
                pe.wait_ge(s_v_tok, g * 2 + 1)
            else:
                pe.wait_ge(s_x1, g * 2 + 1)
            for u in range(4):
                mm = nc.tensor.transpose(mi[:, BM, u * P:(u + 1) * P], xt[:, b, u, :], ident)
            mm.then_inc(s_x1_turned, 1)

        def turn_k(g):
            pe.wait_ge(s_v_tok, g * 2 + 2)
            for kp in range(2):
                mm = nc.tensor.transpose(mi[:, BM, kp * P:(kp + 1) * P], kq[:, 0, kp, 0:P], ident)
            mm.then_inc(s_k_turned, 1)

        def times_a(g, b, lev):
            n = 2 * (lev - 1) + b
            if lev == 1:
                pe.wait_ge(s_x1, g * 2 + (b + 1))
                pe.wait_ge(s_a_paired, g * 2 + (b + 1))
            else:
                pe.wait_ge(s_x_evacuated, g * 12 + (2 * (lev - 2) + b + 1))
            if n >= 1:
                pe.wait_ge(s_w_ready, g * 12 + n)
            half = P // 2
            if lev < NLEV:
                for p in range(2):
                    o = mi[:, BY, p * P:(p + 1) * P].rearrange("p (g s) -> p g s", s=2 ** lev)
                    xe = xi[:, b, p, :].rearrange("p (g t s) -> p g t s", t=2, s=2 ** lev)[:, :, 0, :]
                    mm = nc.tensor.matmul(o, atp[:, b, p, :], xe, start=True, stop=True)
            else:
                for u in range(4):
                    mm = nc.tensor.matmul(mi[:, BY, u * half:(u + 1) * half], at[:, b, u, :],
                                          xi[:, b, u // 2, (u % 2) * half:(u % 2 + 1) * half], start=True, stop=True)
            mm.then_inc(s_ax_psum, 1)

        def next_x(g, b, lev):
            n = 2 * (lev - 1) + b
            pe.wait_ge(s_w_ready, g * 12 + (n + 1))
            if n >= 1:
                pe.wait_ge(s_x_evacuated, g * 12 + n)
            pe.wait_ge(s_xT_evacuated, g * 12 + (n + 1))
            if lev == NLEV:
                pe.wait_ge(s_w_identity_part, g * 1 + 1)
            half = P // 2
            if lev < NLEV:
                for p in range(2):
                    mm = nc.tensor.matmul(mi[:, BX, p * P:(p + 1) * P].rearrange("p (h x) -> p h x", h=2),
                                          xt[:, b, p, :], wy[:, b, 2 * p:2 * p + 2, 0:half], start=True, stop=True)
            else:
                for u in range(4):
                    mm = nc.tensor.matmul(mi[:, BX, u * half:(u + 1) * half], wy[:, b, u, :], xt[:, b, u, half:P],
                                          start=True, stop=True)
            mm.then_inc(s_x_psum, 1)

        def turn_x(g, b, lev):
            n = 2 * lev + b
            if lev == 0:
                pe.wait_ge(s_x1, g * 2 + (b + 1))
                if b == 0 and looped(g):
                    pe.wait_ge(s_o_gated, g * 2)
            else:
                pe.wait_ge(s_x_evacuated, g * 12 + (2 * (lev - 1) + b + 1))
            if n >= 1:
                pe.wait_ge(s_xT_evacuated, g * 12 + n)
            half = P // 2
            for p in range(2):
                for q in range(2):
                    mm = nc.tensor.transpose(mi[:, BT, (2 * p + q) * P:(2 * p + q + 1) * P],
                                             xi[:, b, p, q * P:(q + 1) * P], ident)
                if lev == NLEV - 1:
                    if b == 0 and p == 0:
                        pe.wait_ge(s_k_tok, g * 1 + 1)
                    mm = nc.tensor.transpose(mi[:, BM, p * P:(p + 1) * P], xi[:, b, p, half:half + P], ident)
            mm.then_inc(s_x_turned_level, 1)

        def solve(g, c):
            pe.wait_ge(s_x_evacuated, g * 12 + (11 + c))
            if c == 1:
                pe.wait_ge(s_rhs1, g * 1 + 1)
            for u in range(4):
                mm = nc.tensor.matmul(mi[:, BY, u * P:(u + 1) * P], xt[:, c, u, :], vtok[:, c, u, :],
                                      start=True, stop=True)
            mm.then_inc((s_y0, s_y1)[c], 1)

        def state(g):
            pe.wait_ge(s_vnew0, g * 1 + 1)
            for u in range(4):
                mm = nc.tensor.matmul(mi[:, BY, u * P:(u + 1) * P], kdec[:, u, :], vn[:, 0, u, :],
                                      start=True, stop=True)
            mm.then_inc(s_state_psum, 1)

        def keys_times_state(g):
            pe.wait_ge(s_state, g * 1 + 1)
            for kp in range(2):
                mm = nc.tensor.matmul(mi[:, BY, kp * 256:(kp + 1) * 256], kq[:, 0, kp, P:S],
                                      st[:, 2 * kp:2 * kp + 2, :].rearrange("p a b -> p (a b)"),
                                      start=True, stop=True)
            mm.then_inc(s_k_state, 1)

        def outputs(g, half):
            pe.wait_ge(s_vnew1, g * 1 + 1)
            pe.wait_ge(s_intra_ready, g * 2 + 2)
            for e in range(2):
                u = 2 * half + e
                o = mi[:, (BX, BT)[half], e * S:(e + 1) * S]
                nc.tensor.matmul(o[:, 0:P], vn[:, 0, u, :], intra[:, 0, u, :], start=True, stop=True)
                nc.tensor.matmul(o[:, P:S], vn[:, 1, u, :], intra[:, 1, u, :], start=True, stop=False)
                mm = nc.tensor.matmul(o[:, P:S], st[:, u, :], qd[:, u, :], start=False, stop=True)
            mm.then_inc(s_o_psum, 1)

        def slot(n, g, cur_on, prev_on):
            if prev_on:
                h = g - 1
                m = n + GSLOT
                for b in range(2):
                    lev, odd = divmod(m - 20 - b, 2)
                    if odd == 1 and 1 <= lev + 1 <= NLEV:
                        next_x(h, b, lev + 1)
                for b in range(2):
                    lev, odd = divmod(m - 20 - b, 2)
                    if odd == 0 and 1 <= lev + 1 <= NLEV:
                        times_a(h, b, lev + 1)
                        turn_x(h, b, lev)
                if m == 32:
                    solve(h, 0)
                if m == 33:
                    state(h)
                if m == 34:
                    keys_times_state(h)
                if m == 35:
                    solve(h, 1)
                if m == 36:
                    outputs(h, 0)
                    outputs(h, 1)
            if cur_on:
                if n in (9, 10):
                    decay_rows(g, n - 9)
                if n == (12 if prev_on else 13):
                    norm_sums(g)
            if prev_on and n == 13:
                o_norm_sums(g - 1)
            if cur_on and n == 15:
                norm_rows(g)
            if prev_on and n == 16:
                if not cur_on:
                    pe.wait_ge(s_norm_inverses, NG + 1)
                o_norm_rows(g - 1, 0)
                o_norm_rows(g - 1, 1)
            if cur_on:
                if n in (16, 17):
                    products(g, n - 16)
                if n == 18:
                    turn_v(g, 0)
                if n == 19:
                    turn_x1(g, 0)
                if n == 20:
                    turn_x1(g, 1)
                for b in range(2):
                    lev, odd = divmod(n - 20 - b, 2)
                    if odd == 1 and lev >= 0:
                        next_x(g, b, lev + 1)
                for b in range(2):
                    lev, odd = divmod(n - 20 - b, 2)
                    if odd == 0 and lev >= 0:
                        turn_x(g, b, lev)
                        times_a(g, b, lev + 1)
                if n == 21:
                    turn_v(g, 1)
                if n == 22:
                    turn_k(g)

        def group(g, d, prev_on):
            for n in range(GSLOT):
                b = n // 4
                if n % 4 == 0:
                    begin_block(PH_IN1["b"] + b, d * 6)
                chunk_t(PH_IN1["c"] + n, d * GSLOT, PH_IN1["b"] + b, n % 4)
                if n == 3 and not prev_on:
                    log_decay_sums()
                slot(n, g, True, prev_on)

        group(0, 0, False)
        with pe.Fori(1, NG) as g:
            group(g, g, True)
        out1 = (list(range(NVH // 2)), lambda kt: ((lambda k: ohi[:, kt, k]), (lambda k: olo[:, kt, k])),
                lambda j: pe.wait_ge(s_o_lo, j + 1))
        for n in range(17 + 1):
            if n < NFREE:
                out_chunk(PH_OUT1, 0, 0, n, *out1)
            slot(n, NG, False, True)
            if n in (13, 16):
                pe.wait_ge(s_block_evacuated, PH_OUT1["b"])
                idle_products(7, dn[:, 2 * ((PH_OUT1["b"] + 1) % 2), 0:P])
        out_projection(PH_OUT1, *out1, done=NFREE)
        feed_forward(3, PH_FF1, PH_DN1)

    @block.scalar
    def _(act):
        def split_hi(c, d):
            if c >= CHUNKS and not looped(d):
                return
            act.wait_ge(s_raw_loaded[c % RING], d * (16 // RING) + 16 * (c // RING + 1))
            if c >= RING or looped(d):
                act.wait_ge(s_chunk_used, d + (c - RING + 1))
            nc.scalar.activation(whi[:, c % RING, :], raw[:, c % RING, :], ACT.Copy).then_inc(s_hi_made, 1)

        def copy_half(c_last, dc, b, db, tiles=2):
            act.wait_ge(s_chunk_used, dc + (c_last + 1))
            if b >= 1:
                act.wait_ge(s_block_evacuated, db + b)
            b2 = 2 * (b % 2)
            nc.scalar.activation(halfa[:, 0:tiles, :], dn[:, b2:b2 + tiles, 0:S], ACT.Copy).then_inc(s_half_copied, 1)

        def square_x(n):
            for b in range(NCB):
                for t in range(NT):
                    if n == 0:
                        act.wait_ge(s_x_loaded[b], 16)
                    else:
                        act.wait_ge(s_x_updated, 8 * (n - 1) + NT * b + t + 1)
                    seq = 8 * n + NT * b + t
                    if n >= 1:
                        act.wait_ge(s_out_squared, 8 * n)
                    if seq >= 1:
                        act.wait_ge(s_x_squared, seq)
                    nc.scalar.activation(junk[:, :], x[:, t, b * NW:(b + 1) * NW], ACT.Square,
                                         accum_out=ssx[:, t, b:b + 1]).then_inc(s_x_squared, 1)

        def norm(n):
            square_x(n)
            if n == 0:
                act.wait_ge(s_vec_turned, 1)
                nc.scalar.activation(vecT[:, :], mi[:, BX, 0:4 * KT + 9], ACT.Copy).then_inc(s_vec_ready, 1)
            g0 = n // 2 * KT + (2 * KT if n % 2 else 0)
            if n % 2 == 1:
                nc.scalar.activation(warm[:, :], epsc[:, 0:1], ACT.Tanh)
            act.wait_ge(s_rstd_ready, 2 * n + 1)

            def scale(kg):
                if kg >= 2:
                    act.wait_ge(s_x_turned, 4 * n + kg - 1)
                at_ = (kg % 2) * NT * 512
                nc.scalar.activation(scr[:, at_:at_ + 512], x[:, 0, kg * 512:(kg + 1) * 512], ACT.Copy,
                                     scale=rstd[:, 0, 0:1]).then_inc(s_x_scaled_act, 1)

            scale(0)
            scale(1)
            if n == 0:
                split_hi(0, 0)
                act.wait_ge(s_vec_ready, 1)
            for kg in range(4):
                act.wait_ge(s_x_turned, 4 * n + kg + 1)
                for q in range(4):
                    kt = 4 * kg + q
                    nc.scalar.activation(hn[:, kt, 0:S], mi[:, 2 * (kg % 2) + q // 2, (q % 2) * S:(q % 2 + 1) * S],
                                         ACT.Copy, scale=vecT[:, g0 + kt:g0 + kt + 1]).then_inc(s_hn_hi, 1)
                if kg + 2 < 4:
                    scale(kg + 2)
                if n == 0 and 1 <= kg < LEAD:
                    split_hi(kg, 0)

        def out_projection(ph, n, sq_base, final=False, done=0):
            def body(i, d, done=0):
                for u in range(2):
                    for j in range(0 if u else done, n):
                        c = ph["c"] + u * n + j
                        if not (final and c + LEAD + (d if isinstance(d, int) else 0) >= CHUNKS):
                            split_hi(c + LEAD, d)
                        if j == n - 1:
                            act.wait_ge(s_chunk_used, d + (c + 1))
                            act.wait_ge(s_x_squared, sq_base + 8)
                            for t in range(NT):
                                act.wait_ge(s_out_squared, i * 4 + (sq_base + 2 * u + t))
                                nc.scalar.activation(junk[:, :], dn[:, 2 * ((ph["b"] + u) % 2) + t, :], ACT.Square,
                                                     accum_out=ssm[:, t, i * 2 + u:i * 2 + u + 1] if isinstance(i, int)
                                                     else ssm[:, t, bass.ds(i * 2 + u, 1)]).then_inc(s_out_squared, 1)
            if final:
                for i in range(NCB // 2):
                    body(i, i * 2 * n)
            else:
                if done:
                    body(0, 0, done)
                with act.Fori(1 if done else 0, NCB // 2) as i:
                    body(i, i * (2 * n))

        def feed_forward(layer, ph, pd, final):
            with act.Fori(0, FI) as i:
                for j in range(8):
                    split_hi(ph["c"] + j + LEAD, i * 8)
                    if j == 3:
                        copy_half(ph["c"] + 3, i * 8, ph["b"], i * 2)
                    if j == 4:
                        act.wait_ge(s_block_evacuated, i * 2 + (ph["b"] + 1))
                        nc.scalar.activation(fth, fg, ACT.Tanh, scale=0.5).then_inc(s_ff_tanh, 1)
                    if j == 7:
                        copy_half(ph["c"] + 7, i * 8, ph["b"] + 1, i * 2)
                        act.wait_ge(s_ff_hidden, i + (FI * layer + 1))
                        nc.scalar.activation(hid[:, bass.ds(i * 2, 2), 0:S], fh, ACT.Copy).then_inc(s_ff_hi, 1)
            out_projection(pd, FF // P // 2, 8 * (2 * layer + 1), final)

        norm(0)

        def exps(h):
            act.wait_ge(s_logits_max, NT * (h + 1))
            for t in range(NT):
                w = P * (t + 1)
                v = prob[:, h % 2, t * P:t * P + w]
                nc.scalar.activation(v, v, ACT.Exp, bias=mx[:, h, t:t + 1],
                                     accum_out=psm[:, h, t:t + 1]).then_inc(s_probs, 1)

        for s in range(len(chunks0) + OVER0):
            split_hi(s + LEAD, 0)
            if s in evac_at and blocks0[evac_at[s]][0] != "v":
                n = evac_at[s]
                copy_half(s - 1, 0, n, 0, tiles=1 if n == 0 else 2)
            if 2 <= s < 2 + NH // 2:
                for h in (2 * (s - 2), 2 * (s - 2) + 1):
                    act.wait_ge(s_bias_row_psum, h + 1)
                    nc.scalar.activation(bseg[:, h, :], mi[:, h % 2, 0:SEG], ACT.Copy).then_inc(s_bias_row, 1)
            if 7 <= s < 7 + NIH:
                ih = s - 7
                act.wait_ge(s_dots, ih + 1)
                if ih >= 2:
                    act.wait_ge(s_score_added, NT * (ih - 1))
                nc.scalar.activation(rel[:, ih % 2, :], mi[:, ih % 2, 0:3 * P], ACT.Relu,
                                     scale=DIH ** -0.5).then_inc(s_relu_dots, 1)
            if s - 1 in head_at:
                exps(head_at[s - 1])
            if s - 2 in head_at:
                h = head_at[s - 2]
                act.wait_ge(s_probs_turned, h + 1)
                if h >= 1:
                    act.wait_ge(s_attn_out, h)
                nc.scalar.activation(pT[:, :], mi[:, 1, 0:3 * P], ACT.Copy).then_inc(s_probsT, 1)
            if s - 3 in head_at:
                h = head_at[s - 3]
                act.wait_ge(s_attn_out, h + 1)
                nc.scalar.activation(mix[:, h, 0:S], mi[:, 2, 0:S], ACT.Copy).then_inc(s_attn_hi, 1)
            for k in range(4):
                if s == end0[17 + k] + 2:
                    gi = xp_order[k]
                    act.wait_ge(s_pool_mixed, k + 1)
                    for dt in range(2):
                        col = 4 * KT + 2 * gi + dt
                        nc.scalar.activation(mix[:, NH + 2 * gi + dt, 0:S], mi[:, 3, dt * S:(dt + 1) * S], ACT.Copy,
                                             scale=vecT[:, col:col + 1]).then_inc(s_pool_hi, 1)
        out_projection(PH_OUT0, KT // 2, 0, done=OVER0)
        norm(1)
        feed_forward(0, PH_FF0, PH_DN0, False)
        norm(2)
        split_hi(PH_BA["c"] + LEAD, 0)
        split_hi(PH_BA["c"] + 1 + LEAD, 0)
        act.wait_ge(s_cw_turned, 1)
        nc.scalar.activation(cwT[:, :, :].rearrange("p a b -> p (a b)"), mi[:, BX, 0:256], ACT.Copy,
                             scale=0.5).then_inc(s_cw_ready, 1)
        copy_half(PH_BA["c"] + 1, 0, PH_BA["b"], 0, tiles=1)

        def gates(step):
            if step == 0:
                act.wait_ge(s_a_folded, 1)
                nc.scalar.activation(bat[:, 0, :, :], ba[:, :, 0:NVH], ACT.Exp, scale=-1.0).then_inc(s_ba_exps, 1)
                nc.scalar.activation(bat[:, 2, :, :], bat[:, 2, :, :], ACT.Exp).then_inc(s_ba_exps, 1)
                nc.scalar.activation(avec[:, 1, :], avec[:, 1, :], ACT.Exp).then_inc(s_ba_exps, 1)
            if step == 1:
                act.wait_ge(s_ba_exps, 2)
                nc.scalar.activation(bat[:, 3, :, :], bat[:, 2, :, :], ACT.Ln, bias=1.0).then_inc(s_a_log1p, 1)
            if step == 2:
                act.wait_ge(s_gc_ready, 1)
                nc.scalar.activation(sc4[:, 2, :, :], sc4[:, 1, :, :], ACT.Exp).then_inc(s_gc_exp, 1)

        def evac(g, b):
            copy_half(PH_IN1["c"] + 4 * b + 3, g * GSLOT, PH_IN1["b"] + b, g * 6)

        def tap0(g, b):
            act.wait_ge(s_block_evacuated, g * 6 + (PH_IN1["b"] + b + 1))
            act.wait_ge(s_cwc_ready, g * 1 + 1)
            for f in range(2):
                k = 2 * b + f
                i = nc.scalar.activation(conv_y[:, f, :], cpad[:, f, 3:3 + S], ACT.Copy,
                                         scale=cwc[:, 3, k:k + 1])
            i.then_inc(s_tap0, 1)

        def tanh(g, k):
            if k < 4:
                act.wait_ge(s_taps, g * 24 + 6 * (k + 1))
                nc.scalar.activation(conv_th, conv_y, ACT.Tanh).then_inc(s_conv_tanh, 1)
            else:
                act.wait_ge(s_block_evacuated, g * 6 + (PH_IN1["b"] + k + 1))
                z = zs[:, 2 * (k - 4):2 * (k - 4) + 2, :]
                nc.scalar.activation(conv_th, z, ACT.Tanh, scale=0.5).then_inc(s_conv_tanh, 1)

        def decays(g, c):
            act.wait_ge(s_decay_clamped, g * 2 + (c + 1))
            if c == 1:
                nc.scalar.activation(egc[:, :, :].rearrange("p a b -> p (a b)"), mi[:, BM, :], ACT.Exp).then_inc(s_exp_gc_row, 1)
            nc.scalar.activation(dec[:, c, :, :], dec[:, c, :, :], ACT.Exp).then_inc(s_decay_ready, 1)

        def squares(g):
            act.wait_ge(s_silu_done, g * 4 + 2)
            nc.scalar.activation(sqkq, kqr[:, :, :, :].rearrange("p a b c -> p a (b c)"), ACT.Square).then_inc(s_kq_squared, 1)

        def o_squares(g, k):
            act.wait_ge(s_o_psum, g * 2 + (k + 1))
            nc.scalar.activation(osq[:, k, :], mi[:, (BX, BT)[k], :], ACT.Square).then_inc(s_o_squared, 1)

        def roots(g, kq_on, o_on):
            if kq_on:
                act.wait_ge(s_norm_sums, g * 1 + 1)
            if o_on:
                act.wait_ge(s_o_norm_sums, g * 1)
            if kq_on:
                for k in range(2):
                    i = nc.scalar.activation(nrm[:, 4 * k:4 * k + 4], mi[:, BY, 4 * k:4 * k + 4], ACT.Sqrt,
                                             scale=(1.0, float(DH))[k], bias=epsc[:, k:k + 1])
            if o_on:
                i = nc.scalar.activation(nrm[:, 8:16], mi[:, BY, 8:16], ACT.Sqrt, scale=1.0 / DH, bias=epsc[:, 0:1])
            i.then_inc(s_norm_roots, 1)

        def copy_v(g, half):
            act.wait_ge(s_v_turned, g * 2 + (half + 1))
            nc.scalar.activation(vtok[:, :, 2 * half:2 * half + 2, :],
                                 mi[:, BM, :].rearrange("p (a b c) -> p a b c", a=2, b=2), ACT.Copy).then_inc(s_v_tok, 1)

        def copy_x1(g, b):
            act.wait_ge(s_x1_turned, g * 2 + (b + 1))
            if b == 0 and not looped(g):
                act.wait_ge(s_cpad_zeroed, 2)
            half = P // 2
            src = mi[:, BM, :].rearrange("p (h a x) -> p h a x", h=2, a=2)
            nc.scalar.activation(xi[0:half, b, :, 0:P].rearrange("p h (a x) -> p h a x", a=2), src[0:half, :, :, 0:half],
                                 ACT.Copy)
            for a in range(2):
                i = nc.scalar.activation(xi[half:P, b, :, P + (1 - a) * half:P + (2 - a) * half],
                                         src[half:P, :, a, half:P], ACT.Copy)
            i.then_inc(s_x1, 1)

        def pair_a(g, c):
            half = P // 2
            if c == 0:
                act.wait_ge(s_q_decayed, g * 1 + 1)
            act.wait_ge(s_a_ready, g * 2 + (c + 1))
            src = at[:, c, :, :].rearrange("p (h a) x -> p h a x", h=2)
            nc.scalar.activation(atp[0:half, c, :, :].rearrange("p h (a x) -> p h a x", a=2), src[0:half, :, :, 0:half],
                                 ACT.Copy)
            for a in range(2):
                i = nc.scalar.activation(atp[half:P, c, :, (1 - a) * half:(2 - a) * half], src[half:P, :, a, half:P],
                                         ACT.Copy)
            i.then_inc(s_a_paired, 1)

        def copy_k(g):
            act.wait_ge(s_k_turned, g * 1 + 1)
            nc.scalar.activation(ktok[:, :, :].rearrange("p a b -> p (a b)"), mi[:, BM, 0:256], ACT.Copy).then_inc(s_k_tok, 1)

        def copy_x(g, b, lev):
            act.wait_ge(s_x_psum, g * 12 + (2 * (lev - 1) + b + 1))
            src = mi[:, BX, 0:2 * P]
            if lev < NLEV:
                half = P // 2
                v = src.rearrange("p (h a x) -> p h a x", h=2, a=2)
                for a in range(2):
                    r = slice(a * half, (a + 1) * half)
                    dst = xi[r, b, :, a * P:(a + 1) * P].rearrange("p h (g t s) -> p h g t s", t=2, s=2 ** lev)[:, :, :, 0, :]
                    i = nc.scalar.activation(dst, v[r, :, a, :].rearrange("p h (g s) -> p h g s", s=2 ** lev), ACT.Copy)
                i.then_inc(s_x_evacuated, 1)
            else:
                nc.scalar.activation(xt[:, b, :, P // 2:P], src.rearrange("p (u s) -> p u s", u=4),
                                     ACT.Copy).then_inc(s_x_evacuated, 1)

        def copy_xt(g, b, lev):
            act.wait_ge(s_x_turned_level, g * 12 + (2 * lev + b + 1))
            src = mi[:, BT, :].rearrange("p (h y) -> p h y", h=2)
            if lev < NLEV - 1:
                both = mi[:, BT, :].rearrange("p (h z x) -> p h z x", h=2, x=P // 2)[:, :, 0:4:3, :]
                nc.scalar.activation(xt[:, b, 0:2, :].rearrange("p h (z x) -> p h z x", z=2), both,
                                     ACT.Copy).then_inc(s_xT_evacuated, 1)
                return
            heads = xt[:, b, :, :].rearrange("p (h a) s -> p h a s", h=2)
            half = P // 2
            lo, hi = slice(0, half), slice(half, P)
            nc.scalar.activation(heads[lo, :, 0, lo], src[lo, :, lo], ACT.Copy)
            nc.scalar.activation(heads[hi, :, 0, hi], src[hi, :, P + half:2 * P], ACT.Copy)
            nc.scalar.activation(heads[hi, :, 0, lo], xi[hi, b, :, lo], ACT.Copy)
            nc.scalar.activation(heads[lo, :, 0, hi], xi[lo, b, :, P:P + half], ACT.Copy)
            nc.scalar.activation(heads[:, :, 1, :], mi[:, BM, 0:2 * P].rearrange("p (h x) -> p h x", h=2),
                                 ACT.Copy).then_inc(s_xT_evacuated, 1)

        def slot(n, g, cur_on, prev_on):
            if prev_on:
                h, m = g - 1, n + GSLOT
                for b in range(2):
                    lev, odd = divmod(m - 20 - b, 2)
                    if odd == 1 and 1 <= lev + 1 <= NLEV:
                        copy_x(h, b, lev + 1)
                    if odd == 0 and 1 <= lev < NLEV:
                        copy_xt(h, b, lev)
                if m == 33:
                    act.wait_ge(s_state_psum, h * 1 + 1)
                    nc.scalar.activation(st[:, :, :].rearrange("p a b -> p (a b)"), mi[:, BY, :], ACT.Copy).then_inc(s_state, 1)
                if m == 24:
                    evac(h, 5)
                if m == 25:
                    tanh(h, 5)
            if cur_on:
                if n == 18:
                    copy_v(g, 0)
                if n == 19:
                    copy_x1(g, 0)
                if n == 20:
                    copy_x1(g, 1)
                if n in (19, 20):
                    pair_a(g, n - 19)
                for b in range(2):
                    lev, odd = divmod(n - 20 - b, 2)
                    if odd == 1 and lev >= 0:
                        copy_x(g, b, lev + 1)
                    if odd == 0 and lev >= 0:
                        copy_xt(g, b, lev)
                if n == 21:
                    copy_v(g, 1)
                if n == 22:
                    copy_k(g)
                if n % 4 == 0 and n > 0:
                    evac(g, n // 4 - 1)
                if n in (5, 9, 13, 17):
                    tap0(g, n // 4 - 1)
                if n in (6, 10, 14, 18):
                    tanh(g, n // 4 - 1)
                if n == 21:
                    tanh(g, 4)
                if n in (9, 10):
                    decays(g, n - 9)
                if n == 11:
                    squares(g)
            if prev_on and n == 12:
                o_squares(h, 0)
                o_squares(h, 1)
            if n == 13 and (prev_on or cur_on):
                roots(g, cur_on, prev_on)

        def group(g, d, prev_on):
            for n in range(GSLOT):
                split_hi(PH_IN1["c"] + n + LEAD, d * GSLOT)
                if not prev_on and n in (0, 1):
                    gates(n)
                if not prev_on and n == 4:
                    gates(2)
                slot(n, g, True, prev_on)

        group(0, 0, False)
        with act.Fori(1, NG) as g:
            group(g, g, True)
        def o_hi(j):
            if j == 0:
                act.wait_ge(s_chunk_used, PH_OUT1["c"])
            act.wait_ge(s_o_gated, j + 1)
            nc.scalar.activation(ohi[:, 2 * j:2 * j + 2, :], o32[:, 2 * j:2 * j + 2, :], ACT.Copy).then_inc(s_o_hi, 1)

        o_hi(0)
        o_hi(1)
        for n in range(15 + 1):
            if n < NFREE:
                split_hi(PH_OUT1["c"] + n + LEAD, 0)
                if n + 2 < NFREE:
                    o_hi(n + 2)
            slot(n, NG, False, True)
        o_hi(NFREE)
        o_hi(NFREE + 1)
        out_projection(PH_OUT1, NVH // 2, 16, done=NFREE)
        norm(3)
        feed_forward(1, PH_FF1, PH_DN1, True)

    @block.vector
    def _(v):
        def split_lo(c, d):
            if c >= CHUNKS and not looped(d):
                return
            v.wait_ge(s_hi_made, d + (c + 1))
            nc.vector.tensor_tensor(wlo[:, c % RING, :], raw[:, c % RING, :], whi[:, c % RING, :].bitcast(F32),
                                    ALU.subtract).then_inc(s_lo_made, 1)

        def add_halves(out, b, t, dt, tiles=2):
            v.wait_ge(s_half_copied, dt + (t + 1))
            b2 = 2 * (b % 2)
            nc.vector.tensor_tensor(out, dn[:, b2:b2 + tiles, S:2 * S], halfa[:, 0:tiles, :], ALU.add).then_inc(s_block_evacuated, 1)

        def root_input(n, sums, cond):
            v.wait_ge(*cond)
            if n >= 2:
                v.wait_ge(s_rstd_ready, n - 1)
            nc.vector.tensor_reduce(tot[:, n % 2, :], sums[:, :, :], AX, ALU.add).then_inc(s_squares_summed, 1)
            v.wait_ge(s_squares_summed, n + 1)
            nc.vector.tensor_scalar(meansq[:, n % 2, :], tot[:, n % 2, :], 1.0 / D, EPS, ALU.mult, ALU.add).then_inc(s_meansq_ready, 1)

        def norm(n):
            root_input(2 * n, ssx, (s_x_squared, 8 * (n + 1)))
            if n == 0:
                v.wait_ge(s_vec_ready, 1)
                nc.vector.tensor_scalar(nwh[:, :], vecT[:, 4 * KT + 8:4 * KT + 9], 0.5, None, ALU.mult).then_inc(s_nwh_ready, 1)
            v.wait_ge(s_rstd_ready, 2 * n + 1)
            g0 = n // 2 * KT + (2 * KT if n % 2 else 0)

            def scale(kg):
                if kg >= 2:
                    v.wait_ge(s_x_turned, 4 * n + kg - 1)
                at_ = ((kg % 2) * NT + 1) * 512
                nc.vector.tensor_scalar(scr[:, at_:at_ + 512], x[:, 1, kg * 512:(kg + 1) * 512], rstd[:, 0, 1:2],
                                        None, ALU.mult).then_inc(s_x_scaled_dve, 1)

            scale(0)
            scale(1)
            if n == 0:
                split_lo(0, 0)
            for kg in range(4):
                for q in range(4):
                    kt = 4 * kg + q
                    v.wait_ge(s_hn_hi, 16 * n + 2 * (kt // 2) + 2)
                    nc.vector.scalar_tensor_tensor(out=hn[:, kt, S:2 * S],
                                                   in0=mi[:, 2 * (kg % 2) + q // 2, (q % 2) * S:(q % 2 + 1) * S],
                                                   scalar=vecT[:, g0 + kt:g0 + kt + 1], in1=hn[:, kt, 0:S].bitcast(F32),
                                                   op0=ALU.mult, op1=ALU.subtract).then_inc(s_hn_lo, 1)
                if kg + 2 < 4:
                    scale(kg + 2)
                if n == 0 and 1 <= kg < LEAD:
                    split_lo(kg, 0)

        def update_x(n, m):
            v.wait_ge(s_rstd_ready, 2 * n + 2)
            for b in range(NCB):
                for t in range(NT):
                    cs = slice(b * NW, (b + 1) * NW)
                    nc.vector.scalar_tensor_tensor(out=x[:, t, cs], in0=m[:, t, cs], scalar=rstd[:, 1, t:t + 1],
                                                   in1=x[:, t, cs], op0=ALU.mult, op1=ALU.add).then_inc(s_x_updated, 1)

        def out_projection(n_norm, ph, n, m, gn, final=False, done=0):
            def body(i, d, done=0, last=False):
                for u in range(2):
                    for j in range(0 if u else done, n):
                        c = ph["c"] + u * n + j
                        if not (final and c + LEAD + (d if isinstance(d, int) else 0) >= CHUNKS):
                            split_lo(c + LEAD, d)
                        if j == n - 1:
                            v.wait_ge(s_gain_loaded, 16 * (n_norm + 1))
                            cs = bass.ds(i * (2 * NW) + u * NW, NW)
                            for t in range(NT):
                                v.wait_ge(s_out_squared, i * 4 + (8 * n_norm + 2 * u + t + 1))
                                if last and u == 1 and t == NT - 1:
                                    root_input(2 * n_norm + 1, ssm, (s_out_squared, 8 * (n_norm + 1)))
                                e = nc.vector.tensor_tensor(m[:, t, cs], dn[:, 2 * ((ph["b"] + u) % 2) + t, :],
                                                            gn[:, cs], ALU.mult)
                            e.then_inc(s_block_evacuated, 1)
            if final:
                for i in range(NCB // 2 - 1):
                    body(i, i * 2 * n)
            elif done:
                body(0, 0, done)
            if not final and (1 if done else 0) < NCB // 2 - 1:
                with v.Fori(1 if done else 0, NCB // 2 - 1) as i:
                    body(i, i * (2 * n))
            i = NCB // 2 - 1
            body(i, i * (2 * n), last=True)
            v.wait_ge(s_block_evacuated, ph["b"] + NCB)
            update_x(n_norm, m)

        def feed_forward(layer, ph, pd, final):
            with v.Fori(0, FI) as i:
                for j in range(8):
                    split_lo(ph["c"] + j + LEAD, i * 8)
                    if j == 3:
                        add_halves(fg, ph["b"], ph["t"], i * 2)
                    if j == 5:
                        v.wait_ge(s_ff_tanh, i + (FI * layer + 1))
                        nc.vector.scalar_tensor_tensor(out=fth, in0=fth, scalar=1.0, in1=fg, op0=ALU.add,
                                                       op1=ALU.mult).then_inc(s_ff_gate, 1)
                    if j == 7:
                        add_halves(fu, ph["b"] + 1, ph["t"] + 1, i * 2)
                        v.wait_ge(s_block_evacuated, i * 2 + (ph["b"] + 2))
                        v.wait_ge(s_ff_gate, i + (FI * layer + 1))
                        nc.vector.scalar_tensor_tensor(out=fh, in0=fth, scalar=0.5, in1=fu, op0=ALU.mult,
                                                       op1=ALU.mult).then_inc(s_ff_hidden, 1)
                        v.wait_ge(s_ff_hi, i + (FI * layer + 1))
                        nc.vector.tensor_tensor(hid[:, bass.ds(i * 2, 2), S:2 * S], fh,
                                                hid[:, bass.ds(i * 2, 2), 0:S].bitcast(F32), ALU.subtract).then_inc(s_ff_lo, 1)
            out_projection(2 * layer + 1, pd, FF // P // 2, m_a, gain, final)

        nc.vector.memset(epsc[:, 0:1], EPS).then_inc(s_eps_set, 1)
        nc.vector.memset(epsc[:, 1:2], EPS * DH).then_inc(s_eps_set, 1)
        norm(0)

        def score_add(ih):
            v.wait_ge(s_relu_dots, ih + 1)
            for t in range(NT):
                w = P * (t + 1)
                cs = slice(t * P, t * P + w)
                if ih == 0:
                    nc.vector.tensor_scalar(score[:, cs], rel[:, 0, cs], wi[:, t, 0:1], None, ALU.mult).then_inc(s_score_added, 1)
                else:
                    v.wait_ge(s_score_added, NT * (ih - 1) + t + 1)
                    nc.vector.scalar_tensor_tensor(out=score[:, cs], in0=rel[:, ih % 2, cs], scalar=wi[:, t, ih:ih + 1],
                                                   in1=score[:, cs], op0=ALU.mult, op1=ALU.add).then_inc(s_score_added, 1)

        def topk_round(r):
            if r == 0:
                v.wait_ge(s_score_masked, NT)
            for t in range(NT):
                w = P * (t + 1)
                if r >= 1:
                    v.wait_ge(s_replaced, NT * (r - 1) + t + 1)
                nc.vector.max(top8[:, t, :], score[:, t * P:t * P + w]).then_inc(s_max8, 1)
            for t in range(NT):
                w = P * (t + 1)
                cs = slice(t * P, t * P + w)
                v.wait_ge(s_max8, NT * r + t + 1)
                nc.vector.match_replace(score[:, cs], top8[:, t, :], score[:, cs], TAKEN).then_inc(s_replaced, 1)

        def soften(h):
            v.wait_ge(s_logits, h + 1)
            v.wait_ge(s_bias_masked, h + 1)
            nc.vector.scalar_tensor_tensor(out=prob[:, h % 2, :], in0=mi[:, 0, 0:3 * P], scalar=float(DH) ** -0.5,
                                           in1=bm[:, h, :], op0=ALU.mult, op1=ALU.add).then_inc(s_logits_biased, 1)
            v.wait_ge(s_logits_biased, h + 1)
            for t in range(NT):
                w = P * (t + 1)
                nc.vector.tensor_reduce(mx[:, h, t:t + 1], prob[:, h % 2, t * P:t * P + w], AX, ALU.max,
                                        negate=True).then_inc(s_logits_max, 1)

        def scale_probs(h):
            v.wait_ge(s_probs, NT * (h + 1))
            nc.vector.reciprocal(rps[:, h, :], psm[:, h, :]).then_inc(s_probs_sum_inv, 1)
            v.wait_ge(s_probs_sum_inv, h + 1)
            for t in range(NT):
                w = P * (t + 1)
                pv = prob[:, h % 2, t * P:t * P + w]
                nc.vector.tensor_scalar(pv, pv, rps[:, h, t:t + 1], None, ALU.mult).then_inc(s_probs_scaled, 1)

        wins = [0]

        def pool_window(k):
            gi = xp_order[k]
            n = len(blocks0) - 4 + k
            v.wait_ge(s_block_evacuated, n + 1)
            if k >= 1:
                v.wait_ge(s_pool_mixed, k)
            src, step = xpad, 1
            for lev in range(gi + 1):
                dst = winb if (gi - lev) % 2 == 0 else wina
                lo = 2 * step - 1
                if wins[0]:
                    v.wait_ge(s_window_sum, wins[0])
                nc.vector.tensor_tensor(dst[:, :, lo:16 + S], src[:, :, lo:16 + S], src[:, :, lo - step:16 + S - step],
                                        ALU.add).then_inc(s_window_sum, 1)
                wins[0] += 1
                src, step = dst, 2 * step
            v.wait_ge(s_window_sum, wins[0])
            if k == 0:
                v.wait_ge(s_cst_loaded, 16)
            inv = cst[:, K_INV + 16 * gi:K_INV + 16 * gi + 16].unsqueeze(1).broadcast_to([P, 2, 16])
            nc.vector.tensor_tensor(wina[:, :, 16:32], winb[:, :, 16:32], inv, ALU.mult).then_inc(s_window_sum, 1)
            wins[0] += 1
            v.wait_ge(s_window_sum, wins[0])
            nc.vector.tensor_tensor(wina[:, :, 16:32], wina[:, :, 16:32], xpad[:, :, 16:32], ALU.subtract).then_inc(s_pooled, 1)
            nc.vector.scalar_tensor_tensor(out=wina[:, :, 32:16 + S], in0=winb[:, :, 32:16 + S], scalar=1.0 / WINDOWS[gi],
                                           in1=xpad[:, :, 32:16 + S], op0=ALU.mult, op1=ALU.subtract).then_inc(s_pooled, 1)

        for s in range(len(chunks0) + OVER0):
            split_lo(s + LEAD, 0)
            if s in evac_at:
                n = evac_at[s]
                kind, idx, _, _ = blocks0[n]
                if kind == "kw":
                    add_halves(kiw[:, :].unsqueeze(1), n, tidx0[n], 0, tiles=1)
                elif kind == "qi":
                    add_halves(qiT[:, idx % 2, :, :], n, tidx0[n], 0)
                elif kind == "v":
                    v.wait_ge(s_chunk_used, s)
                    b2 = 2 * (n % 2)
                    nc.vector.tensor_copy(vtm[:, idx % 2, :, :], dn[:, b2:b2 + 2, 0:TW]).then_inc(s_block_evacuated, 1)
                elif kind == "k":
                    add_halves(kqT[:, 0, :, :], n, tidx0[n], 0)
                elif kind == "q":
                    add_halves(kqT[:, 1, :, :], n, tidx0[n], 0)
                else:
                    if n == len(blocks0) - 4:
                        v.wait_ge(s_pads_zeroed, 3)
                    else:
                        v.wait_ge(s_pooled, 2 * (n - len(blocks0) + 4))
                    add_halves(xpad[:, :, 16:16 + S], n, tidx0[n], 0)
            if s == 4:
                v.wait_ge(s_wi_turned, 1)
                nc.vector.tensor_scalar(wi[:, :, :], mi[:, BX, 0:2 * P].rearrange("p (t f) -> p t f", t=2)[:, :, DIH:DIH + NIH],
                                        NIH ** -0.5, None, ALU.mult).then_inc(s_wi_ready, 1)
                v.wait_ge(s_wi_ready, 1)
            if 7 <= s < 7 + NIH:
                score_add(s - 7)
            if SC0 < s <= SC0 + NR:
                topk_round(s - SC0 - 1)
            if s == SC0 + NR + 1:
                v.wait_ge(s_replaced, NT * NR)
                nc.vector.tensor_scalar(score[:, :], score[:, :], TAKEN / 3, NEG, ALU.is_gt, ALU.mult).then_inc(s_selection, 1)
            if s in head_at:
                soften(head_at[s])
            if s - 1 in head_at:
                scale_probs(head_at[s - 1])
            if s - 3 in head_at:
                h = head_at[s - 3]
                v.wait_ge(s_attn_hi, h + 1)
                nc.vector.tensor_tensor(mix[:, h, S:2 * S], mi[:, 2, 0:S], mix[:, h, 0:S].bitcast(F32),
                                        ALU.subtract).then_inc(s_attn_lo, 1)
            for k in range(4):
                if s == end0[17 + k] + 1:
                    pool_window(k)
                if s == end0[17 + k] + 2:
                    gi = xp_order[k]
                    v.wait_ge(s_pool_hi, 2 * (k + 1))
                    for dt in range(2):
                        col = 4 * KT + 2 * gi + dt
                        i = nc.vector.scalar_tensor_tensor(out=mix[:, NH + 2 * gi + dt, S:2 * S], in0=mi[:, 3, dt * S:(dt + 1) * S],
                                                           scalar=vecT[:, col:col + 1], in1=mix[:, NH + 2 * gi + dt, 0:S].bitcast(F32),
                                                           op0=ALU.mult, op1=ALU.subtract)
                    i.then_inc(s_pool_lo, 1)
        out_projection(0, PH_OUT0, KT // 2, m_a, gain, done=OVER0)
        norm(1)
        feed_forward(0, PH_FF0, PH_DN0, False)
        norm(2)
        split_lo(PH_BA["c"] + LEAD, 0)
        split_lo(PH_BA["c"] + 1 + LEAD, 0)
        add_halves(conv_y[:, 0:1, :], PH_BA["b"], PH_BA["t"], 0, tiles=1)

        def gates(step):
            if step == 0:
                v.wait_ge(s_ba_turned, 1)
                nc.vector.tensor_copy(ba[:, :, :], mi[:, BY, 0:2 * P].rearrange("p (t f) -> p t f", t=2)[:, :, P - 2 * NVH:P]).then_inc(s_ba_ready, 1)
                v.wait_ge(s_ba_ready, 1)
                v.wait_ge(s_avec_loaded, 32)
                nc.vector.tensor_tensor(bat[:, 1, :, :], ba[:, :, NVH:2 * NVH],
                                        avec[:, 0:1, :].broadcast_to([P, 2, NVH]), ALU.add).then_inc(s_a_biased, 1)
                v.wait_ge(s_a_biased, 1)
                nc.vector.scalar_tensor_tensor(out=bat[:, 2, :, :], in0=bat[:, 1, :, :], scalar=-1.0,
                                               in1=bat[:, 1, :, :], op0=ALU.mult, op1=ALU.min).then_inc(s_a_folded, 1)
            if step == 1:
                v.wait_ge(s_ba_exps, 3)
                nc.vector.tensor_scalar(bat[:, 0, :, :], bat[:, 0, :, :], 1.0, None, ALU.add).then_inc(s_a_biased, 1)
                v.wait_ge(s_a_biased, 2)
                nc.vector.reciprocal(sc4[:, 3, :, :], bat[:, 0, :, :]).then_inc(s_a_biased, 1)
            if step == 2:
                v.wait_ge(s_a_log1p, 1)
                nc.vector.scalar_tensor_tensor(out=bat[:, 1, :, :], in0=bat[:, 1, :, :], scalar=0.0,
                                               in1=bat[:, 3, :, :], op0=ALU.max, op1=ALU.add).then_inc(s_softplus, 1)
                v.wait_ge(s_softplus, 1)
                nc.vector.scalar_tensor_tensor(out=sc4[:, 0, :, :], in0=bat[:, 1, :, :], scalar=-1.0,
                                               in1=avec[:, 1:2, :].broadcast_to([P, 2, NVH]), op0=ALU.mult,
                                               op1=ALU.mult).then_inc(s_g_ready, 1)
            if step == 3:
                v.wait_ge(s_gc_psum, 1)
                nc.vector.tensor_copy(sc4[:, 1, :, :], mi[:, BX, 256:256 + 2 * NVH].rearrange("p (a b) -> p a b", a=2)).then_inc(s_gc_ready, 1)
            if step == 4:
                v.wait_ge(s_gc_exp, 1)
                nc.vector.tensor_scalar(sc4[:, 2, :, :], sc4[:, 2, :, :], -1.0, None, ALU.mult).then_inc(s_scalars_ready, 1)

        def take_scalars(g):
            if not looped(g):
                v.wait_ge(s_scalars_ready, 1)
                v.wait_ge(s_a_biased, 3)
            else:
                v.wait_ge(s_vnew1, g * 1)
            nc.vector.tensor_copy(cur[:, :, :, :], sc4[:, :, :, bass.ds(g * 4, 4)]).then_inc(s_cur_ready, 1)

        def take_gc(g):
            if not looped(g):
                v.wait_ge(s_scalars_ready, 1)
            else:
                v.wait_ge(s_decay_clamped, g * 2)
            nc.vector.tensor_copy(gch[:, :, :], sc4[:, 1, :, bass.ds(g * 4, 4)]).then_inc(s_gc_taken, 1)

        def take_taps(g):
            if not looped(g):
                v.wait_ge(s_cw_ready, 1)
            for at_, w, base, step in ((0, 2, NKH, 2), (2, 2, 0, 2), (4, 4, 2 * NKH, 4)):
                i = nc.vector.tensor_copy(cwc[:, :, at_:at_ + w], cwT[:, :, bass.ds(g * step + base, w)])
            i.then_inc(s_cwc_ready, 1)

        def evac(g, b):
            out = cpad[:, :, 3:3 + S] if b < 4 else zs[:, 2 * (b - 4):2 * (b - 4) + 2, :]
            add_halves(out, PH_IN1["b"] + b, PH_IN1["t"] + b, g * 6)

        def taps(g, b):
            v.wait_ge(s_tap0, g * 4 + (b + 1))
            for k in range(3):
                for f in range(2):
                    if k >= 1:
                        v.wait_ge(s_taps, g * 24 + (6 * b + 2 * (k - 1) + f + 1))
                    nc.vector.scalar_tensor_tensor(out=conv_y[:, f, :], in0=cpad[:, f, 2 - k:2 - k + S],
                                                   scalar=cwc[:, 2 - k, 2 * b + f:2 * b + f + 1], in1=conv_y[:, f, :],
                                                   op0=ALU.mult, op1=ALU.add).then_inc(s_taps, 1)

        def silu(g, b):
            v.wait_ge(s_conv_tanh, g * 6 + (b + 1))
            out = kqr[:, b, :, :] if b < 2 else vfm[:, :, :]
            if b == 3:
                v.wait_ge(s_v_turned, g * 2 + 1)
            nc.vector.scalar_tensor_tensor(out=out, in0=conv_th, scalar=1.0, in1=conv_y, op0=ALU.add,
                                           op1=ALU.mult).then_inc(s_silu_done, 1)

        def gate_z(g, k):
            v.wait_ge(s_conv_tanh, g * 6 + (5 + k))
            z = zs[:, 2 * k:2 * k + 2, :]
            nc.vector.scalar_tensor_tensor(out=z, in0=conv_th, scalar=1.0, in1=z, op0=ALU.add,
                                           op1=ALU.mult).then_inc(s_z_gated, 1)

        def clamp(g, c):
            v.wait_ge(s_gc_rows, g * 2 + (c + 1))
            for u in range(4):
                i = nc.vector.tensor_scalar(dec[:, c, u, :], mi[:, BM, u * P:(u + 1) * P], gch[:, c, u:u + 1], 0.0,
                                            ALU.subtract, ALU.min)
            i.then_inc(s_decay_clamped, 1)

        def invert_norms(g, kq_on, o_on):
            v.wait_ge(s_norm_roots, g * 1 + 1)
            cs = slice(0 if kq_on else 8, 16 if o_on else 8)
            nc.vector.reciprocal(nrm[:, cs], nrm[:, cs]).then_inc(s_norm_inverses, 1)

        def norm_kq(g):
            for k in range(2):
                v.wait_ge(s_norm_rows, g * 2 + (k + 1))
                nc.vector.tensor_tensor(kq[:, k, :, :].rearrange("p b c -> p (b c)"),
                                        kqr[:, k, :, :].rearrange("p b c -> p (b c)"), mi[:, (BM, BY)[k], :],
                                        ALU.mult).then_inc(s_kq_normed, 1)

        def o_heads(g, k):
            return o32[:, bass.ds(g * 4 + 2 * k, 2), :]

        def gate_o(g, k):
            v.wait_ge(s_o_squared, g * 2 + (k + 1))
            v.wait_ge(s_z_gated, g * 2 + (k + 1))
            nc.vector.scalar_tensor_tensor(out=o_heads(g, k), in0=mi[:, (BX, BT)[k], :].rearrange("p (a b) -> p a b", a=2),
                                           scalar=nwh[:, 0:1], in1=zs[:, 2 * k:2 * k + 2, :], op0=ALU.mult,
                                           op1=ALU.mult).then_inc(s_o_normed, 1)

        def norm_o(g, k):
            v.wait_ge(s_o_norm_rows, g * 2 + (k + 1))
            v.wait_ge(s_o_normed, g * 2 + (k + 1))
            nc.vector.tensor_tensor(o_heads(g, k), o_heads(g, k), mi[:, (BX, BT)[k], :].rearrange("p (a b) -> p a b", a=2),
                                    ALU.mult).then_inc(s_o_gated, 1)

        def weigh(g, c):
            v.wait_ge(s_kk_qk, g * 2 + (c + 1))
            v.wait_ge(s_decay_ready, g * 2 + (c + 1))
            for u in range(4):
                kp = u // 2
                i = nc.vector.scalar_tensor_tensor(out=at[:, c, u, :], in0=mi[:, BM, kp * 256:kp * 256 + P],
                                                   scalar=cur[:, 3, c, u:u + 1], in1=dec[:, c, u, :], op0=ALU.mult,
                                                   op1=ALU.mult)
            i.then_inc(s_a_raw, 1)
            for kp in range(2):
                i = nc.vector.tensor_tensor(intra[:, c, 2 * kp:2 * kp + 2, :],
                                            mi[:, BM, kp * 256 + P:kp * 256 + 2 * P].unsqueeze(1).broadcast_to([P, 2, P]),
                                            dec[:, c, 2 * kp:2 * kp + 2, :], ALU.mult)
            i.then_inc(s_intra_raw, 1)

        def first_x(g, b):
            v.wait_ge(s_a_ready, g * 2 + (b + 1))
            nc.vector.tensor_tensor(xt[:, b, :, :], at[:, b, :, :],
                                    cst[:, K_M0:K_M0 + P].unsqueeze(1).broadcast_to([P, 4, P]), ALU.mult).then_inc(s_x1T, 1)

        def mask_w(g, b, lev):
            v.wait_ge(s_ax_psum, g * 12 + (2 * (lev - 1) + b + 1))
            half = P // 2
            src = mi[:, BY, 0:2 * P]
            if lev < NLEV:
                mk = cst[:, K_MT + (lev - 1) * P:K_MT + lev * P].rearrange("p (a x) -> p a x", a=2)
                nc.vector.tensor_tensor(wy[:, b, :, 0:half].rearrange("p (h a) x -> p h a x", h=2),
                                        src.rearrange("p (h a x) -> p h a x", h=2, a=2),
                                        mk.unsqueeze(1).broadcast_to([P, 2, 2, half]), ALU.mult).then_inc(s_w_ready, 1)
            else:
                mk = cst[:, K_MT + (lev - 1) * P:K_MT + (lev - 1) * P + half].unsqueeze(1).broadcast_to([P, 4, half])
                nc.vector.tensor_tensor(wy[:, b, :, 0:half], src.rearrange("p (u s) -> p u s", u=4), mk,
                                        ALU.mult).then_inc(s_w_ready, 1)

        def decay_q(g):
            v.wait_ge(s_exp_gc_row, g * 1 + 1)
            v.wait_ge(s_kq_normed, g * 2 + 2)
            for kp in range(2):
                i = nc.vector.tensor_tensor(qd[:, 2 * kp:2 * kp + 2, :], egc[:, 2 * kp:2 * kp + 2, :],
                                            kq[:, 1, kp:kp + 1, P:S].broadcast_to([P, 2, P]), ALU.mult)
            i.then_inc(s_q_decayed, 1)

        def decay_k(g):
            v.wait_ge(s_k_tok, g * 1 + 1)
            for u in range(4):
                i = nc.vector.tensor_scalar(kdec[:, u, :], ktok[:, u // 2, :], dec[:, 0, u, P - 1:P], None, ALU.mult)
            i.then_inc(s_k_decayed, 1)

        def times_beta(g, c):
            v.wait_ge((s_y0, s_y1)[c], g * 1 + 1)
            for u in range(4):
                i = nc.vector.tensor_scalar(vn[:, c, u, :], mi[:, BY, u * P:(u + 1) * P], cur[:, 3, c, u:u + 1], None,
                                            ALU.mult)
            i.then_inc((s_vnew0, s_vnew1)[c], 1)

        def rhs1(g):
            v.wait_ge(s_k_state, g * 1 + 1)
            for u in range(4):
                i = nc.vector.scalar_tensor_tensor(out=vtok[:, 1, u, :], in0=mi[:, BY, u * P:(u + 1) * P],
                                                   scalar=cur[:, 2, 1, u:u + 1], in1=vtok[:, 1, u, :], op0=ALU.mult,
                                                   op1=ALU.add)
            i.then_inc(s_rhs1, 1)

        def urgent(n, g, cur_on, prev_on):
            if prev_on and n + GSLOT == 35:
                times_beta(g - 1, 1)
            if cur_on:
                if n == 15:
                    norm_kq(g)
                if n in (16, 17):
                    weigh(g, n - 16)
                if n in (17, 18):
                    first_x(g, n - 17)

        def slot(n, g, cur_on, prev_on):
            if prev_on:
                h, m = g - 1, n + GSLOT
                if m == 24:
                    evac(h, 5)
                if m == 26:
                    gate_z(h, 1)
                for b in range(2):
                    lev, odd = divmod(m - 20 - b, 2)
                    if odd == 0 and 1 <= lev + 1 <= NLEV:
                        mask_w(h, b, lev + 1)
                if m == 32:
                    times_beta(h, 0)
                if m == 34:
                    rhs1(h)
            if cur_on:
                if n == 3:
                    take_taps(g)
                if n == 8:
                    take_gc(g)
                if n in (9, 10):
                    clamp(g, n - 9)
                if n == 11:
                    take_scalars(g)
            if n == 13 and (cur_on or prev_on):
                invert_norms(g, cur_on, prev_on)
            if prev_on and n == 13:
                gate_o(h, 0)
                gate_o(h, 1)
            if cur_on and n == 18:
                decay_q(g)
            if prev_on and n in (17, 18):
                norm_o(h, n - 17)
            if cur_on:
                for b in range(2):
                    lev, odd = divmod(n - 20 - b, 2)
                    if odd == 0 and lev >= 0:
                        mask_w(g, b, lev + 1)
                if n % 4 == 0 and n > 0:
                    evac(g, n // 4 - 1)
                if n in (7, 11, 15, 19):
                    silu(g, n // 4 - 1)
                if n in (5, 9, 13, 17):
                    taps(g, n // 4 - 1)
                if n == 22:
                    gate_z(g, 0)
                if n == 23:
                    decay_k(g)
        def group(g, d, prev_on):
            for n in range(GSLOT):
                urgent(n, g, True, prev_on)
                split_lo(PH_IN1["c"] + n + LEAD, d * GSLOT)
                if not prev_on and n < 5:
                    gates(n)
                slot(n, g, True, prev_on)

        v.wait_ge(s_cpad_zeroed, 1)
        group(0, 0, False)
        with v.Fori(1, NG) as g:
            group(g, g, True)
        def o_lo(j):
            v.wait_ge(s_o_hi, j + 1)
            nc.vector.tensor_tensor(olo[:, 2 * j:2 * j + 2, :], o32[:, 2 * j:2 * j + 2, :],
                                    ohi[:, 2 * j:2 * j + 2, :].bitcast(F32), ALU.subtract).then_inc(s_o_lo, 1)

        o_lo(0)
        o_lo(1)
        for n in range(19 + 1):
            urgent(n, NG, False, True)
            if n < NFREE:
                split_lo(PH_OUT1["c"] + n + LEAD, 0)
                if n + 2 < NFREE:
                    o_lo(n + 2)
            slot(n, NG, False, True)
        o_lo(NFREE)
        o_lo(NFREE + 1)
        out_projection(2, PH_OUT1, NVH // 2, m_b, gain_b, done=NFREE)
        norm(3)
        feed_forward(1, PH_FF1, PH_DN1, True)


_INS = ["x", "rel_bias", "even_w_in", "even_w_o", "pool_w", "pool_scale", "odd_w_in", "conv_w", "a_log", "dt_bias",
        "gdn_norm_w", "odd_w_o", "ffn_w_gate", "ffn_w_up", "ffn_w_down", "mix_pre_g", "mix_post_g", "ffn_pre_g",
        "ffn_post_g"]


def kernel(**inputs):
    import numpy as _np
    import concourse.bacc as _bacc
    from concourse.bass_utils import run_bass_kernel_spmd as _run

    nc = _bacc.Bacc("TRN2", target_bir_lowering=False, num_devices=1)
    arrays, io = {}, {}
    given = {n: _np.ascontiguousarray(inputs[n]) for n in _INS}
    given["consts"] = constants()
    given["onehot"] = bucket_onehot()
    for name, a in given.items():
        arrays[f"in_{name}"] = a
        io[name] = nc.dram_tensor(f"in_{name}", a.shape, F32, kind="ExternalInput").ap()
    io["out"] = nc.dram_tensor("out_x", (1, S, D), F32, kind="ExternalOutput").ap()
    trunk(nc, io)
    r = _run(nc, [arrays], core_ids=[0])
    return r.results[0]["out_x"]
```
